# Optimizing a Trainium2 kernel written in Bass

```python
import math
import jax, jax.numpy as jnp
from jax import lax
import numpy as np

D_MODEL = 2048
BATCH = 1
SEQ = 256
DEPTH = 2

CHUNK = 64
N_META = 16
Q_BLOCK = 128
N_MIXERS = 2
RMS_EPS = 1e-6

DA_HEADS = 8
DA_HEAD_DIM = D_MODEL // (2 * DA_HEADS)
DA_V_DIM = 2 * DA_HEAD_DIM
ROPE_THETA = 500000.0
ROPE_DIM = DA_HEAD_DIM // 4

POOL_WINDOWS = (2, 4, 8, 16)
POOL_GROUPS = len(POOL_WINDOWS)
POOL_GROUP_DIM = D_MODEL // POOL_GROUPS

N_ATTN_LAYERS = (DEPTH + 1) // 2
N_POOL_LAYERS = DEPTH // 2


def rms_norm(x, g):
    xf = x.astype(jnp.float32)
    y = xf * lax.rsqrt(jnp.mean(xf * xf, axis=-1, keepdims=True) + RMS_EPS)
    return (y * g.astype(jnp.float32)).astype(x.dtype)

def chunk_ids(length):
    p = jnp.arange(length)
    return jnp.where(p < N_META, 0, (p - N_META) // CHUNK + 1)

def rope_tables(length):
    pos = jnp.arange(length, dtype=jnp.float32)
    inv = ROPE_THETA ** (-jnp.arange(0, ROPE_DIM, 2, dtype=jnp.float32) / ROPE_DIM)
    ang = pos[:, None] * inv[None, :]
    return jnp.cos(ang), jnp.sin(ang)

def apply_partial_rope(t, cos, sin):
    half = ROPE_DIM // 2
    c = cos.astype(t.dtype)
    s = sin.astype(t.dtype)
    r1 = t[..., :half]
    r2 = t[..., half:ROPE_DIM]
    return jnp.concatenate([r1 * c - r2 * s, r2 * c + r1 * s, t[..., ROPE_DIM:]], axis=-1)

def diff_attend(q1, q2, k1, k2, v, qc, kc, lam):
    scale = DA_HEAD_DIM ** -0.5
    mask = kc[None, :] <= qc[:, None]
    neg = jnp.finfo(jnp.float32).min
    s1 = jnp.einsum('bhqd,bhkd->bhqk', q1, k1).astype(jnp.float32) * scale
    s2 = jnp.einsum('bhqd,bhkd->bhqk', q2, k2).astype(jnp.float32) * scale
    p1 = jax.nn.softmax(jnp.where(mask, s1, neg), axis=-1)
    p2 = jax.nn.softmax(jnp.where(mask, s2, neg), axis=-1)
    a = p1 - lam * p2
    return jnp.einsum('bhqk,bhkd->bhqd', a.astype(v.dtype), v)

def diff_attention_mixer(h, w_in, w_out, lq1, lk1, lq2, lk2, subln_g, layer_idx, cos, sin):
    B, L, D = h.shape
    proj = h @ w_in
    q, k, v, g = jnp.split(proj, 4, axis=-1)
    q = q.reshape(B, L, DA_HEADS, 2, DA_HEAD_DIM).transpose(0, 2, 3, 1, 4)
    k = k.reshape(B, L, DA_HEADS, 2, DA_HEAD_DIM).transpose(0, 2, 3, 1, 4)
    v = v.reshape(B, L, DA_HEADS, DA_V_DIM).transpose(0, 2, 1, 3)
    q1 = apply_partial_rope(q[:, :, 0], cos, sin)
    q2 = apply_partial_rope(q[:, :, 1], cos, sin)
    k1 = apply_partial_rope(k[:, :, 0], cos, sin)
    k2 = apply_partial_rope(k[:, :, 1], cos, sin)

    lam_init = 0.8 - 0.6 * math.exp(-0.3 * layer_idx)
    lam = (jnp.exp(jnp.sum(lq1.astype(jnp.float32) * lk1.astype(jnp.float32)))
           - jnp.exp(jnp.sum(lq2.astype(jnp.float32) * lk2.astype(jnp.float32)))
           + lam_init)

    cid = chunk_ids(L)
    outs = [diff_attend(q1[:, :, :N_META], q2[:, :, :N_META], k1[:, :, :N_META],
                        k2[:, :, :N_META], v[:, :, :N_META], cid[:N_META], cid[:N_META], lam)]
    n_blocks = (L - N_META) // Q_BLOCK
    for b in range(n_blocks):
        q0 = N_META + b * Q_BLOCK
        q1e = q0 + Q_BLOCK
        outs.append(diff_attend(q1[:, :, q0:q1e], q2[:, :, q0:q1e], k1[:, :, :q1e],
                                k2[:, :, :q1e], v[:, :, :q1e], cid[q0:q1e], cid[:q1e], lam))
    o = jnp.concatenate(outs, axis=2)
    o = rms_norm(o, subln_g) * (1.0 - lam_init)
    o = o.transpose(0, 2, 1, 3).reshape(B, L, D)
    return (o * jax.nn.silu(g)) @ w_out

def pool_mixer(h, w_in, w_group, scale, w_out):
    B, L, D = h.shape
    proj = h @ w_in
    u, g = jnp.split(proj, 2, axis=-1)
    ug = u.reshape(B, L, POOL_GROUPS, POOL_GROUP_DIM)
    cs = jnp.cumsum(ug.astype(jnp.float32), axis=1)
    csp = jnp.concatenate([jnp.zeros((B, 1, POOL_GROUPS, POOL_GROUP_DIM), jnp.float32), cs], axis=1)
    t = jnp.arange(L)
    pooled = []
    for gi, w in enumerate(POOL_WINDOWS):
        start = jnp.maximum(t + 1 - w, 0)
        cnt = jnp.minimum(t + 1, w).astype(jnp.float32)
        s = csp[:, 1:, gi] - csp[:, start, gi]
        pooled.append(s / cnt[None, :, None])
    pooled = jnp.stack(pooled, axis=2).astype(u.dtype)
    mixed = pooled - ug
    mixed = jnp.einsum('blgc,gcd->blgd', mixed, w_group).reshape(B, L, D) * scale
    return (mixed * jax.nn.silu(g)) @ w_out

def first_inputs(seed: int = 0) -> dict:
    key = jax.random.key(seed)
    ks = jax.random.split(key, 16)
    D = D_MODEL
    f = jnp.float32
    nrm = jax.random.normal
    return {
        "x": nrm(ks[0], (BATCH, SEQ, D), f),
        "meta_tokens": nrm(ks[1], (N_META, D), f),
        "pre_norm_g": 1.0 + 0.05 * nrm(ks[2], (DEPTH, D), f),
        "post_norm_g": 1.0 + 0.05 * nrm(ks[3], (DEPTH, D), f),
        "attn_w_in": nrm(ks[4], (N_ATTN_LAYERS, D, 4 * D), f) * D ** -0.5,
        "attn_w_out": nrm(ks[5], (N_ATTN_LAYERS, D, D), f) * D ** -0.5,
        "attn_lambda_q1": 0.1 * nrm(ks[6], (N_ATTN_LAYERS, DA_HEAD_DIM), f),
        "attn_lambda_k1": 0.1 * nrm(ks[7], (N_ATTN_LAYERS, DA_HEAD_DIM), f),
        "attn_lambda_q2": 0.1 * nrm(ks[8], (N_ATTN_LAYERS, DA_HEAD_DIM), f),
        "attn_lambda_k2": 0.1 * nrm(ks[9], (N_ATTN_LAYERS, DA_HEAD_DIM), f),
        "attn_subln_g": 1.0 + 0.05 * nrm(ks[10], (N_ATTN_LAYERS, DA_V_DIM), f),
        "pool_w_in": nrm(ks[11], (N_POOL_LAYERS, D, 2 * D), f) * D ** -0.5,
        "pool_w_group": nrm(ks[12], (N_POOL_LAYERS, POOL_GROUPS, POOL_GROUP_DIM, POOL_GROUP_DIM), f) * POOL_GROUP_DIM ** -0.5,
        "pool_scale": 1.0 + 0.1 * nrm(ks[13], (N_POOL_LAYERS, D), f),
        "pool_w_out": nrm(ks[14], (N_POOL_LAYERS, D, D), f) * D ** -0.5,
    }

def first_block(x, meta_tokens, pre_norm_g, post_norm_g, attn_w_in, attn_w_out,
              attn_lambda_q1, attn_lambda_k1, attn_lambda_q2, attn_lambda_k2, attn_subln_g,
              pool_w_in, pool_w_group, pool_scale, pool_w_out):
    B = x.shape[0]
    meta = jnp.broadcast_to(meta_tokens.astype(x.dtype)[None], (B, N_META, x.shape[-1]))
    h = jnp.concatenate([meta, x], axis=1)
    L = h.shape[1]
    cos, sin = rope_tables(L)
    for i in range(DEPTH):
        j = i // N_MIXERS
        hn = rms_norm(h, pre_norm_g[i])
        if i % N_MIXERS == 0:
            y = diff_attention_mixer(hn, attn_w_in[j], attn_w_out[j], attn_lambda_q1[j],
                                     attn_lambda_k1[j], attn_lambda_q2[j], attn_lambda_k2[j],
                                     attn_subln_g[j], i, cos, sin)
        else:
            y = pool_mixer(hn, pool_w_in[j], pool_w_group[j], pool_scale[j], pool_w_out[j])
        h = h + rms_norm(y, post_norm_g[i])
    return h[:, N_META:]


DEPTH_2 = 1

PLE_DIM = 256
NORM_EPS = 1e-6

RW_HEADS = 16
RW_HEAD_DIM = 64
RW_WIDTH = RW_HEADS * RW_HEAD_DIM
RW_DECAY_LORA = 64
RW_A_LORA = 64
RW_GATE_LORA = 160
RW_GN_EPS = 64e-5
RW_COLS = 3 * RW_WIDTH + RW_DECAY_LORA + RW_A_LORA + RW_GATE_LORA
RW_SPLITS = (RW_WIDTH, 2 * RW_WIDTH, 3 * RW_WIDTH, 3 * RW_WIDTH + RW_DECAY_LORA, 3 * RW_WIDTH + RW_DECAY_LORA + RW_A_LORA)

MLA_HEADS = 8
MLA_Q_RANK = 512
MLA_KV_RANK = 512
MLA_NOPE = 128
MLA_ROPE = 64
MLA_V = 128
MLA_COLS = MLA_Q_RANK + MLA_KV_RANK + MLA_ROPE
ROPE_BASE = 10000.0

GATE_COLS = 2 * D_MODEL
IN_COLS = RW_COLS + MLA_COLS + GATE_COLS

D_FF = 5632
CONV_W = 3


def rms_norm_2(x, g):
    xf = x.astype(jnp.float32)
    y = xf * lax.rsqrt(jnp.mean(xf * xf, axis=-1, keepdims=True) + NORM_EPS)
    return (y * g.astype(jnp.float32)).astype(x.dtype)

def token_shift(z):
    return jnp.pad(z, ((0, 0), (1, 0), (0, 0)))[:, :-1]

def rope(x, cos, sin):
    x1, x2 = jnp.split(x, 2, axis=-1)
    return jnp.concatenate([x1 * cos - x2 * sin, x2 * cos + x1 * sin], axis=-1)

def rwkv7_scan(r, decay, k, v, kk, a):
    B, S, H, N = r.shape

    def step(state, inp):
        r_t, w_t, k_t, v_t, kk_t, a_t = inp
        sa = jnp.einsum('bhvk,bhk->bhv', state, -kk_t)
        state = (state * w_t[:, :, None, :]
                 + sa[..., None] * (kk_t * a_t)[:, :, None, :]
                 + v_t[..., None] * k_t[:, :, None, :])
        y_t = jnp.einsum('bhvk,bhk->bhv', state, r_t)
        return state, y_t

    xs = tuple(jnp.moveaxis(t.astype(jnp.float32), 1, 0) for t in (r, decay, k, v, kk, a))
    s0 = jnp.zeros((B, H, N, N), jnp.float32)
    _, y = lax.scan(step, s0, xs)
    return jnp.moveaxis(y, 0, 1)

def rwkv7_mixer(z, mu, w0, w2, a0, a2, g2, k_k, k_a, r_k, lnx_w, lnx_b):
    B, S, _ = z.shape
    z = z + (token_shift(z) - z) * mu
    r, k, v, wd, ad, gd = jnp.split(z, RW_SPLITS, axis=-1)
    w_log = -jax.nn.softplus(-(w0 + jnp.tanh(wd) @ w2).astype(jnp.float32)) - 0.5
    decay = jnp.exp(-jnp.exp(w_log))
    a = jax.nn.sigmoid(a0 + ad @ a2)
    g = jax.nn.sigmoid(gd) @ g2

    def heads(t):
        return t.reshape(B, S, RW_HEADS, RW_HEAD_DIM)

    kk = heads(k * k_k).astype(jnp.float32)
    kk = kk / jnp.maximum(jnp.sqrt(jnp.sum(kk * kk, axis=-1, keepdims=True)), 1e-12)
    k = k * (1 + (a - 1) * k_a)
    r_h, k_h, v_h, a_h = heads(r), heads(k), heads(v), heads(a)
    y = rwkv7_scan(r_h, heads(decay), k_h, v_h, kk, a_h)
    mean = jnp.mean(y, axis=-1, keepdims=True)
    var = jnp.mean(jnp.square(y - mean), axis=-1, keepdims=True)
    y = ((y - mean) * lax.rsqrt(var + RW_GN_EPS)).reshape(B, S, RW_WIDTH)
    y = (y * lnx_w.astype(jnp.float32) + lnx_b.astype(jnp.float32)).astype(z.dtype)
    bonus = (jnp.sum(r_h * k_h * r_k, axis=-1, keepdims=True) * v_h).reshape(B, S, RW_WIDTH)
    return (y + bonus) * g

def chunk_causal_attention(q, k, v):
    B, S, H, Dqk = q.shape
    Dv = v.shape[-1]
    nb = S // Q_BLOCK
    scale = Dqk ** -0.5
    kf = k.astype(jnp.float32)
    vf = v.astype(jnp.float32)
    key_chunk = jnp.arange(S) // CHUNK
    qb = q.reshape(B, nb, Q_BLOCK, H, Dqk).transpose(1, 0, 3, 2, 4)

    def one_block(args):
        q_blk, i = args
        s = jnp.einsum('bhqd,bkhd->bhqk', q_blk.astype(jnp.float32), kf) * scale
        q_chunk = (i * Q_BLOCK + jnp.arange(Q_BLOCK)) // CHUNK
        mask = key_chunk[None, :] <= q_chunk[:, None]
        s = jnp.where(mask, s, -1e30)
        pr = jax.nn.softmax(s, axis=-1)
        return jnp.einsum('bhqk,bkhd->bqhd', pr, vf)

    o = lax.map(one_block, (qb, jnp.arange(nb)))
    return o.transpose(1, 0, 2, 3, 4).reshape(B, S, H * Dv).astype(v.dtype)

def mla_mixer(z, cos, sin, q_norm, w_q_up, kv_norm, w_kv_up):
    B, S, _ = z.shape
    cq, ckv, k_pe = jnp.split(z, (MLA_Q_RANK, MLA_Q_RANK + MLA_KV_RANK), axis=-1)
    q = (rms_norm_2(cq, q_norm) @ w_q_up).reshape(B, S, MLA_HEADS, MLA_NOPE + MLA_ROPE)
    kv = (rms_norm_2(ckv, kv_norm) @ w_kv_up).reshape(B, S, MLA_HEADS, MLA_NOPE + MLA_V)
    q_nope, q_pe = jnp.split(q, (MLA_NOPE,), axis=-1)
    k_nope, v = jnp.split(kv, (MLA_NOPE,), axis=-1)
    q_pe = rope(q_pe, cos[:, :, None, :], sin[:, :, None, :])
    k_pe = rope(k_pe, cos, sin)[:, :, None, :]
    q = jnp.concatenate([q_nope, q_pe], axis=-1)
    k = jnp.concatenate([k_nope, jnp.broadcast_to(k_pe, (B, S, MLA_HEADS, MLA_ROPE))], axis=-1)
    return chunk_causal_attention(q, k, v)

def causal_dwconv(x, w, b):
    C = x.shape[-1]
    y = lax.conv_general_dilated(x, w[:, None, :], window_strides=(1,), padding=[(CONV_W - 1, 0)],
                                 dimension_numbers=('NWC', 'WIO', 'NWC'), feature_group_count=C)
    return y + b

def second_inputs(seed: int = 0) -> dict:
    key = jax.random.key(seed)
    ks = iter(jax.random.split(key, 48))
    L, D = DEPTH_2, D_MODEL

    def nrm(shape, fan_in, s=1.0):
        return jax.random.normal(next(ks), shape, jnp.float32) * (s * fan_in ** -0.5)

    def gain(shape):
        return 1.0 + 0.02 * jax.random.normal(next(ks), shape, jnp.float32)

    def small(shape, s):
        return s * jax.random.normal(next(ks), shape, jnp.float32)

    def unif(shape, lo, hi):
        return jax.random.uniform(next(ks), shape, jnp.float32, lo, hi)

    x = jax.random.normal(next(ks), (BATCH, SEQ, D), jnp.float32)
    p = jax.random.normal(next(ks), (L, BATCH, SEQ, PLE_DIM), jnp.float32)
    start = jax.random.randint(next(ks), (BATCH, 1), 0, 4096, jnp.int32)
    positions = start + jnp.arange(SEQ, dtype=jnp.int32)[None, :]
    return {
        'x': x,
        'p': p,
        'positions': positions,
        'pre_mix_norm': gain((L, D)),
        'w_in': nrm((L, D, IN_COLS), D),
        'rw_mu': unif((L, RW_COLS), 0.0, 1.0),
        'rw_w0': unif((L, RW_WIDTH), -6.0, 1.0),
        'rw_w2': nrm((L, RW_DECAY_LORA, RW_WIDTH), RW_DECAY_LORA, 0.1),
        'rw_a0': small((L, RW_WIDTH), 0.5),
        'rw_a2': nrm((L, RW_A_LORA, RW_WIDTH), RW_A_LORA, 0.5),
        'rw_g2': nrm((L, RW_GATE_LORA, RW_WIDTH), RW_GATE_LORA),
        'rw_k_k': 0.85 + small((L, RW_WIDTH), 0.05),
        'rw_k_a': 1.0 + small((L, RW_WIDTH), 0.05),
        'rw_r_k': small((L, RW_HEADS, RW_HEAD_DIM), 0.1),
        'rw_lnx_w': gain((L, RW_WIDTH)),
        'rw_lnx_b': small((L, RW_WIDTH), 0.02),
        'mla_q_norm': gain((L, MLA_Q_RANK)),
        'mla_w_q_up': nrm((L, MLA_Q_RANK, MLA_HEADS * (MLA_NOPE + MLA_ROPE)), MLA_Q_RANK),
        'mla_kv_norm': gain((L, MLA_KV_RANK)),
        'mla_w_kv_up': nrm((L, MLA_KV_RANK, MLA_HEADS * (MLA_NOPE + MLA_V)), MLA_KV_RANK),
        'w_branch_rw': nrm((L, RW_WIDTH, D), RW_WIDTH),
        'w_branch_mla': nrm((L, MLA_HEADS * MLA_V, D), MLA_HEADS * MLA_V),
        'w_out': nrm((L, D, D), D),
        'post_mix_norm': gain((L, D)),
        'pre_ffn_norm': gain((L, D)),
        'w_up': nrm((L, D, 2 * D_FF), D),
        'conv_w': nrm((L, CONV_W, 2 * D_FF), CONV_W),
        'conv_b': small((L, 2 * D_FF), 0.02),
        'w_down': nrm((L, D_FF, D), D_FF),
        'post_ffn_norm': gain((L, D)),
        'w_ple': nrm((L, PLE_DIM, D), PLE_DIM),
        'w_ple_gate': nrm((L, D, D), D),
        'ple_norm': gain((L, D)),
    }

def second_block(x, p, positions, pre_mix_norm, w_in, rw_mu, rw_w0, rw_w2, rw_a0, rw_a2, rw_g2,
              rw_k_k, rw_k_a, rw_r_k, rw_lnx_w, rw_lnx_b, mla_q_norm, mla_w_q_up, mla_kv_norm,
              mla_w_kv_up, w_branch_rw, w_branch_mla, w_out, post_mix_norm, pre_ffn_norm, w_up,
              conv_w, conv_b, w_down, post_ffn_norm, w_ple, w_ple_gate, ple_norm):
    inv_freq = ROPE_BASE ** (-jnp.arange(0, MLA_ROPE, 2, dtype=jnp.float32) / MLA_ROPE)
    ang = positions.astype(jnp.float32)[..., None] * inv_freq
    cos = jnp.cos(ang).astype(x.dtype)
    sin = jnp.sin(ang).astype(x.dtype)
    h = x
    for i in range(DEPTH_2):
        u = rms_norm_2(h, pre_mix_norm[i])
        z = u @ w_in[i]
        z_rw, z_mla, z_gate = jnp.split(z, (RW_COLS, RW_COLS + MLA_COLS), axis=-1)
        y_rw = rwkv7_mixer(z_rw, rw_mu[i], rw_w0[i], rw_w2[i], rw_a0[i], rw_a2[i], rw_g2[i],
                           rw_k_k[i], rw_k_a[i], rw_r_k[i], rw_lnx_w[i], rw_lnx_b[i])
        y_mla = mla_mixer(z_mla, cos, sin, mla_q_norm[i], mla_w_q_up[i], mla_kv_norm[i], mla_w_kv_up[i])
        g_rw, g_mla = jnp.split(jax.nn.sigmoid(z_gate), 2, axis=-1)
        mix = (g_rw * (y_rw @ w_branch_rw[i]) + g_mla * (y_mla @ w_branch_mla[i])) @ w_out[i]
        h = h + rms_norm_2(mix, post_mix_norm[i])
        u = rms_norm_2(h, pre_ffn_norm[i])
        up = causal_dwconv(u @ w_up[i], conv_w[i], conv_b[i])
        gate, val = jnp.split(up, 2, axis=-1)
        f = (jax.nn.gelu(gate, approximate=True) * val) @ w_down[i]
        h = h + rms_norm_2(f, post_ffn_norm[i])
        e = p[i] @ w_ple[i]
        h = h + rms_norm_2(jax.nn.sigmoid(h @ w_ple_gate[i]) * e, ple_norm[i])
    return h


def setup_inputs(seed=0):
    out = dict(first_inputs(seed))
    for name, value in second_inputs(seed + 1).items():
        if name != "x":
            out[name + "_2"] = value
    return out


def reference(
    x, meta_tokens, pre_norm_g, post_norm_g, attn_w_in, attn_w_out, attn_lambda_q1,
    attn_lambda_k1, attn_lambda_q2, attn_lambda_k2, attn_subln_g, pool_w_in, pool_w_group,
    pool_scale, pool_w_out, p_2, positions_2, pre_mix_norm_2, w_in_2, rw_mu_2, rw_w0_2, rw_w2_2,
    rw_a0_2, rw_a2_2, rw_g2_2, rw_k_k_2, rw_k_a_2, rw_r_k_2, rw_lnx_w_2, rw_lnx_b_2,
    mla_q_norm_2, mla_w_q_up_2, mla_kv_norm_2, mla_w_kv_up_2, w_branch_rw_2, w_branch_mla_2,
    w_out_2, post_mix_norm_2, pre_ffn_norm_2, w_up_2, conv_w_2, conv_b_2, w_down_2,
    post_ffn_norm_2, w_ple_2, w_ple_gate_2, ple_norm_2,
):
    x = first_block(
        x, meta_tokens, pre_norm_g, post_norm_g, attn_w_in, attn_w_out, attn_lambda_q1,
        attn_lambda_k1, attn_lambda_q2, attn_lambda_k2, attn_subln_g, pool_w_in, pool_w_group,
        pool_scale, pool_w_out,
    )
    return second_block(
        x, p_2, positions_2, pre_mix_norm_2, w_in_2, rw_mu_2, rw_w0_2, rw_w2_2, rw_a0_2,
        rw_a2_2, rw_g2_2, rw_k_k_2, rw_k_a_2, rw_r_k_2, rw_lnx_w_2, rw_lnx_b_2, mla_q_norm_2,
        mla_w_q_up_2, mla_kv_norm_2, mla_w_kv_up_2, w_branch_rw_2, w_branch_mla_2, w_out_2,
        post_mix_norm_2, pre_ffn_norm_2, w_up_2, conv_w_2, conv_b_2, w_down_2, post_ffn_norm_2,
        w_ple_2, w_ple_gate_2, ple_norm_2,
    )


_drawn_inputs = setup_inputs


def setup_inputs(seed=0):
    import zlib

    import numpy as np

    out = dict(_drawn_inputs(seed))
    spreads = {}
    factors = {'pre_mix_norm_2': 2.904,
     'rw_w2_2': 8.0,
     'rw_k_k_2': 7.636,
     'rw_lnx_w_2': 35.959,
     'rw_lnx_b_2': 36.711,
     'mla_q_norm_2': 8.0,
     'mla_kv_norm_2': 8.0,
     'post_mix_norm_2': 5.35,
     'pre_ffn_norm_2': 4.68,
     'conv_b_2': 4.758,
     'post_ffn_norm_2': 22.845,
     'ple_norm_2': 30.396}
    for name, (base, spread) in spreads.items():
        noise = np.random.default_rng([zlib.crc32(name.encode()), seed]).standard_normal(out[name].shape)
        drawn = base * np.exp(spread * noise) if base else spread * noise
        out[name] = __import__('jax').numpy.asarray(drawn.astype(out[name].dtype))
    for name, factor in factors.items():
        out[name] = (out[name] * factor).astype(out[name].dtype)
    return out
```

```python
from contextlib import ExitStack
import math

import numpy as np

import concourse.bass as bass
from concourse import mybir

F32 = mybir.dt.float32
F32R = mybir.dt.float32r
I32 = mybir.dt.int32
ALU = mybir.AluOpType
ACT = mybir.ActivationFunctionType
AX = mybir.AxisListType

P = 128
D = 2048
META = 16
SEQ = 256
ROWS = META + SEQ
KT = D // P
SLOT_K = 4
SLOT_N = 512
RAW = 4
SPLIT = 2
BOTH = slice(META, ROWS)
HEADS = 8
HEAD_V = 256
LAM_INIT = 0.8 - 0.6 * math.exp(-0.3 * 0)
EPS = 1e-6
POOL_WINDOWS = (2, 4, 8, 16)
RW_WIDTH = 1024
RW_N = 64
RW_EPS = 64e-5
D_FF = 5632
FF_STEPS = D_FF // SLOT_N
MLA_HEADS = 8
MLA_SCALE = 192 ** -0.5

SLOTS_OF = [
    ("attn_in", HEADS * 8), ("attn_out", 16), ("pool_in", 32), ("pool_group", 4), ("pool_out", 16),
    ("rw_down", 4), ("rw_half0", 13), ("rw_half1", 13), ("mla_in", 8), ("mla_q", 3), ("mla_kv", 4),
    ("mix", 48), ("mix_out", 16), ("ffn", FF_STEPS * 12), ("ple", 2), ("ple_gate", 16),
]
FIRST_SLOT, N_SLOTS = {}, 0
for _name, _count in SLOTS_OF:
    FIRST_SLOT[_name] = N_SLOTS
    N_SLOTS += _count

PARAMS_OF = [
    ("pre0", 16), ("pre1", 16), ("post0", 16), ("post1", 16), ("subln", 2), ("lam", 4), ("pool_scale", 16),
    ("pre_mix", 16), ("mu_rkv", 24), ("mu_lora", 3), ("w0", 8), ("a0", 8), ("k_k", 8), ("k_a", 8), ("r_k", 8),
    ("lnx_w", 8), ("lnx_b", 8), ("q_norm", 4), ("kv_norm", 4), ("post_mix", 16), ("pre_ffn", 16),
    ("conv_w", 3 * 88), ("conv_b", 88), ("post_ffn", 16), ("ple_norm", 16), ("inv_freq", 1), ("rope_sign", 1),
]
PARAM, N_PARAMS = {}, 0
for _name, _count in PARAMS_OF:
    PARAM[_name] = N_PARAMS
    N_PARAMS += _count

CONSTS_OF = [("ident", 128), ("ones", 128), ("head_ones", 128)]
CONSTS_FIRST = [("rope_cos", ROWS), ("rope_sin", ROWS), ("inv_count", 4 * 16)]
CONSTS_RW = [("before", 64), ("upto", 64), ("after", 64), ("eye", 64), ("level0_t", 64)] + [
    (f"level{n}", 64) for n in range(6)]


def columns(table):
    at, n = {}, 0
    for name, count in table:
        at[name] = (n, n + count)
        n += count
    return at, n


def stage_consts():
    def fill(table, parts):
        at, n = columns(table)
        out = np.zeros((P, n), np.float32)
        for name, (a, b) in at.items():
            out[:, a:b] = parts[name]
        return out
    p = np.arange(P)
    head = (p[:, None] // 64 == p[None, :] // 64).astype(np.float32)
    base = fill(CONSTS_OF, {"ident": np.eye(P), "ones": np.ones((P, P)), "head_ones": head})
    inv = np.float32(500000.0) ** (-np.arange(0, 32, 2, dtype=np.float32) / np.float32(32))
    ang = (np.arange(ROWS, dtype=np.float32)[:, None] * inv[None, :]).astype(np.float32)
    ang = ang[:, p % 16].T
    sign = np.where(p % 32 < 16, -1.0, 1.0)[:, None]
    t = np.arange(16)
    counts = np.concatenate([1.0 / np.minimum(t + 1, w) for w in POOL_WINDOWS])
    first = fill(CONSTS_FIRST, {"rope_cos": np.cos(ang), "rope_sin": np.sin(ang) * sign, "inv_count": counts[None]})
    i, t = (p % 64)[:, None], np.arange(64)[None, :]
    parts = {"before": i < t, "upto": i <= t, "after": i > t, "eye": i == t}
    for n in range(6):
        b = 2 ** n
        parts[f"level{n}"] = (i // (2 * b) == t // (2 * b)) & (i // b % 2 == 1) & (t // b % 2 == 0)
    parts["level0_t"] = (t // 2 == i // 2) & (t % 2 == 1) & (i % 2 == 0)
    return base, first, fill(CONSTS_RW, parts)


def at(value, i, step):
    return value if i is None else i * step + value


class Steps:

    def __init__(self, engine, sem):
        self.engine, self.sem, self.n, self.turn, self.per = engine, sem, 0, None, 0

    def did(self, instruction):
        instruction.then_inc(self.sem, 1)
        self.n += 1
        self.settle()

    def settle(self):
        self.engine.wait_ge(self.sem, at(self.n, self.turn, self.per))

    def enter(self, turn, per):
        self.turn, self.per, self.start = turn, per, self.n

    def leave(self, turns):
        assert self.n - self.start == self.per, f"a turn has {self.n - self.start} steps"
        self.n = self.start + self.per * turns
        self.turn = None


class Chip:

    def __init__(self, nc, ctx):
        self.nc, self.ctx, self.names = nc, ctx, {}
        self.raw = [self.sb(ctx, f"raw_weights{i}", [P, SLOT_K, SLOT_N]) for i in range(RAW)]
        self.w_hi = [self.sb(ctx, f"weights_hi{i}", [P, SLOT_K, SLOT_N], F32R) for i in range(SPLIT)]
        self.w_lo = [self.sb(ctx, f"weights_lo{i}", [P, SLOT_K, SLOT_N], F32R) for i in range(SPLIT)]
        self.xa = [self.sb(ctx, f"xa_{x}", [P, KT, ROWS], F32R) for x in ("hi", "lo")]
        self.h = self.sb(ctx, "h", [P, KT, ROWS])
        self.y = self.sb(ctx, "y", [P, KT, ROWS])
        self.params = self.sb(ctx, "params", [P, N_PARAMS])
        self.consts = self.sb(ctx, "consts", [P, columns(CONSTS_OF)[1]])
        self.small = self.sb(ctx, "small", [P, 64])
        self.ps = ctx.enter_context(nc.psum_tensor("banks", [P, 8, 512], F32))
        self.raw_full = [self.sem(f"raw_full{i}") for i in range(RAW)]

    def sb(self, ctx, name, shape, dt=F32):
        return ctx.enter_context(self.nc.sbuf_tensor(name + "_sb", shape, dt))

    def sem(self, name):
        if name not in self.names:
            self.names[name] = self.ctx.enter_context(self.nc.semaphore(name))
        return self.names[name]

    def const(self, name):
        a, b = columns(CONSTS_OF)[0][name]
        return self.consts[:, a:b]

    def param(self, name, k, rows=P):
        return self.params[0:rows, PARAM[name] + k:PARAM[name] + k + 1]


def wide(table, n):
    return table.unsqueeze(1).to_broadcast([P, n, table.shape[1]])


def split_hi(c, act, n, i=None, step=0):
    act.wait_ge(c.raw_full[n % RAW], at(16 * (n // RAW + 1), i, 16 * (step // RAW)))
    if n >= SPLIT:
        act.wait_ge(c.sem("slot_used"), at(n - SPLIT + 1, i, step))
    act.copy(c.w_hi[n % SPLIT][:], c.raw[n % RAW][:]).then_inc(c.sem("hi_done"), 1)


def split_lo(c, dve, n, i=None, step=0):
    dve.wait_ge(c.sem("hi_done"), at(n + 1, i, step))
    dve.tensor_tensor(c.w_lo[n % SPLIT][:], c.raw[n % RAW][:], c.w_hi[n % SPLIT][:].bitcast(F32),
                      ALU.subtract).then_inc(c.sem("lo_done"), 1)


def products(c, pe, n, x, tiles, outs, cols, first, last, i=None, step=0, used=True, pause=None):
    pe.wait_ge(c.sem("lo_done"), at(n + 1, i, step))
    w_hi, w_lo = c.w_hi[n % SPLIT], c.w_lo[n % SPLIT]
    x_hi, x_lo = x
    for j, out in outs:
        if pause and j == 3:
            pause()
        for k, tile in tiles:
            a = slice(j * P, j * P + P)
            begin, end = first and k == tiles[0][0], last and k == tiles[-1][0]
            pe.matmul(out, w_hi[:, k, a], x_hi[:, tile, cols], start=begin, stop=False)
            pe.matmul(out, w_hi[:, k, a], x_lo[:, tile, cols], start=False, stop=False)
            done = pe.matmul(out, w_lo[:, k, a], x_hi[:, tile, cols], start=False, stop=end)
    if used:
        done.then_inc(c.sem("slot_used"), 1)
    return done


def banks(c, half, length):
    return [(j, c.ps[:, 4 * half + j, 0:length]) for j in range(4)]


def load_weights(c, sp, wall):
    for n in range(RAW):
        sp.dma_start(c.raw[n][:], wall[n]).then_inc(c.raw_full[n], 16)
    turns = (N_SLOTS - RAW) // RAW
    with sp.Fori(0, turns) as i:
        for s in range(RAW):
            sp.wait_ge(c.sem("lo_done"), i * RAW + s + 1)
            sp.dma_start(c.raw[s][:], wall[i * RAW + (s + RAW)]).then_inc(c.raw_full[s], 16)
    for n in range(RAW + turns * RAW, N_SLOTS):
        sp.wait_ge(c.sem("lo_done"), n - RAW + 1)
        sp.dma_start(c.raw[n % RAW][:], wall[n]).then_inc(c.raw_full[n % RAW], 16)



def sum_squares(c, pe, acc, bank, cols, ready, value, done):
    pe.wait_ge(ready, value)
    n = cols.stop - cols.start
    for j in range(4):
        m = pe.matmul(c.ps[:, bank, 0:n], c.const("ones"), acc[:, j, cols], start=j == 0, stop=j == 3)
    m.then_inc(done, 1)


def root(c, act, bank, out, cols, ready, value, done, width=D, eps="eps"):
    act.wait_ge(ready, value)
    act.activation(out[:, cols], c.ps[:, bank, 0:cols.stop - cols.start], ACT.Sqrt,
                   bias=c.eps[eps], scale=1.0 / width).then_inc(done, 1)


def operands_dve(c, dve, st, b, cols, t, g_post, g_pre, n):
    for kg in range(4):
        ks = slice(4 * kg, 4 * kg + 4)
        if g_post is not None:
            st.did(dve.tensor_tensor(t["tmp"][:, :, cols], c.y[:, ks, cols], wide(t["rs"][:, cols], 4), ALU.mult))
            for j in range(4):
                k = 4 * kg + j
                m = dve.scalar_tensor_tensor(out=c.h[:, k, cols], in0=t["tmp"][:, j, cols], scalar=c.param(g_post, k),
                                             in1=c.h[:, k, cols], op0=ALU.mult, op1=ALU.add)
            m.then_inc(c.sem("h_ready"), 1)
            dve.wait_ge(c.sem("h_ready"), 4 * (b - 1) + kg + 1)
        dve.wait_ge(c.sem("x_hi_ready"), 4 * b + kg + 1)
        for j in range(4):
            k = 4 * kg + j
            if g_pre is None:
                m = dve.tensor_tensor(c.xa[1][:, k, cols], c.h[:, k, cols], c.xa[0][:, k, cols].bitcast(F32), ALU.subtract)
            else:
                m = dve.scalar_tensor_tensor(out=c.xa[1][:, k, cols], in0=c.h[:, k, cols], scalar=c.param(g_pre, k),
                                             in1=c.xa[0][:, k, cols].bitcast(F32), op0=ALU.mult, op1=ALU.subtract)
        m.then_inc(c.sem("x_ready"), 1)
        if kg >= 2 and n + kg < N_SLOTS:
            split_lo(c, dve, n + kg)


def operands_act(c, act, b, cols, g_pre, n):
    for kg in range(4):
        if b:
            act.wait_ge(c.sem("h_ready"), 4 * (b - 1) + kg + 1)
        for j in range(4):
            k = 4 * kg + j
            if g_pre is None:
                m = act.copy(c.xa[0][:, k, cols], c.h[:, k, cols])
            else:
                m = act.activation(c.xa[0][:, k, cols], c.h[:, k, cols], ACT.Copy, scale=c.param(g_pre, k))
        m.then_inc(c.sem("x_hi_ready"), 1)
        if kg >= 2 and n + kg < N_SLOTS:
            split_hi(c, act, n + kg)


def squares_pool(c, pool, st, b, cols, acc, sq):
    for kg in range(4):
        if b:
            pool.wait_ge(c.sem("h_ready"), 4 * (b - 1) + kg + 1)
        hk = c.h[:, 4 * kg:4 * kg + 4, cols]
        st.did(pool.tensor_tensor((sq if kg else acc)[:, :, cols], hk, hk, ALU.mult))
        if 0 < kg < 3:
            st.did(pool.tensor_tensor(acc[:, :, cols], acc[:, :, cols], sq[:, :, cols], ALU.add))
        if kg == 3:
            pool.tensor_tensor(acc[:, :, cols], acc[:, :, cols], sq[:, :, cols], ALU.add).then_inc(c.sem("squares_ready"), 1)



def y_stage_pe(c, pe, n0, x, cols, base, wait_x=None):
    for chunk in range(4):
        if chunk >= 2:
            pe.wait_ge(c.sem("y_taken"), base + chunk - 1)
        for s in range(4):
            if chunk == 0 and wait_x:
                wait_x(s)
            products(c, pe, n0 + 4 * chunk + s, x, [(k, 4 * s + k) for k in range(4)],
                     banks(c, chunk % 2, cols.stop - cols.start), cols, s == 0, s == 3)


def y_take_act(c, act, chunk, cols, base, t):
    act.wait_ge(c.sem("y_taken"), base + chunk + 1)
    act.activation((t["sq"] if chunk else t["acc"])[:, :, cols], c.y[:, 4 * chunk:4 * chunk + 4, cols],
                   ACT.Square).then_inc(c.sem("y_squared"), 1)


def y_take_dve(c, dve, chunk, done, cols, base, t):
    n = cols.stop - cols.start
    dve.wait_ge(c.sem("slot_used"), done)
    dve.tensor_copy(c.y[:, 4 * chunk:4 * chunk + 4, cols],
                    c.ps[:, 4 * (chunk % 2):4 * (chunk % 2) + 4, 0:n]).then_inc(c.sem("y_taken"), 1)
    dve.wait_ge(c.sem("y_squared"), base + chunk + 1)
    if chunk:
        dve.tensor_tensor(t["acc"][:, :, cols], t["acc"][:, :, cols], t["sq"][:, :, cols],
                          ALU.add).then_inc(c.sem("y_added"), 1)
        dve.wait_ge(c.sem("y_added"), base // 4 * 3 + chunk)


def y_stage_split(c, split, take, n0):
    for m in range(2, 18):
        if n0 + m < N_SLOTS:
            split(n0 + m)
        if m % 4 == 1:
            take((m - 5) // 4, n0 + m - 1)



BLOCKS = [(0, 0, 16, 16), (1, 0, 64, 80), (1, 64, 128, 144), (2, 0, 64, 208), (2, 64, 128, 272)]
QUERIES = [(0, 16), (16, 144), (144, 272)]
SCORES_AT = [0, 16, 160]
SCALE = 128 ** -0.5


def attn_load(c, t, sp, a):
    sp.dma_start(c.h[:], a["h0"]).then_inc(c.sem("h_in"), 16)
    sp.dma_start(c.params[:], a["params"]).then_inc(c.sem("params_in"), 16)
    sp.dma_start(c.consts[:], a["consts"]).then_inc(c.sem("params_in"), 16)
    sp.dma_start(t["first"][:], a["consts_first"]).then_inc(c.sem("params_in"), 16)


def attn_pe(c, t, pe):
    ps, S = c.ps, c.sem
    pe.wait_ge(S("lam_products"), 1)
    pe.matmul(ps[:, 4, 0:2], c.const("ones"), t["lam"][:, 0:2], start=True, stop=True).then_inc(S("lam_sums"), 1)

    def scores(v):
        for comp in range(2):
            for q, (a, b) in enumerate(QUERIES):
                m = pe.matmul(ps[0:b - a, 4 + comp, SCORES_AT[q]:SCORES_AT[q] + b], t["qk"][:, comp, a:b],
                              t["qk"][:, 2 + comp, 0:b], start=True, stop=True)
        m.then_inc(S("scores_done"), 1)

    def values():
        for j in range(2):
            for kb, (a, b) in enumerate([(0, 272), (16, 272), (144, 272)]):
                m = pe.matmul(ps[:, 6 + j, a:b], t["vn"][:, kb, j * P:j * P + P], t["at"][:, kb, a:b],
                              start=kb == 0, stop=kb == 2)
        m.then_inc(S("values_done"), 1)

    def head(h, i, proj, cur, old):
        s0 = 8 * h
        w = lambda sem, v: pe.wait_ge(S(sem), at(v, i, 1))
        if proj:
            if h:
                w("values_out_taken", h)
            for s in range(4):
                if h == 0:
                    pe.wait_ge(S("x_ready"), s + 1)
                products(c, pe, s0 + s, c.xa, [(k, 4 * s + k) for k in range(4)], banks(c, 0, ROWS),
                         slice(0, ROWS), s == 0, s == 3, i, 8)
            if h == 0:
                sum_squares(c, pe, t["acc"], 7, slice(0, ROWS), S("squares_ready"), 1, S("stats_done"))
        if cur:
            w("qk_ready", h)
            if old:
                w("at_ready", h - 1)
                w("vn_ready", h - 1)
            scores(h)
        if old:
            if not cur:
                w("at_ready", h - 1)
                w("vn_ready", h - 1)
            values()
        if proj:
            w("keys_taken", h + 1)
            for s in range(4):
                products(c, pe, s0 + 4 + s, c.xa, [(k, 4 * s + k) for k in range(4)], banks(c, 0, ROWS),
                         slice(0, ROWS), s == 0, s == 3, i, 8)
        if old:
            if cur:
                w("probs_ready", h)
            w("osq_ready", h - 1)
            for j in range(2):
                m = pe.matmul(ps[:, 5, 0:ROWS], c.const("ones"), t["osq"][:, j, :], start=j == 0, stop=j == 1)
            m.then_inc(S("osum_done"), 1)
        if cur:
            w("a_ready", h)
            if old:
                w("o_ready", h - 1)
            idt = c.const("ident")
            a = t["a"].rearrange("p (t k) -> p t k", t=3)
            pe.transpose(ps[:, 6, 16:144], a[:, 1, 0:P], idt)
            pe.transpose(ps[:, 6, 0:16], a[0:16, 0, 0:P], idt[0:16, 0:16])
            pe.transpose(ps[:, 6, 144:272], a[:, 2, 0:P], idt)
            pe.transpose(ps[:, 7, 0:128], a[:, 1, P:2 * P], idt)
            pe.transpose(ps[:, 7, 128:256], a[:, 2, P:2 * P], idt)
            pe.transpose(ps[:, 6, 272:400], a[:, 2, 2 * P:3 * P], idt)
            for j in range(2):
                pe.transpose(ps[:, 4, j * P:j * P + P], t["vt"][:, j, 0:P], idt)
                pe.transpose(ps[:, 4, 256 + j * P:384 + j * P], t["vt"][:, j, P:2 * P], idt)
                m = pe.transpose(ps[:, 7, 256 + j * P:384 + j * P], t["vt"][:, j, 2 * P:3 * P], idt)
            m.then_inc(S("turned"), 1)

    head(0, None, True, False, False)
    head(1, None, True, True, False)
    with pe.Fori(0, HEADS - 2) as i:
        head(2, i, True, True, True)
    head(HEADS, None, False, True, True)
    head(HEADS + 1, None, False, False, True)


def attn_act(c, t, act):
    ps, S = c.ps, c.sem
    for n in range(2):
        split_hi(c, act, n)
    act.wait_ge(S("params_in"), 48)
    act.wait_ge(S("h_in"), 16)
    operands_act(c, act, 0, slice(0, ROWS), "pre0", 0)
    act.wait_ge(S("lam_sums"), 1)
    act.activation(t["lam"][:, 2:4], ps[:, 4, 0:2], ACT.Exp).then_inc(S("lam_exps"), 1)

    def head(h, i, proj, cur, old):
        n = 8 * h
        w = lambda sem, v: act.wait_ge(S(sem), at(v, i, 1))
        sp = lambda s: split_hi(c, act, n + s, i, 8)
        if proj:
            if h:
                sp(2)
                sp(3)
            sp(4)
        if h == 0:
            root(c, act, 7, t["sd"], slice(0, ROWS), S("stats_done"), 1, S("root_done"))
        if proj:
            sp(5)
        if cur:
            w("negmax_ready", h)
            if old:
                w("a_ready", h - 1)
            for comp in range(2):
                for q, a, b, keys in BLOCKS:
                    s = SCORES_AT[q]
                    m = act.activation(t["p"][a:b, comp, q, 0:keys], ps[a:b, 4 + comp, s:s + keys], ACT.Exp,
                                       bias=t["st"][a:b, 6 + 3 * comp + q:7 + 3 * comp + q], scale=SCALE,
                                       accum_out=t["st"][a:b, 12 + 3 * comp + q:13 + 3 * comp + q])
            m.then_inc(S("probs_ready"), 1)
        if old:
            w("o_ready", h - 1)
            act.activation(t["osq"][:], t["o"][:], ACT.Square).then_inc(S("osq_ready"), 1)
        if proj:
            sp(6)
            sp(7)
            sp(8)
        if old:
            w("osum_done", h - 1)
            act.activation(t["so"][:], ps[:, 5, 0:ROWS], ACT.Sqrt, bias=c.eps["eps"],
                           scale=1.0 / HEAD_V).then_inc(S("oroot_done"), 1)
        if cur:
            w("turned", h)
            act.copy(t["at"][:, 0, :], ps[:, 6, 0:272])
            act.copy(t["at"][:, 1, 16:272], ps[:, 7, 0:256])
            act.copy(t["vn"][:, 2, :], ps[:, 7, 256:512])
            act.copy(t["at"][:, 2, 144:272], ps[:, 6, 272:400]).then_inc(S("at_ready"), 1)
        if proj:
            sp(9)
            w("g_ready", h + 1)
            g = c.y[:, bass.ds(at(2 * h, i, 2), 2), :]
            act.activation(g, g, ACT.Silu).then_inc(S("gate_ready"), 1)
        if old:
            w("z_ready", h - 1)
            act.copy(c.xb[0][:, bass.ds(at(2 * h - 4, i, 2), 2), :], t["o"][:]).then_inc(S("z_hi_ready"), 1)

    head(0, None, True, False, False)
    head(1, None, True, True, False)
    with act.Fori(0, HEADS - 2) as i:
        head(2, i, True, True, True)
    head(HEADS, None, False, True, True)
    head(HEADS + 1, None, False, False, True)


def attn_pool(c, t, pool, st):
    S = c.sem
    pool.wait_ge(S("h_in"), 16)
    squares_pool(c, pool, st, 0, slice(0, ROWS), t["acc"], t["sq"])
    pool.wait_ge(S("stats_done"), 1)
    pool.memset(t["p"][:], 0.0)
    pool.memset(t["a"][:], 0.0)
    pool.memset(t["at"][:], 0.0)
    pool.memset(t["vt"][:], 0.0)
    pool.memset(t["st"][:, 12:18], 1.0)
    pool.memset(t["st"][:, 0:12], 0.0).then_inc(S("zeros_ready"), 1)


def attn_dve(c, t, dve, st):
    ps, S = c.ps, c.sem
    R = slice(0, ROWS)
    dve.memset(c.small[:, 0:1], EPS).then_inc(S("eps_ready"), 1)
    dve.memset(c.small[:, 1:2], RW_EPS).then_inc(S("eps_ready"), 1)
    for n in range(2):
        split_lo(c, dve, n)
    dve.wait_ge(S("params_in"), 48)
    lam = c.params[:, PARAM["lam"]:PARAM["lam"] + 4].rearrange("p (a b) -> p a b", b=2)
    dve.tensor_tensor(t["lam"][:, 0:2], lam[:, :, 0], lam[:, :, 1], ALU.mult).then_inc(S("lam_products"), 1)
    operands_dve(c, dve, st, 0, R, t, None, "pre0", 0)
    dve.wait_ge(S("lam_exps"), 1)
    st.did(dve.scalar_tensor_tensor(out=t["lam"][:, 4:5], in0=t["lam"][:, 2:3], scalar=LAM_INIT,
                                    in1=t["lam"][:, 3:4], op0=ALU.add, op1=ALU.subtract))
    first, _ = columns(CONSTS_FIRST)
    cos = t["first"][0:32, first["rope_cos"][0]:first["rope_cos"][1]]
    sin = t["first"][0:32, first["rope_sin"][0]:first["rope_sin"][1]]
    wide32 = lambda x, n: x.unsqueeze(1).to_broadcast([32, n, ROWS])
    swap = [(p + 16) % 32 for p in range(32)]
    a3 = t["a"].rearrange("p (t k) -> p t k", t=3)
    stat = lambda n, q: t["st"][:, n + q:n + q + 1]

    def head(h, i, proj, cur, old):
        n = 8 * h
        w = lambda sem, v: dve.wait_ge(S(sem), at(v, i, 1))
        sp = lambda s: split_lo(c, dve, n + s, i, 8)
        if proj:
            if h:
                sp(2)
                sp(3)
            sp(4)
            if h == 0:
                dve.wait_ge(S("root_done"), 1)
                st.did(dve.reciprocal(t["rs"][:], t["sd"][:]))
            dve.wait_ge(S("slot_used"), at(n + 4, i, 8))
            if cur:
                w("scores_done", h)
            dve.tensor_tensor(t["qk"][:], ps[:, 0:4, 0:ROWS], wide(t["rs"][:], 4), ALU.mult).then_inc(S("keys_taken"), 1)
            w("keys_taken", h + 1)
            for j in range(0, 4, 2):
                q = t["qk"][0:32, j:j + 2, :]
                dve.tensor_tensor(t["osq"][0:32], q, wide32(cos, 2), ALU.mult)
                st.did(dve.stream_shuffle(t["rot"][0:32], q, swap))
                st.did(dve.tensor_tensor(t["rot"][0:32], t["rot"][0:32], wide32(sin, 2), ALU.mult))
                m = dve.tensor_tensor(q, t["osq"][0:32], t["rot"][0:32], ALU.add)
                if j == 0:
                    st.did(m)
            m.then_inc(S("qk_ready"), 1)
            w("qk_ready", h + 1)
            sp(5)
        elif cur:
            w("scores_done", h)
        if cur:
            if h == 1:
                dve.wait_ge(S("zeros_ready"), 1)
            for q, a, b, keys in BLOCKS:
                s = SCORES_AT[q]
                m = dve.tensor_reduce(t["st"][a:b, q:q + 4:3], ps[a:b, 4:6, s:s + keys], AX.X, ALU.max)
            st.did(m)
            dve.tensor_scalar(t["st"][:, 6:12], t["st"][:, 0:6], -SCALE, None, ALU.mult).then_inc(S("negmax_ready"), 1)
        if old:
            w("values_done", h - 1)
            dve.tensor_copy(t["o"][:], ps[:, 6:8, 0:ROWS]).then_inc(S("o_ready"), 1)
        if cur:
            w("probs_ready", h)
            st.did(dve.reciprocal(t["st"][:, 18:24], t["st"][:, 12:18]))
            st.did(dve.tensor_scalar(t["st"][:, 21:24], t["st"][:, 21:24], t["lam"][:, 4:5], None, ALU.mult))
            for q in range(3):
                m = dve.tensor_scalar(t["p"][:, 1, q, :], t["p"][:, 1, q, :], stat(21, q), None, ALU.mult)
            st.did(m)
            for q in range(3):
                m = dve.scalar_tensor_tensor(out=a3[:, q, 0:ROWS], in0=t["p"][:, 0, q, :], scalar=stat(18, q),
                                             in1=t["p"][:, 1, q, :], op0=ALU.mult, op1=ALU.subtract)
            m.then_inc(S("a_ready"), 1)
        if proj:
            sp(6)
            sp(7)
            sp(8)
            dve.wait_ge(S("slot_used"), at(n + 8, i, 8))
        if cur:
            w("turned", h)
        if proj:
            if h == 0:
                dve.wait_ge(S("zeros_ready"), 1)
            dve.tensor_tensor(c.y[:, bass.ds(at(2 * h, i, 2), 2), :], ps[:, 2:4, 0:ROWS], wide(t["rs"][:], 2),
                              ALU.mult).then_inc(S("g_ready"), 1)
            dve.tensor_tensor(t["vt"][:, :, 0:ROWS], ps[:, 0:2, 0:ROWS], wide(t["rs"][:], 2),
                              ALU.mult).then_inc(S("values_out_taken"), 1)
        if cur:
            dve.tensor_copy(t["vn"][:, 0:2, :], ps[:, 4, :].rearrange("p (b n) -> p b n", b=2)).then_inc(S("vn_ready"), 1)
        if proj:
            sp(9)
        if old:
            w("oroot_done", h - 1)
            st.did(dve.reciprocal(t["ro"][:], t["so"][:]))
            w("o_ready", h - 1)
            st.did(dve.tensor_tensor(t["o"][:], t["o"][:], wide(t["ro"][:], 2), ALU.mult))
            w("gate_ready", h - 1)
            for j in range(2):
                m = dve.scalar_tensor_tensor(out=t["o"][:, j, :], in0=t["o"][:, j, :], scalar=t["gain"][:, j:j + 1],
                                             in1=c.y[:, bass.ds(at(2 * h - 4 + j, i, 2), 1), :].rearrange("p a r -> p (a r)"),
                                             op0=ALU.mult, op1=ALU.mult)
            m.then_inc(S("z_ready"), 1)
            w("z_hi_ready", h - 1)
            w("z_ready", h - 1)
            zs = bass.ds(at(2 * h - 4, i, 2), 2)
            dve.tensor_tensor(c.xb[1][:, zs, :], t["o"][:], c.xb[0][:, zs, :].bitcast(F32),
                              ALU.subtract).then_inc(S("z_lo_ready"), 1)
            w("z_lo_ready", h - 1)

    st.did(dve.tensor_scalar(t["gain"][:], c.params[:, PARAM["subln"]:PARAM["subln"] + 2], 1.0 - LAM_INIT, None, ALU.mult))
    head(0, None, True, False, False)
    head(1, None, True, True, False)
    with dve.Fori(0, HEADS - 2) as i:
        st.enter(i, 11)
        head(2, i, True, True, True)
    st.leave(HEADS - 2)
    head(HEADS, None, False, True, True)
    head(HEADS + 1, None, False, False, True)



def norm_between_pe(c, pe, t, base, cols, norm):
    sum_squares(c, pe, t["acc"], 0, cols, c.sem("y_added"), base // 4 * 3 + 3, c.sem("stats_done"))


def boundary_act(c, act, t, b, norm, cols, g_pre, n):
    root(c, act, 0, t["sd"], cols, c.sem("stats_done"), norm + 1, c.sem("root_done"))
    operands_act(c, act, b, cols, g_pre, n)


def boundary_dve(c, dve, st, t, b, norm, cols, g_post, g_pre, n):
    dve.wait_ge(c.sem("root_done"), norm + 1)
    st.did(dve.reciprocal(t["rs"][:, cols], t["sd"][:, cols]))
    operands_dve(c, dve, st, b, cols, t, g_post, g_pre, n)


def pre_root_act(c, act, t, norm, cols):
    root(c, act, 7, t["sd"], cols, c.sem("stats_done"), norm + 1, c.sem("root_done"))


def pre_root_dve(c, dve, st, t, norm, cols):
    dve.wait_ge(c.sem("root_done"), norm + 1)
    st.did(dve.reciprocal(t["rs"][:, cols], t["sd"][:, cols]))


def first_chunk_pe(c, pe, t, n0, x, b, cols, norm, squares):
    for s in range(4):
        pe.wait_ge(c.sem("x_ready"), 4 * b + s + 1)
        products(c, pe, n0 + s, x, [(k, 4 * s + k) for k in range(4)],
                 banks(c, 0, cols.stop - cols.start), cols, s == 0, s == 3)
    if squares:
        sum_squares(c, pe, t["acc"], 7, cols, c.sem("squares_ready"), squares, c.sem("stats_done"))


def mid_pe(c, t, pe):
    S = c.sem
    R = slice(0, ROWS)
    n0 = FIRST_SLOT["attn_out"]
    pe.wait_ge(S("z_lo_ready"), HEADS)
    y_stage_pe(c, pe, n0, c.xb, R, 0)
    norm_between_pe(c, pe, t, 0, R, 1)
    n0 = FIRST_SLOT["pool_in"]
    first_chunk_pe(c, pe, t, n0, c.xa, 1, R, 2, 2)

    def chunk(n, half, free, i=None, pause=None):
        if free is not None:
            pe.wait_ge(S("pool_in_taken"), at(free, i, 2))
        for s in range(4):
            products(c, pe, n + s, c.xa, [(k, 4 * s + k) for k in range(4)], banks(c, half, ROWS), R, s == 0, s == 3, i, 8,
                     pause=pause if s == 0 else None)

    chunk(n0 + 4, 1, None, pause=lambda: pe.wait_ge(S("root_done"), 3))
    with pe.Fori(0, 3) as i:
        chunk(n0 + 8, 0, 1, i)
        chunk(n0 + 12, 1, 2, i)
    for g in range(4):
        pe.wait_ge(S("pool_in_taken" if g < 2 else "pooled_done"), 7 + g if g < 2 else g - 1)
        pe.wait_ge(S("mixed_ready"), g + 1)
        products(c, pe, FIRST_SLOT["pool_group"] + g, c.xb, [(k, 4 * g + k) for k in range(4)],
                 banks(c, g % 2, ROWS), R, True, True)
    n0 = FIRST_SLOT["pool_out"]
    pe.wait_ge(S("pooled_done"), 3)
    y_stage_pe(c, pe, n0, c.xa, BOTH, 4, lambda s: pe.wait_ge(S("pooled_ready"), s + 1))
    norm_between_pe(c, pe, t, 4, BOTH, 3)


def mid_act(c, t, act):
    S = c.sem
    R = slice(0, ROWS)
    n0 = FIRST_SLOT["attn_out"]
    y_stage_split(c, lambda n: split_hi(c, act, n), lambda chunk, n: y_take_act(c, act, chunk, R, 0, t), n0)
    boundary_act(c, act, t, 1, 1, R, "pre1", FIRST_SLOT["pool_in"])
    n0 = FIRST_SLOT["pool_in"]

    def mixed(g):
        act.wait_ge(S("mixed_done"), g + 1)
        act.copy(c.xb[0][:, 4 * g:4 * g + 4, :], t["mixed"][:]).then_inc(S("mixed_hi"), 1)

    for m in range(4, 34):
        split_hi(c, act, n0 + m)
        if m == 5:
            pre_root_act(c, act, t, 2, R)
        if m % 4 == 3 and 7 <= m <= 19:
            mixed((m - 7) // 4)
        if m % 4 == 1 and m >= 21:
            chunk = (m - 5) // 4
            act.wait_ge(S("pool_in_taken"), chunk + 1)
            g = c.y[:, 4 * chunk - 16:4 * chunk - 12, :]
            act.activation(g, g, ACT.Silu).then_inc(S("pool_gate"), 1)
    for g in range(4):
        split_hi(c, act, n0 + 34 + g)
        act.wait_ge(S("pooled_done"), g + 1)
        act.copy(c.xa[0][:, 4 * g:4 * g + 4, :], t["tmp"][:]).then_inc(S("pooled_hi"), 1)
    y_tail(c, lambda n: split_hi(c, act, n), lambda chunk, n: y_take_act(c, act, chunk, BOTH, 4, t),
           FIRST_SLOT["pool_out"])
    boundary_act(c, act, t, 2, 3, BOTH, "pre_mix", FIRST_SLOT["rw_down"])


def y_tail(c, split, take, n0):
    y_stage_split(c, split, take, n0)


def mid_pool(c, t, pool, st):
    S = c.sem
    R = slice(0, ROWS)
    squares_pool(c, pool, st, 1, R, t["acc"], t["sq"])
    first, _ = columns(CONSTS_FIRST)
    for g, width in enumerate(POOL_WINDOWS):
        u = t["u"][g % 2]
        pool.wait_ge(S("pool_in_taken"), g + 1)
        src, flip = u, 0
        for n in range(g + 1):
            s, dst = 2 ** n, t["sums"][flip]
            pool.tensor_copy(dst[:, :, 0:s], src[:, :, 0:s])
            st.did(pool.tensor_tensor(dst[:, :, s:], src[:, :, s:], src[:, :, 0:ROWS - s], ALU.add))
            src, flip = dst, 1 - flip
        a = first["inv_count"][0] + 16 * g
        count = t["first"][:, a:a + 16]
        if g:
            pool.wait_ge(S("mixed_ready"), g)
        pool.tensor_tensor(t["mixed"][:, :, 0:16], src[:, :, 0:16], wide(count, 4), ALU.mult)
        st.did(pool.tensor_scalar(t["mixed"][:, :, 16:], src[:, :, 16:], 1.0 / width, None, ALU.mult))
        pool.tensor_tensor(t["mixed"][:], t["mixed"][:], u[:], ALU.subtract).then_inc(S("mixed_done"), 1)
        pool.wait_ge(S("mixed_done"), g + 1)
    squares_pool(c, pool, st, 2, BOTH, t["acc"], t["sq"])


def mid_dve(c, t, dve, st):
    S, ps = c.sem, c.ps
    R = slice(0, ROWS)
    n0 = FIRST_SLOT["attn_out"]
    y_stage_split(c, lambda n: split_lo(c, dve, n), lambda chunk, n: y_take_dve(c, dve, chunk, n - 1, R, 0, t), n0)
    boundary_dve(c, dve, st, t, 1, 1, R, "post0", "pre1", FIRST_SLOT["pool_in"])
    n0 = FIRST_SLOT["pool_in"]

    def mixed(g):
        dve.wait_ge(S("mixed_hi"), g + 1)
        dve.tensor_tensor(c.xb[1][:, 4 * g:4 * g + 4, :], t["mixed"][:], c.xb[0][:, 4 * g:4 * g + 4, :].bitcast(F32),
                          ALU.subtract).then_inc(S("mixed_ready"), 1)

    for m in range(4, 34):
        split_lo(c, dve, n0 + m)
        if m == 5:
            pre_root_dve(c, dve, st, t, 2, R)
        if m % 4 == 1:
            chunk = (m - 5) // 4
            dve.wait_ge(S("slot_used"), n0 + m - 1)
            if 2 <= chunk < 4:
                dve.wait_ge(S("mixed_done"), chunk - 1)
            out = t["u"][chunk % 2][:] if chunk < 4 else c.y[:, 4 * chunk - 16:4 * chunk - 12, :]
            dve.tensor_tensor(out, ps[:, 4 * (chunk % 2):4 * (chunk % 2) + 4, 0:ROWS], wide(t["rs"][:], 4),
                              ALU.mult).then_inc(S("pool_in_taken"), 1)
        if m % 4 == 3 and 7 <= m <= 19:
            mixed((m - 7) // 4)
    for g in range(4):
        split_lo(c, dve, n0 + 34 + g)
        dve.wait_ge(S("slot_used"), n0 + 33 + g)
        dve.wait_ge(S("pool_gate"), g + 1)
        for j in range(4):
            k = 4 * g + j
            m = dve.scalar_tensor_tensor(out=t["tmp"][:, j, :], in0=ps[:, 4 * (g % 2) + j, 0:ROWS], scalar=c.param("pool_scale", k),
                                         in1=c.y[:, k, :], op0=ALU.mult, op1=ALU.mult)
        m.then_inc(S("pooled_done"), 1)
        dve.wait_ge(S("pooled_done"), g + 1)
        dve.wait_ge(S("pooled_hi"), g + 1)
        dve.tensor_tensor(c.xa[1][:, 4 * g:4 * g + 4, :], t["tmp"][:], c.xa[0][:, 4 * g:4 * g + 4, :].bitcast(F32),
                          ALU.subtract).then_inc(S("pooled_ready"), 1)
        dve.wait_ge(S("pooled_ready"), g + 1)
    y_tail(c, lambda n: split_lo(c, dve, n), lambda chunk, n: y_take_dve(c, dve, chunk, n - 1, BOTH, 4, t),
           FIRST_SLOT["pool_out"])
    boundary_dve(c, dve, st, t, 2, 3, BOTH, "post1", "pre_mix", FIRST_SLOT["rw_down"])



CHUNKS = SEQ // RW_N
DECAY = math.exp(-0.5)


def unit(j, cc, p):
    return p * 8 + j * 2 + cc


def angles_dve(c, t, dve, st):
    pi = 3.1415925
    parts = (6.28125, 2029 * 2.0 ** -20, 2 * math.pi - 6.28125 - 2029 * 2.0 ** -20)
    x, turns = t["cos2"], t["sin2"]
    dve.wait_ge(c.sem("positions_in"), 16)
    st.did(dve.tensor_copy(t["kpe"][:], t["positions"][:]))
    st.did(dve.tensor_scalar(x[:], t["kpe"][:], c.param("inv_freq", 0), None, ALU.mult))
    st.did(dve.tensor_scalar(turns[:], x[:], 1 / (2 * math.pi), 12582912.0, ALU.mult, ALU.add))
    st.did(dve.tensor_scalar(turns[:], turns[:], 12582912.0, None, ALU.subtract))
    for part in parts:
        st.did(dve.scalar_tensor_tensor(out=x[:], in0=turns[:], scalar=-part, in1=x[:], op0=ALU.mult, op1=ALU.add))
    st.did(dve.tensor_scalar(turns[:], x[:], pi, -pi, ALU.min, ALU.max))
    st.did(dve.tensor_scalar(t["kpe"][:], x[:], math.pi / 2, 2 * math.pi, ALU.is_gt, ALU.mult))
    st.did(dve.scalar_tensor_tensor(out=x[:], in0=x[:], scalar=math.pi / 2, in1=t["kpe"][:], op0=ALU.add, op1=ALU.subtract))
    dve.tensor_scalar(x[:], x[:], pi, -pi, ALU.min, ALU.max).then_inc(c.sem("angles_ready"), 1)


def shifted(c, dve, st, t, half, tiles, mu, mu_at, out, taken):
    z = t["zp"]
    dve.memset(z[:, :, 0:1], 0.0)
    st.did(dve.tensor_tensor(z[:, :, 1:257], c.ps[:, 4 * half:4 * half + 4, 0:SEQ], wide(t["rs"][:, BOTH], 4), ALU.mult))
    st.did(dve.tensor_tensor(out[:, 0:tiles, :], z[:, 0:tiles, 0:256], z[:, 0:tiles, 1:257], ALU.subtract))
    for j in range(tiles):
        m = dve.scalar_tensor_tensor(out=out[:, j, :], in0=out[:, j, :], scalar=c.param(mu, mu_at + j),
                                     in1=z[:, j, 1:257], op0=ALU.mult, op1=ALU.add)
    m.then_inc(c.sem(taken), 1)


def rw_pe(c, t, pe):
    ps, S = c.ps, c.sem
    first_chunk_pe(c, pe, t, FIRST_SLOT["rw_down"], c.xa, 2, BOTH, 4, 3)
    t4 = lambda s: [(k, 4 * s + k) for k in range(4)]
    ones = c.const("head_ones")
    at_, cuts = [slice(0, 64), slice(64, 128)], [slice(64 * x, 64 * x + 64) for x in range(CHUNKS)]

    def head_sums(src, bank, done):
        for j in range(4):
            m = pe.matmul(ps[:, bank + j // 2, 256 * (j % 2):256 * (j % 2) + 256], ones, src[:, j, :], start=True, stop=True)
        m.then_inc(S(done), 1)

    for b in range(2):
        n = FIRST_SLOT[f"rw_half{b}"]
        if b:
            pe.wait_ge(S("yt_added"), 3)
        for s in range(4):
            pause = (lambda: pe.wait_ge(S("root_done"), 5)) if s == b == 0 else None
            products(c, pe, n + s, c.xa, t4(s), banks(c, 1, SEQ), BOTH, s == 0, s == 3, pause=pause)
        pe.wait_ge(S("lo_done"), n + 5)
        pe.wait_ge(S("lora_ready"), 1)
        pe.wait_ge(S("vars_rooted" if b else "down_taken_rw"), 1)
        w_hi, w_lo = c.w_hi[(n + 4) % SPLIT], c.w_lo[(n + 4) % SPLIT]
        x_hi, x_lo = t["lora_hi"], t["lora_lo"]
        for bank, parts in ((0, [(0, at_[0])]), (2, [(0, at_[1])]), (4, [(1, slice(0, P)), (2, slice(0, P))])):
            if bank == 4:
                pe.wait_ge(S("rw_k_taken"), b + 1)
            for j in range(4):
                out = ps[:, bank + j // 2, 256 * (j % 2):256 * (j % 2) + 256]
                for k, rows in parts:
                    a = slice(j * P, j * P + P)
                    pe.matmul(out, w_hi[rows, k, a], x_hi[rows, k, :], start=k == parts[0][0], stop=False)
                    pe.matmul(out, w_hi[rows, k, a], x_lo[rows, k, :], start=False, stop=False)
                    m = pe.matmul(out, w_lo[rows, k, a], x_hi[rows, k, :], start=False, stop=k == parts[-1][0])
        m.then_inc(S("slot_used"), 1)
        pe.wait_ge(S("wa_taken"), b + 1)
        for s in range(4):
            products(c, pe, n + 5 + s, c.xa, t4(s), banks(c, 0, SEQ), BOTH, s == 0, s == 3)
            if s == 1:
                pe.wait_ge(S("kk_squared"), b + 1)
                head_sums(t["bon"], 6, "kk_summed")
        pe.wait_ge(S("g_taken"), b + 1)
        pe.wait_ge(S("kk_rooted"), b + 1)
        for s in range(4):
            products(c, pe, n + 9 + s, c.xa, t4(s), banks(c, 1, SEQ), BOTH, s == 0, s == 3)
        pe.wait_ge(S("bonus_in"), b + 1)
        head_sums(t["bon"], 0, "bonus_summed")
        pe.wait_ge(S("tilde_ready"), b + 1)
        pe.wait_ge(S("bonus_taken"), b + 1)
        pe.wait_ge(S("rw_v_taken"), b + 1)
        for base, src, done in ((0, t["bt"], "gram_b"), (4, t["kt"], "gram_k")):
            for j in range(4):
                for x in range(CHUNKS):
                    for p in range(2):
                        u = unit(j, x // 2, p)
                        m = pe.matmul(ps[at_[x % 2], base + u // 4, 128 * (u % 4):128 * (u % 4) + 128],
                                      src[at_[p], j, cuts[x]], t["ar"][at_[p], j, x, :], start=True, stop=True)
            m.then_inc(S(done), 1)
        pe.wait_ge(S("gram_b_taken"), b + 1)
        for j in range(4):
            for x in range(CHUNKS):
                for p in range(2):
                    u = unit(j, x // 2, p)
                    m = pe.matmul(ps[at_[x % 2], u // 8, 64 * (u % 8):64 * (u % 8) + 64],
                                  t["ar"][at_[p], j, x, 0:64], t["bt"][at_[p], j, cuts[x]], start=True, stop=True)
        m.then_inc(S("gram_l"), 1)
        pe.wait_ge(S("gram_k_taken"), b + 1)
        pe.wait_ge(S("gram_l_taken"), b + 1)
        for level in range(1, 6):
            v = 2 * (5 * b + level - 1)
            pe.wait_ge(S("masked_ready"), 5 * b + level)
            for g in range(2):
                if level > 1:
                    pe.wait_ge(S("xy_ready"), v - 2 + g + 1)
                for u in range(8 * g, 8 * g + 8):
                    for q in range(2):
                        m = pe.matmul(ps[at_[q], g, 64 * (u % 8):64 * (u % 8) + 64], t["lm"][at_[q], u, :],
                                      t["yy"][at_[q], u, :], start=True, stop=True)
                m.then_inc(S("tm_done"), 1)
            for g in range(2):
                pe.wait_ge(S("t_ready"), v + g + 1)
                for u in range(8 * g, 8 * g + 8):
                    for q in range(2):
                        cut = slice(64 * (u % 8), 64 * (u % 8) + 64)
                        if level < 5:
                            pe.matmul(ps[at_[q], 2 + g, cut], t["tt"][at_[q], u, :], t["xx"][at_[q], u, :], start=True, stop=True)
                        m = pe.matmul(ps[at_[q], 4 + g, cut], t["xx"][at_[q], u, :], t["tt"][at_[q], u, :], start=True, stop=True)
                m.then_inc(S("xy_done"), 1)
        pe.wait_ge(S("xy_ready"), 10 * b + 10)
        for n_, (src, base) in enumerate(((t["bt"], 0), (t["kt"], 2), (t["v"], 6))):
            for j in range(4):
                for cc in range(2):
                    m = pe.transpose(ps[:, base + j // 2, 128 * (2 * (j % 2) + cc):128 * (2 * (j % 2) + cc) + 128],
                                     src[:, j, 128 * cc:128 * cc + 128], c.const("ident"))
            m.then_inc(S("turned_rw"), 1)
        pe.wait_ge(S("turned_taken"), 3 * b + 3)
        for p in range(2):
            for u in range(8 * p, 8 * p + 8):
                for q in range(2):
                    m = pe.matmul(ps[at_[q], p, 64 * (u % 8):64 * (u % 8) + 64], t["la"][at_[q], u, :], t["nv"][at_[q], u, :],
                                  start=True, stop=True)
        m.then_inc(S("lv_done"), 1)
        pe.wait_ge(S("lv_taken"), b + 1)
        for x in range(CHUNKS):
            q, cc, v = x % 2, x // 2, CHUNKS * b + x
            own = [(p, j, unit(j, cc, p), 4 * p + j, slice(64 * j, 64 * j + 64)) for p in range(2) for j in range(4)]
            if x:
                pe.wait_ge(S("state_ready"), 3 * b + x)
                for p, j, u, u8, cut in own:
                    m = pe.matmul(ps[at_[q], 4 + p, cut], t["ar"][at_[p], j, x, 0:64], t["state"][at_[p], j, :], start=True, stop=True)
                m.then_inc(S("p_done"), 1)
                pe.wait_ge(S("yt_copied"), v)
                if x > 1:
                    pe.wait_ge(S("yt_added"), 3 * b + x - 1)
                for p, j, u, u8, cut in own:
                    m = pe.matmul(ps[at_[p], 2, cut], t["state"][at_[p], j, :], t["ar"][at_[p], j, x, 64:128], start=True, stop=True)
                m.then_inc(S("ys_done"), 1)
                pe.wait_ge(S("p_taken"), 3 * b + x)
            for p, j, u, u8, cut in own:
                rhs = t["pb"][at_[q], u8, :] if x else t["la"][at_[q], u, :]
                m = pe.matmul(ps[at_[q], 6, 64 * u8:64 * u8 + 64], t["yy"][at_[q], u, :], rhs, start=True, stop=True)
            m.then_inc(S("sa_done"), 1)
            pe.wait_ge(S("sa_taken"), v + 1)
            if x < CHUNKS - 1:
                for p, j, u, u8, cut in own:
                    out = ps[at_[p], 7, cut]
                    pe.matmul(out, t["nb"][at_[q], u, :], t["sa"][at_[q], u8, :], start=True, stop=False)
                    m = pe.matmul(out, t["nk"][at_[q], u, :], t["nv"][at_[q], u, :], start=False, stop=True)
                m.then_inc(S("ds_done"), 1)
            for p, j, u, u8, cut in own:
                out = ps[at_[p], 3, cut]
                pe.matmul(out, t["sa"][at_[q], u8, :], t["mr"][at_[q], u, :], start=True, stop=False)
                m = pe.matmul(out, t["nv"][at_[q], u, :], t["mk"][at_[q], u, :], start=False, stop=True)
            m.then_inc(S("yt_done"), 1)
        pe.wait_ge(S("yt_added"), 3 * (b + 1))
        head_sums(t["yt"], 0, "means_done")
        pe.wait_ge(S("centred_squared"), b + 1)
        head_sums(t["sq"], 2, "vars_done")


def rw_act(c, t, act):
    ps, S = c.ps, c.sem
    n = FIRST_SLOT["rw_down"]
    half = lambda x: ps[:, x:x + 2, :].rearrange("p b (j r) -> p (b j) r", j=2)
    for m in range(4, 6):
        split_hi(c, act, n + m)
    root(c, act, 7, t["sd"], BOTH, S("stats_done"), 5, S("root_done"))
    act.wait_ge(S("down_taken_rw"), 1)
    x = t["lora"]
    act.activation(x[0:64, 0, :], x[0:64, 0, :], ACT.Tanh)
    act.activation(x[:, 1:3, :], x[:, 1:3, :], ACT.Sigmoid).then_inc(S("lora_acts"), 1)
    act.wait_ge(S("lora_acts"), 1)
    act.copy(t["lora_hi"][:], x[:]).then_inc(S("lora_hi"), 1)
    act.wait_ge(S("angles_ready"), 1)
    act.activation(t["sin2"][:], t["sin2"][:], ACT.Sin)
    act.activation(t["cos2"][:], t["cos2"][:], ACT.Sin).then_inc(S("sines_ready"), 1)
    for b in range(2):
        n = FIRST_SLOT[f"rw_half{b}"]
        for m in range(2, 7):
            split_hi(c, act, n + m)
        for bank, out, name in ((0, t["w"], "w0"), (2, t["a"], "a0")):
            for j in range(4):
                m = act.activation(out[:, j, :], ps[:, bank + j // 2, 256 * (j % 2):256 * (j % 2) + 256], ACT.Sigmoid,
                                   bias=c.param(name, 4 * b + j))
        m.then_inc(S("wa_taken"), 1)
        act.copy(t["g"][:], half(4)).then_inc(S("g_taken"), 1)
        split_hi(c, act, n + 7)
        split_hi(c, act, n + 8)
        act.wait_ge(S("kk_summed"), b + 1)
        act.activation(t["bon"][:], half(6), ACT.Sqrt).then_inc(S("kk_rooted"), 1)
        split_hi(c, act, n + 9)
        act.wait_ge(S("logs_ready"), b + 1)
        act.activation(t["w"][:], t["w"][:], ACT.Exp, scale=-DECAY)
        act.activation(t["cs"][:], t["tt4"], ACT.Exp, scale=-DECAY).then_inc(S("exp_w"), 1)
        act.wait_ge(S("exp_w"), b + 1)
        act.activation(t["tt4"], t["tt4"], ACT.Exp, scale=DECAY).then_inc(S("exps_ready"), 1)
        for m in range(10, 15):
            split_hi(c, act, n + m)
        for level in range(1, 6):
            for g in range(2):
                v = 2 * (5 * b + level - 1) + g + 1
                act.wait_ge(S("tm_done"), v)
                act.copy(t["tt"][:, 8 * g:8 * g + 8, :], ps[:, g, :].rearrange("p (u i) -> p u i", u=8)).then_inc(S("t_ready"), 1)
        for i, (dst, base) in enumerate(((t["nb"], 0), (t["nk"], 2), (t["nv"], 6))):
            act.wait_ge(S("turned_rw"), 3 * b + i + 1)
            act.copy(dst[:].rearrange("p (q u) i -> p q u i", q=2),
                     ps[:, base:base + 2, :].rearrange("p b (m q i) -> p q (b m) i", m=4, q=2)).then_inc(S("turned_taken"), 1)
        act.wait_ge(S("lv_done"), b + 1)
        act.copy(t["la"][:], ps[:, 0:2, :].rearrange("p b (u i) -> p (b u) i", u=8)).then_inc(S("lv_taken"), 1)
        for x in range(CHUNKS):
            q, v = slice(64 * (x % 2), 64 * (x % 2) + 64), CHUNKS * b + x + 1
            act.wait_ge(S("sa_done"), v)
            act.copy(t["sa"][q], ps[q, 6, :].rearrange("p (u i) -> p u i", u=8)).then_inc(S("sa_taken"), 1)
            act.wait_ge(S("yt_done"), v)
            act.copy(t["yt"][:, :, 64 * x:64 * x + 64], ps[:, 3, 0:256].rearrange("p (j i) -> p j i", j=4)).then_inc(S("yt_copied"), 1)
        act.wait_ge(S("centred"), b + 1)
        act.activation(t["sq"][:], t["yt"][:], ACT.Square).then_inc(S("centred_squared"), 1)
        act.wait_ge(S("vars_done"), b + 1)
        act.activation(t["sq"][:], half(2), ACT.Sqrt, bias=c.eps["rw"], scale=1.0 / RW_N).then_inc(S("vars_rooted"), 1)


def rw_pool(c, t, pool, st, a):
    S = c.sem
    pool.wait_ge(S("squares_ready"), 3)
    pool.wait_ge(S("stats_done"), 5)
    pool.wait_ge(S("x_ready"), 12)
    pool.dma_start(t["masks"][:], a["consts_rw"]).then_inc(S("consts_rw_in"), 16)
    pool.dma_start(t["positions"][:], a["positions"].partition_broadcast(P)).then_inc(S("positions_in"), 16)
    masks, _ = columns(CONSTS_RW)
    for b in range(2):
        pool.wait_ge(S("rw_k_taken"), b + 1)
        for j in range(4):
            m = pool.tensor_scalar(t["kk"][:, j, :], t["k"][:, j, :], c.param("k_k", 4 * b + j), None, ALU.mult)
        st.did(m)
        pool.tensor_tensor(t["bon"][:], t["kk"][:], t["kk"][:], ALU.mult).then_inc(S("kk_squared"), 1)
        pool.wait_ge(S("consts_rw_in"), 16)
        pool.wait_ge(S("gram_l_taken"), b + 1)
        for level in range(1, 6):
            if level > 1:
                pool.wait_ge(S("tm_done"), 2 * (5 * b + level - 1))
            mask = t["masks"][:, masks[f"level{level}"][0]:masks[f"level{level}"][1]]
            pool.tensor_tensor(t["lm"][:], t["ll"][:], wide(mask, 16), ALU.mult).then_inc(S("masked_ready"), 1)


def rw_dve(c, t, dve, st):
    ps, S = c.ps, c.sem
    n = FIRST_SLOT["rw_down"]
    masks, _ = columns(CONSTS_RW)
    mask = lambda name, k=16: wide(t["masks"][:, masks[name][0]:masks[name][1]], k)
    half = lambda x: ps[:, x:x + 2, :].rearrange("p b (j r) -> p (b j) r", j=2)
    for m in range(4, 6):
        split_lo(c, dve, n + m)
    dve.wait_ge(S("root_done"), 5)
    st.did(dve.reciprocal(t["rs"][:, BOTH], t["sd"][:, BOTH]))
    dve.wait_ge(S("slot_used"), n + 4)
    shifted(c, dve, st, t, 0, 3, "mu_lora", 0, t["lora"], "down_taken_rw")
    dve.wait_ge(S("down_taken_rw"), 1)
    dve.wait_ge(S("lora_hi"), 1)
    dve.tensor_tensor(t["lora_lo"][:], t["lora"][:], t["lora_hi"][:].bitcast(F32), ALU.subtract).then_inc(S("lora_ready"), 1)
    dve.wait_ge(S("consts_rw_in"), 16)
    angles_dve(c, t, dve, st)
    dve.wait_ge(S("sines_ready"), 1)
    st.did(dve.tensor_scalar(t["sin2"][:], t["sin2"][:], c.param("rope_sign", 0), None, ALU.mult))
    swap = [(p + 16) % 32 for p in range(32)]
    key = t["zp"][:, 3, 1:257]
    st.did(dve.stream_shuffle(t["kpe"][:], key, swap))
    dve.tensor_tensor(t["kpe"][:], t["kpe"][:], t["sin2"][:], ALU.mult)
    st.did(dve.tensor_tensor(key, key, t["cos2"][:], ALU.mult))
    st.did(dve.tensor_tensor(t["kpe"][:], t["kpe"][:], key, ALU.add))
    for b in range(2):
        n = FIRST_SLOT[f"rw_half{b}"]
        for m in range(2, 5):
            split_lo(c, dve, n + m)
        dve.wait_ge(S("slot_used"), n + 4)
        shifted(c, dve, st, t, 1, 4, "mu_rkv", 8 + 4 * b, t["k"], "rw_k_taken")
        dve.wait_ge(S("rw_k_taken"), b + 1)
        split_lo(c, dve, n + 5)
        split_lo(c, dve, n + 6)
        split_lo(c, dve, n + 7)
        dve.wait_ge(S("wa_taken"), b + 1)
        by_chunk = lambda x: x.rearrange("p j (x i) -> p (j x) i", x=CHUNKS)
        src, dst, other = t["w"][:], t["cs"][:], t["tt4"]
        for level in range(6):
            s, a, d = 2 ** level, by_chunk(src), by_chunk(dst)
            dve.tensor_copy(d[:, :, 0:s], a[:, :, 0:s])
            st.did(dve.tensor_tensor(d[:, :, s:], a[:, :, s:], a[:, :, 0:RW_N - s], ALU.add))
            src, dst, other = dst, other, dst
            if level == 2:
                split_lo(c, dve, n + 8)
        dve.tensor_tensor(t["w"][:], src, t["w"][:], ALU.subtract).then_inc(S("logs_ready"), 1)
        split_lo(c, dve, n + 9)
        dve.wait_ge(S("kk_rooted"), b + 1)
        st.did(dve.tensor_scalar(t["bon"][:], t["bon"][:], 1e-12, None, ALU.max))
        st.did(dve.reciprocal(t["bon"][:], t["bon"][:]))
        st.did(dve.tensor_tensor(t["kk"][:], t["kk"][:], t["bon"][:], ALU.mult))
        split_lo(c, dve, n + 10)
        st.did(dve.scalar_tensor_tensor(out=t["bon"][:], in0=t["a"][:], scalar=1.0, in1=t["k"][:], op0=ALU.subtract, op1=ALU.mult))
        for j in range(4):
            m = dve.scalar_tensor_tensor(out=t["k"][:, j, :], in0=t["bon"][:, j, :], scalar=c.param("k_a", 4 * b + j),
                                         in1=t["k"][:, j, :], op0=ALU.mult, op1=ALU.add)
        st.did(m)
        dve.wait_ge(S("exps_ready"), b + 1)
        ar = t["ar"][:].rearrange("p j x (s i) -> p (j x) s i", s=2)
        dve.scalar_tensor_tensor(out=ar[:, :, 0, :], in0=by_chunk(t["kk"][:]), scalar=-1.0, in1=by_chunk(t["w"][:]),
                                 op0=ALU.mult, op1=ALU.mult)
        dve.tensor_tensor(t["kt"][:], t["k"][:], t["tt4"], ALU.mult)
        st.did(dve.tensor_tensor(t["bt"][:], t["kk"][:], t["a"][:], ALU.mult))
        dve.wait_ge(S("slot_used"), n + 9)
        shifted(c, dve, st, t, 0, 4, "mu_rkv", 4 * b, t["r"], "rw_r_taken")
        st.did(dve.tensor_tensor(t["bt"][:], t["bt"][:], t["tt4"], ALU.mult))
        dve.wait_ge(S("rw_r_taken"), b + 1)
        split_lo(c, dve, n + 11)
        split_lo(c, dve, n + 12)
        dve.tensor_copy(t["ends"][:], t["cs"][:].rearrange("p j (x i) -> p j x i", x=CHUNKS)[:, :, :, RW_N - 1])
        dve.tensor_tensor(ar[:, :, 1, :], by_chunk(t["r"][:]), by_chunk(t["cs"][:]), ALU.mult).then_inc(S("tilde_ready"), 1)
        for j in range(4):
            m = dve.scalar_tensor_tensor(out=t["bon"][:, j, :], in0=t["r"][:, j, :], scalar=c.param("r_k", 4 * b + j),
                                         in1=t["k"][:, j, :], op0=ALU.mult, op1=ALU.mult)
        m.then_inc(S("bonus_in"), 1)
        split_lo(c, dve, n + 13)
        dve.wait_ge(S("slot_used"), n + 13)
        shifted(c, dve, st, t, 1, 4, "mu_rkv", 16 + 4 * b, t["v"], "rw_v_taken")
        dve.wait_ge(S("rw_v_taken"), b + 1)
        split_lo(c, dve, n + 14)
        dve.wait_ge(S("bonus_summed"), b + 1)
        dve.tensor_tensor(t["bon"][:], half(0), t["v"][:], ALU.mult).then_inc(S("bonus_taken"), 1)
        dve.wait_ge(S("gram_b"), b + 1)
        gram = lambda x, s: ps[:, x:x + 4, :].rearrange("p b (u s i) -> p (b u) s i", u=4, s=2)[:, :, s, :]
        dve.tensor_tensor(t["mr"][:], gram(0, 1), mask("upto"), ALU.mult)
        dve.tensor_tensor(t["yy"][:], gram(0, 0), mask("level0_t"), ALU.mult).then_inc(S("gram_b_taken"), 1)
        dve.wait_ge(S("gram_b_taken"), b + 1)
        st.did(dve.tensor_tensor(t["yy"][:], t["yy"][:], mask("eye"), ALU.add))
        dve.wait_ge(S("gram_k"), b + 1)
        dve.tensor_tensor(t["la"][:], gram(4, 0), mask("before"), ALU.mult)
        dve.tensor_tensor(t["mk"][:], gram(4, 1), mask("upto"), ALU.mult).then_inc(S("gram_k_taken"), 1)
        dve.wait_ge(S("gram_l"), b + 1)
        lower = ps[:, 0:2, :].rearrange("p b (u i) -> p (b u) i", u=8)
        st.did(dve.tensor_tensor(t["ll"][:], lower, mask("after"), ALU.mult))
        st.did(dve.tensor_tensor(t["xx"][:], t["ll"][:], mask("level0"), ALU.mult))
        dve.tensor_tensor(t["xx"][:], t["xx"][:], mask("eye"), ALU.add).then_inc(S("gram_l_taken"), 1)
        dve.wait_ge(S("gram_l_taken"), b + 1)
        for level in range(1, 6):
            for g in range(2):
                v = 2 * (5 * b + level - 1) + g + 1
                dve.wait_ge(S("xy_done"), v)
                us = slice(8 * g, 8 * g + 8)
                if level < 5:
                    st.did(dve.tensor_tensor(t["xx"][:, us, :], t["xx"][:, us, :], ps[:, 2 + g, :].rearrange("p (u i) -> p u i", u=8), ALU.add))
                dve.tensor_tensor(t["yy"][:, us, :], t["yy"][:, us, :], ps[:, 4 + g, :].rearrange("p (u i) -> p u i", u=8),
                                  ALU.add).then_inc(S("xy_ready"), 1)
                dve.wait_ge(S("xy_ready"), v)
        lv = t["la"][:].rearrange("p (q j y) i -> p q j y i", q=2, y=2)

        def y_added(x):
            dve.wait_ge(S("yt_copied"), CHUNKS * b + x + 1)
            dve.wait_ge(S("ys_done"), 3 * b + x)
            y = t["yt"][:, :, 64 * x:64 * x + 64]
            dve.tensor_tensor(y, y, ps[:, 2, 0:256].rearrange("p (j i) -> p j i", j=4), ALU.add).then_inc(S("yt_added"), 1)

        for x in range(CHUNKS):
            q, v = slice(64 * (x % 2), 64 * (x % 2) + 64), CHUNKS * b + x + 1
            if x:
                dve.wait_ge(S("p_done"), 3 * b + x)
                dve.tensor_tensor(t["pb"][q].rearrange("p (q j) i -> p q j i", q=2), lv[q, :, :, x // 2, :],
                                  ps[q, 4:6, 0:256].rearrange("p b (j i) -> p b j i", j=4), ALU.add).then_inc(S("p_taken"), 1)
            if x < CHUNKS - 1:
                end = t["ends"][:, :, x:x + 1].to_broadcast([P, 4, RW_N])
                grown = ps[:, 7, 0:256].rearrange("p (j i) -> p j i", j=4)
                dve.wait_ge(S("ds_done"), 3 * b + x + 1)
                if x:
                    st.did(dve.tensor_tensor(t["state"][:], t["state"][:], grown, ALU.add))
                    grown = t["state"][:]
                dve.tensor_tensor(t["state"][:], grown, end, ALU.mult).then_inc(S("state_ready"), 1)
                dve.wait_ge(S("state_ready"), 3 * b + x + 1)
            if x:
                y_added(x)
        dve.wait_ge(S("means_done"), b + 1)
        dve.scalar_tensor_tensor(out=t["yt"][:], in0=half(0), scalar=-1.0 / RW_N, in1=t["yt"][:],
                                 op0=ALU.mult, op1=ALU.add).then_inc(S("centred"), 1)
        dve.wait_ge(S("vars_rooted"), b + 1)
        st.did(dve.reciprocal(t["sq"][:], t["sq"][:]))
        st.did(dve.tensor_tensor(t["yt"][:], t["yt"][:], t["sq"][:], ALU.mult))
        for j in range(4):
            m = dve.tensor_scalar(t["yt"][:, j, :], t["yt"][:, j, :], c.param("lnx_w", 4 * b + j),
                                  c.param("lnx_b", 4 * b + j), ALU.mult, ALU.add)
        st.did(m)
        st.did(dve.tensor_tensor(t["yt"][:], t["yt"][:], t["bon"][:], ALU.add))
        dve.tensor_tensor(c.y[:, 4 * b:4 * b + 4, 0:SEQ], t["yt"][:], t["g"][:], ALU.mult).then_inc(S("rw_out"), 1)
        dve.wait_ge(S("rw_out"), b + 1)



MLA_BLOCKS = [(0, 0, 64, 64), (0, 64, 128, 128), (1, 0, 64, 192), (1, 64, 128, 256)]


def mla_pe(c, t, pe):
    ps, S = c.ps, c.sem
    n = FIRST_SLOT["mla_in"]
    pe.wait_ge(S("vars_rooted"), 2)
    for x in range(2):
        for s in range(4):
            products(c, pe, n + 4 * x + s, c.xa, [(k, 4 * s + k) for k in range(4)], banks(c, x, SEQ), BOTH, s == 0, s == 3)
    for x in range(2):
        pe.wait_ge(S("low_squared"), x + 1)
        for j in range(4):
            m = pe.matmul(ps[:, 4 * x, 0:SEQ], c.const("ones"), t["sq4"][:, j, :], start=j == 0, stop=j == 3)
        m.then_inc(S("low_summed"), 1)
    n = FIRST_SLOT["mla_q"]
    for x in range(7):
        if x < 2:
            pe.wait_ge(S("low_rooted"), x + 1)
        else:
            pe.wait_ge(S("up_taken"), x - 1)
        pe.wait_ge(S("low_ready"), 1 if x < 3 else 2)
        products(c, pe, n + x, c.xb, [(k, (8 if x < 3 else 12) + k) for k in range(4)], banks(c, x % 2, SEQ), BOTH, True, True)
        if x >= 5:
            pe.wait_ge(S("up_taken"), x + 1)
            for j in range(4):
                for kb in range(2):
                    m = pe.transpose(ps[:, 4 * (x % 2) + kb, P * j:P * j + P], t["vt4"][:, j, P * kb:P * kb + P], c.const("ident"))
            m.then_inc(S("v_turned"), 1)

    def scores(h):
        e, bank = h % 2, h % 2
        rows = slice(64 * e, 64 * e + 64)
        for b in range(2):
            out = ps[:, bank, SEQ * b:SEQ * b + P * (b + 1)]
            pe.matmul(out, t["qn"][:, h, P * b:P * b + P], t["kn"][:, h, 0:P * (b + 1)], start=True, stop=False)
            m = pe.matmul(out, t["qp"][rows, h // 2, P * b:P * b + P], t["kpe"][rows, 0:P * (b + 1)], start=False, stop=True)
        m.then_inc(S("mla_scores"), 1)

    def turned(h):
        bank = 2 + h % 2
        pe.wait_ge(S("mla_probs"), h + 1)
        pe.transpose(ps[:, bank, 0:P], t["pm"][:, h % 2, 0, 0:P], c.const("ident"))
        pe.transpose(ps[:, bank, P:2 * P], t["pm"][:, h % 2, 1, 0:P], c.const("ident"))
        pe.transpose(ps[:, bank, 2 * P:3 * P], t["pm"][:, h % 2, 1, P:2 * P], c.const("ident")).then_inc(S("mla_turned"), 1)

    def values(h):
        out = ps[:, 4 + h % 2, 0:SEQ]
        pe.wait_ge(S("mla_turned_taken"), h + 1)
        if h >= 2:
            pe.wait_ge(S("mla_out"), h - 1)
        pe.matmul(out, t["vn2"][:, 0, P * h:P * h + P], t["at2"][:, h % 2, 0:SEQ], start=True, stop=False)
        pe.matmul(out[:, P:], t["vn2"][:, 1, P * h:P * h + P], t["at2"][:, h % 2, SEQ:SEQ + P], start=False,
                  stop=True).then_inc(S("mla_values"), 1)

    pe.wait_ge(S("q_roped"), 1)
    pe.wait_ge(S("v_taken"), 2)
    scores(0)
    scores(1)
    for h in range(MLA_HEADS):
        turned(h)
        if h:
            values(h - 1)
        if h + 2 < MLA_HEADS:
            scores(h + 2)
    values(MLA_HEADS - 1)


def mla_act(c, t, act):
    ps, S = c.ps, c.sem
    n = FIRST_SLOT["mla_in"]
    for m in range(2, 10):
        split_hi(c, act, n + m)
        if m == 3:
            act.wait_ge(S("rw_out"), 2)
            act.copy(c.xb[0][:, 0:8, BOTH], c.y[:, 0:8, 0:SEQ]).then_inc(S("rw_hi"), 1)
        if m in (5, 9):
            x = (m - 5) // 4
            act.wait_ge(S("low_taken"), x + 1)
            if x:
                act.wait_ge(S("low_summed"), 1)
            act.activation(t["sq4"][:], t["low"][:, 4 * x:4 * x + 4, :], ACT.Square).then_inc(S("low_squared"), 1)
            for j in range(4):
                m_ = act.activation(c.xb[0][:, 8 + 4 * x + j, BOTH], t["low"][:, 4 * x + j, :], ACT.Copy,
                                    scale=c.param(("q_norm", "kv_norm")[x], j))
            m_.then_inc(S("low_hi"), 1)
    for x in range(2):
        act.wait_ge(S("low_summed"), x + 1)
        act.activation(t["low_rs"][:, x, :], ps[:, 4 * x, 0:SEQ], ACT.Sqrt, bias=c.eps["eps"], scale=1.0 / 512).then_inc(S("low_rooted"), 1)
    n = FIRST_SLOT["mla_q"]
    for x in range(7):
        split_hi(c, act, n + 2 + x)
        if x >= 5:
            act.wait_ge(S("v_turned"), x - 4)
            for kb in range(2):
                m = act.copy(t["vn2"][:, kb, 512 * (x - 5):512 * (x - 5) + 512], ps[:, 4 * (x % 2) + kb, :])
            m.then_inc(S("v_taken"), 1)

    def turned_taken(h):
        act.wait_ge(S("mla_turned"), h + 1)
        if h >= 2:
            act.wait_ge(S("mla_values"), h - 1)
        act.copy(t["at2"][:, h % 2, :], ps[:, 2 + h % 2, 0:3 * P]).then_inc(S("mla_turned_taken"), 1)

    def out_hi(h):
        act.wait_ge(S("mla_values"), h + 1)
        act.copy(c.xb[0][:, 8 + h, BOTH], ps[:, 4 + h % 2, 0:SEQ]).then_inc(S("mla_hi"), 1)

    for h in range(MLA_HEADS):
        act.wait_ge(S("mla_negmax"), h + 1)
        if h >= 2:
            act.wait_ge(S("mla_turned"), h - 1)
        for i, (b, a, z, keys) in enumerate(MLA_BLOCKS):
            m = act.activation(t["pm"][a:z, h % 2, b, 0:keys], ps[a:z, h % 2, SEQ * b:SEQ * b + keys], ACT.Exp,
                               bias=t["ms"][a:z, h % 2, 2 + b:3 + b], scale=MLA_SCALE, accum_out=t["ms"][a:z, h % 2, 4 + b:5 + b])
        m.then_inc(S("mla_exps"), 1)
        if h:
            turned_taken(h - 1)
        if h >= 2:
            out_hi(h - 2)
    turned_taken(MLA_HEADS - 1)
    out_hi(MLA_HEADS - 2)
    out_hi(MLA_HEADS - 1)


def mla_pool(c, t, pool, st):
    pool.wait_ge(c.sem("low_taken"), 1)
    pool.memset(t["pm"][:], 0.0)
    pool.memset(t["ms"][:], 0.0).then_inc(c.sem("mla_zeros"), 1)


def mla_dve(c, t, dve, st):
    ps, S = c.ps, c.sem
    n = FIRST_SLOT["mla_in"]
    for m in range(2, 10):
        split_lo(c, dve, n + m)
        if m == 3:
            dve.wait_ge(S("rw_hi"), 1)
            dve.tensor_tensor(c.xb[1][:, 0:8, BOTH], c.y[:, 0:8, 0:SEQ], c.xb[0][:, 0:8, BOTH].bitcast(F32),
                              ALU.subtract).then_inc(S("rw_operand"), 1)
        if m in (5, 9):
            x = (m - 5) // 4
            dve.wait_ge(S("slot_used"), n + 4 * x + 4)
            dve.tensor_tensor(t["low"][:, 4 * x:4 * x + 4, :], ps[:, 4 * x:4 * x + 4, 0:SEQ], wide(t["rs"][:, BOTH], 4),
                              ALU.mult).then_inc(S("low_taken"), 1)
            dve.wait_ge(S("low_taken"), x + 1)
            dve.wait_ge(S("low_hi"), x + 1)
            for j in range(4):
                m_ = dve.scalar_tensor_tensor(out=c.xb[1][:, 8 + 4 * x + j, BOTH], in0=t["low"][:, 4 * x + j, :],
                                              scalar=c.param(("q_norm", "kv_norm")[x], j),
                                              in1=c.xb[0][:, 8 + 4 * x + j, BOTH].bitcast(F32), op0=ALU.mult, op1=ALU.subtract)
            m_.then_inc(S("low_ready"), 1)
    dve.wait_ge(S("rw_operand"), 1)
    dve.wait_ge(S("low_rooted"), 2)
    st.did(dve.reciprocal(t["low_rs"][:], t["low_rs"][:]))
    n = FIRST_SLOT["mla_q"]
    outs = [t["qn"][:, 0:4, :], t["qn"][:, 4:8, :], t["qp"][:], t["kn"][:, 0:4, :], t["kn"][:, 4:8, :], t["vt4"][:], t["vt4"][:]]
    swap = [(p + 16) % 32 for p in range(32)]
    for x in range(7):
        split_lo(c, dve, n + 2 + x)
        dve.wait_ge(S("slot_used"), n + x + 1)
        if x == 5:
            dve.wait_ge(S("q_roped"), 1)
        if x == 6:
            dve.wait_ge(S("v_turned"), 1)
        dve.tensor_tensor(outs[x], ps[:, 4 * (x % 2):4 * (x % 2) + 4, 0:SEQ], wide(t["low_rs"][:, x // 3 if x < 6 else 1, :], 4),
                          ALU.mult).then_inc(S("up_taken"), 1)
        if x == 2:
            dve.wait_ge(S("up_taken"), 3)
            st.did(dve.stream_shuffle(t["vt4"][:], t["qp"][:], swap))
            dve.tensor_tensor(t["vt4"][:], t["vt4"][:], wide(t["sin2"][:], 4), ALU.mult)
            st.did(dve.tensor_tensor(t["qp"][:], t["qp"][:], wide(t["cos2"][:], 4), ALU.mult))
            dve.tensor_tensor(t["qp"][:], t["qp"][:], t["vt4"][:], ALU.add).then_inc(S("q_roped"), 1)
    dve.wait_ge(S("mla_zeros"), 1)

    def out_lo(h):
        dve.wait_ge(S("mla_hi"), h + 1)
        dve.tensor_tensor(c.xb[1][:, 8 + h, BOTH], ps[:, 4 + h % 2, 0:SEQ], c.xb[0][:, 8 + h, BOTH].bitcast(F32),
                          ALU.subtract).then_inc(S("mla_out"), 1)

    for h in range(MLA_HEADS + 1):
        if h < MLA_HEADS:
            dve.wait_ge(S("mla_scores"), h + 1)
            ms = t["ms"][:, h % 2, :]
            for b, a, z, keys in MLA_BLOCKS:
                m = dve.tensor_reduce(ms[a:z, b:b + 1], ps[a:z, h % 2, SEQ * b:SEQ * b + keys], AX.X, ALU.max)
            st.did(m)
            dve.tensor_scalar(ms[:, 2:4], ms[:, 0:2], -MLA_SCALE, None, ALU.mult).then_inc(S("mla_negmax"), 1)
        if h:
            g = h - 1
            dve.wait_ge(S("mla_exps"), g + 1)
            ms = t["ms"][:, g % 2, :]
            st.did(dve.reciprocal(ms[:, 6:8], ms[:, 4:6]))
            for b in range(2):
                m = dve.tensor_scalar(t["pm"][:, g % 2, b, :], t["pm"][:, g % 2, b, :], ms[:, 6 + b:7 + b], None, ALU.mult)
            m.then_inc(S("mla_probs"), 1)
            dve.wait_ge(S("mla_probs"), g + 1)
        if h >= 3:
            out_lo(h - 3)
    out_lo(MLA_HEADS - 2)
    out_lo(MLA_HEADS - 1)



def mix_pe(c, t, pe):
    S = c.sem
    n = FIRST_SLOT["mix"]
    t4 = lambda s: [(k, 4 * s + k) for k in range(4)]
    pe.wait_ge(S("mla_out"), MLA_HEADS)

    def turn(n, i=None):
        for x, (x_op, first, count) in enumerate(((c.xa, 0, 4), (c.xa, 4, 4), (c.xb, 8, 2), (c.xb, 10, 2))):
            if x >= 2 or i is not None:
                pe.wait_ge(S("mix_taken"), at(x - 1 if i is None else x + 3, i, 4))
            for s in range(count):
                products(c, pe, n + first + s, x_op, t4(s + (2 if x == 3 else 0)), banks(c, x % 2, SEQ), BOTH,
                         s == 0, s == count - 1, i, 12)

    turn(n)
    with pe.Fori(0, 3) as i:
        turn(n + 12, i)
    n = FIRST_SLOT["mix_out"]
    y_stage_pe(c, pe, n, c.xa, BOTH, 8, lambda s: pe.wait_ge(S("mix_ready"), s + 1))
    norm_between_pe(c, pe, t, 8, BOTH, 5)


MIX_TAKES = {5: 0, 9: 1, 11: 2, 13: 3}


def mix_act(c, t, act):
    S = c.sem
    n = FIRST_SLOT["mix"]

    def turn(n, i=None):
        for m in range(2, 14):
            split_hi(c, act, n + m, i, 12)
            if m in (5, 9):
                x = MIX_TAKES[m]
                act.wait_ge(S("mix_taken"), at(x + 1, i, 4) if i is None else at(x + 5, i, 4))
                act.activation(t["gates"][x][:], t["gates"][x][:], ACT.Sigmoid).then_inc(S("mix_gate"), 1)

    turn(n)
    with act.Fori(0, 3) as i:
        turn(n + 12, i)
    n = FIRST_SLOT["mix_out"]
    for kg in range(4):
        ks = slice(4 * kg, 4 * kg + 4)
        act.wait_ge(S("mixed"), 4)
        act.copy(c.xa[0][:, ks, BOTH], c.y[:, ks, 0:SEQ]).then_inc(S("mix_hi"), 1)
    y_stage_split(c, lambda n: split_hi(c, act, n), lambda chunk, n: y_take_act(c, act, chunk, BOTH, 8, t), n)
    boundary_act(c, act, t, 3, 5, BOTH, "pre_ffn", FIRST_SLOT["ffn"])


def mix_dve(c, t, dve, st):
    S, ps = c.sem, c.ps
    n = FIRST_SLOT["mix"]

    def turn(n, i=None):
        base = 0 if i is None else 1
        for m in range(2, 14):
            split_lo(c, dve, n + m, i, 12)
            if m in MIX_TAKES:
                x = MIX_TAKES[m]
                out = ps[:, 4 * (x % 2):4 * (x % 2) + 4, 0:SEQ]
                dve.wait_ge(S("slot_used"), at(n + m - 1, i, 12))
                if x < 2:
                    dve.tensor_tensor(t["gates"][x][:], out, wide(t["rs"][:, BOTH], 4), ALU.mult).then_inc(S("mix_taken"), 1)
                else:
                    dve.wait_ge(S("mix_gate"), at(2 * base + x - 1, i, 2))
                    dve.tensor_tensor(t["gates"][x - 2][:], out, t["gates"][x - 2][:], ALU.mult).then_inc(S("mix_taken"), 1)
        dve.wait_ge(S("mix_taken"), at(4 * base + 4, i, 4))
        ks = slice(0, 4) if i is None else bass.ds(at(4, i, 4), 4)
        dve.tensor_tensor(c.y[:, ks, 0:SEQ], t["gates"][0][:], t["gates"][1][:], ALU.add).then_inc(S("mixed"), 1)
        dve.wait_ge(S("mixed"), at(base + 1, i, 1))

    turn(n)
    with dve.Fori(0, 3) as i:
        turn(n + 12, i)
    n = FIRST_SLOT["mix_out"]
    for kg in range(4):
        ks = slice(4 * kg, 4 * kg + 4)
        dve.wait_ge(S("mix_hi"), kg + 1)
        dve.tensor_tensor(c.xa[1][:, ks, BOTH], c.y[:, ks, 0:SEQ], c.xa[0][:, ks, BOTH].bitcast(F32),
                          ALU.subtract).then_inc(S("mix_ready"), 1)
    dve.wait_ge(S("mix_ready"), 4)
    y_stage_split(c, lambda n: split_lo(c, dve, n), lambda chunk, n: y_take_dve(c, dve, chunk, n - 1, BOTH, 8, t), n)
    boundary_dve(c, dve, st, t, 3, 5, BOTH, "post_mix", "pre_ffn", FIRST_SLOT["ffn"])



def ffn_pe(c, t, pe):
    S = c.sem
    n = FIRST_SLOT["ffn"]
    t4 = lambda s: [(k, 4 * s + k) for k in range(4)]
    first_chunk_pe(c, pe, t, n, c.xa, 3, BOTH, 6, 4)
    for s in range(4):
        pause = (lambda: pe.wait_ge(S("root_done"), 7)) if s == 0 else None
        products(c, pe, n + 4 + s, c.xa, t4(s), banks(c, 1, SEQ), BOTH, s == 0, s == 3, pause=pause)

    def down(n, x, i=None):
        products(c, pe, n + x, c.xf, [(k, k) for k in range(4)], banks(c, x % 2, SEQ), slice(0, SEQ), True, True, i, 12)

    with pe.Fori(0, FF_STEPS - 1) as i:
        for x in range(2):
            if x == 0:
                pe.wait_ge(S("up_out_taken"), i * 2 + 1)
                pe.wait_ge(S("down_taken"), i * 4 + 1)
            else:
                pe.wait_ge(S("up_out_taken"), i * 2 + 2)
            for s in range(4):
                products(c, pe, n + 8 + 4 * x + s, c.xa, t4(s), banks(c, x, SEQ), BOTH, s == 0, s == 3, i, 12)
        pe.wait_ge(S("ff_ready"), i + 1)
        for x in range(4):
            if x < 2:
                pe.wait_ge(S("up_out_taken"), i * 2 + (3 + x))
            else:
                pe.wait_ge(S("down_taken"), i * 4 + x)
            down(n + 16, x, i)
    n += 8 + 12 * (FF_STEPS - 1)
    pe.wait_ge(S("ff_ready"), FF_STEPS)
    pe.wait_ge(S("down_taken"), 4 * (FF_STEPS - 1) + 1)
    pe.wait_ge(S("up_out_taken"), 2 * FF_STEPS)
    for x in range(4):
        if x >= 2:
            pe.wait_ge(S("y_taken"), 12 + x - 1)
        down(n, x)
    n = FIRST_SLOT["ple"]

    def ple(slot, j2, half):
        w_hi, w_lo = c.w_hi[(n + slot) % SPLIT], c.w_lo[(n + slot) % SPLIT]
        pe.wait_ge(S("lo_done"), n + slot + 1)
        for j in range(4):
            out, a = c.ps[:, 4 * half + j, 0:SEQ], slice(P * j, P * j + P)
            for k in range(2):
                pe.matmul(out, w_hi[:, 2 * k + j2, a], t["ple_hi"][:, k, :], start=k == 0, stop=False)
                pe.matmul(out, w_hi[:, 2 * k + j2, a], t["ple_lo"][:, k, :], start=False, stop=False)
                m = pe.matmul(out, w_lo[:, 2 * k + j2, a], t["ple_hi"][:, k, :], start=False, stop=k == 1)
        m.then_inc(S("slot_used" if j2 else "ple_done"), 1)

    pe.wait_ge(S("ple_ready"), 1)
    pe.wait_ge(S("y_taken"), 15)
    ple(0, 0, 0)
    pe.wait_ge(S("y_taken"), 16)
    ple(0, 1, 1)
    pe.wait_ge(S("e_taken"), 1)
    norm_between_pe(c, pe, t, 12, BOTH, 7)
    pe.wait_ge(S("e_taken"), 2)
    ple(1, 0, 1)
    pe.wait_ge(S("root_done"), 8)
    ple(1, 1, 0)
    n = FIRST_SLOT["ple_gate"]
    pe.wait_ge(S("e_taken"), 4)
    y_stage_pe(c, pe, n, c.xa, BOTH, 16, lambda s: pe.wait_ge(S("x_ready"), 17 + s))
    norm_between_pe(c, pe, t, 16, BOTH, 8)


def conv_param(c, tap, tile, i):
    first = PARAM["conv_b"] if tap == 3 else PARAM["conv_w"] + 88 * tap
    return c.params[:, bass.ds(at(first + tile, i, 4), 1)] if i is not None else c.params[:, first + tile:first + tile + 1]


def ffn_act(c, t, act):
    S = c.sem
    n = FIRST_SLOT["ffn"]

    def scaled(x, f, i):
        act.wait_ge(S("up_out_taken"), at(2 * f + x + 1, i, 2))
        if x == 0 and (f or i is not None):
            act.wait_ge(S("ff_f"), at(f, i, 1))
        for j in range(4):
            tile = 44 * x + 4 * f + j
            m = act.activation(t["conv"][x][:, j, :], t["up"][x][:, j, 2:], ACT.Identity,
                               bias=conv_param(c, 3, tile, i), scale=conv_param(c, 2, tile, i))
        m.then_inc(S("conv_scaled"), 1)

    def gelu(f, i):
        act.wait_ge(S("conv_done"), at(2 * f + 1, i, 2))
        act.activation(t["conv"][0][:], t["conv"][0][:], ACT.Gelu_apprx_tanh).then_inc(S("gelu_done"), 1)

    def hi(f, i):
        act.wait_ge(S("ff_f"), at(f + 1, i, 1))
        act.copy(c.xf[0][:], t["ff"][:]).then_inc(S("ff_hi"), 1)

    for m in range(4, 6):
        split_hi(c, act, n + m)
    root(c, act, 7, t["sd"], BOTH, S("stats_done"), 7, S("root_done"))
    scaled(0, 0, None)
    for m in range(6, 10):
        split_hi(c, act, n + m)
    gelu(0, None)
    scaled(1, 0, None)
    hi(0, None)
    act.wait_ge(S("ple_in"), 16)
    act.copy(t["ple_hi"][:], t["ple"][:]).then_inc(S("ple_hi"), 1)
    with act.Fori(0, FF_STEPS - 1) as i:
        for m in range(2, 14):
            split_hi(c, act, n + 8 + m, i, 12)
            if m == 5:
                scaled(0, 1, i)
            if m == 7:
                gelu(1, i)
            if m == 9:
                scaled(1, 1, i)
        hi(1, i)
    n += 8 + 12 * (FF_STEPS - 1)

    def squares(x, base):
        act.wait_ge(S("y_taken"), base + x + 1)
        act.activation((t["sq"] if x else t["acc"])[:, :, BOTH], c.y[:, 4 * x:4 * x + 4, BOTH], ACT.Square).then_inc(S("y_squared"), 1)

    for x in range(4):
        split_hi(c, act, n + 2 + x)
        squares(x, 12)
    n = FIRST_SLOT["ple"]

    def e_taken(x, half):
        act.wait_ge(S("slot_used" if x % 2 else "ple_done"), n + x // 2 + 1 if x % 2 else x // 2 + 1)
        act.copy(t["e"][:, 4 * x:4 * x + 4, :], c.ps[:, 4 * half:4 * half + 4, 0:SEQ]).then_inc(S("e_taken"), 1)

    e_taken(0, 0)
    e_taken(1, 1)
    root(c, act, 0, t["sd"], BOTH, S("stats_done"), 8, S("root_done"))
    e_taken(2, 1)
    split_hi(c, act, n + 2)
    e_taken(3, 0)
    split_hi(c, act, n + 3)
    n = FIRST_SLOT["ple_gate"]
    operands_act(c, act, 4, BOTH, None, n)
    for m in range(4, 18):
        if m < 16:
            split_hi(c, act, n + m)
        if m % 4 == 1:
            x = (m - 5) // 4
            act.wait_ge(S("slot_used"), n + m - 1)
            act.activation(c.y[:, 4 * x:4 * x + 4, BOTH], c.ps[:, 4 * (x % 2):4 * (x % 2) + 4, 0:SEQ],
                           ACT.Sigmoid).then_inc(S("ple_gated"), 1)
            squares(x, 16)
    root(c, act, 0, t["sd"], BOTH, S("stats_done"), 9, S("root_done"))


def ffn_pool(c, t, pool, st, a):
    S = c.sem
    squares_pool(c, pool, st, 3, BOTH, t["acc"], t["sq"])
    pool.wait_ge(S("h_ready"), 12)
    pool.memset(c.y[:], 0.0).then_inc(S("down_taken"), 1)
    for x in range(2):
        m = pool.memset(t["up"][x][:, :, 0:2], 0.0)
    m.then_inc(S("ffn_zeros"), 1)
    pool.dma_start(t["ple"][:], a["ple_in"]).then_inc(S("ple_in"), 16)


def ffn_dve(c, t, dve, st):
    S, ps = c.sem, c.ps
    n = FIRST_SLOT["ffn"]
    out = lambda x: ps[:, 4 * (x % 2):4 * (x % 2) + 4, 0:SEQ]

    def taken(x, f, i, done):
        dve.wait_ge(S("slot_used"), done)
        dve.tensor_tensor(t["up"][x][:, :, 2:], out(x), wide(t["rs"][:, BOTH], 4), ALU.mult).then_inc(S("up_out_taken"), 1)

    def conv(x, f, i):
        dve.wait_ge(S("conv_scaled"), at(2 * f + x + 1, i, 2))
        for tap in (1, 0):
            for j in range(4):
                m = dve.scalar_tensor_tensor(out=t["conv"][x][:, j, :], in0=t["up"][x][:, j, tap:tap + SEQ],
                                             scalar=conv_param(c, tap, 44 * x + 4 * f + j, i),
                                             in1=t["conv"][x][:, j, :], op0=ALU.mult, op1=ALU.add)
            if tap:
                st.did(m)
        m.then_inc(S("conv_done"), 1)
        dve.wait_ge(S("conv_done"), at(2 * f + x + 1, i, 2))

    def product(f, i):
        dve.wait_ge(S("gelu_done"), at(f + 1, i, 1))
        dve.tensor_tensor(t["ff"][:], t["conv"][0][:], t["conv"][1][:], ALU.mult).then_inc(S("ff_f"), 1)

    def lo(f, i):
        dve.wait_ge(S("ff_hi"), at(f + 1, i, 1))
        dve.tensor_tensor(c.xf[1][:], t["ff"][:], c.xf[0][:].bitcast(F32), ALU.subtract).then_inc(S("ff_ready"), 1)
        dve.wait_ge(S("ff_ready"), at(f + 1, i, 1))

    for m in range(4, 6):
        split_lo(c, dve, n + m)
    pre_root_dve(c, dve, st, t, 6, BOTH)
    dve.wait_ge(S("ffn_zeros"), 1)
    taken(0, 0, None, n + 4)
    split_lo(c, dve, n + 6)
    conv(0, 0, None)
    for m in range(7, 10):
        split_lo(c, dve, n + m)
    taken(1, 0, None, n + 8)
    conv(1, 0, None)
    product(0, None)
    lo(0, None)
    dve.wait_ge(S("ple_hi"), 1)
    dve.tensor_tensor(t["ple_lo"][:], t["ple"][:], t["ple_hi"][:].bitcast(F32), ALU.subtract).then_inc(S("ple_ready"), 1)
    with dve.Fori(0, FF_STEPS - 1) as i:
        st.enter(i, 2)
        base = n + 8
        for m in range(2, 14):
            split_lo(c, dve, base + m, i, 12)
            if m == 5:
                taken(0, 1, i, at(base + 4, i, 12))
            if m == 6:
                conv(0, 1, i)
            if m == 9:
                taken(1, 1, i, at(base + 8, i, 12))
            if m >= 10:
                x = m - 10
                dve.wait_ge(S("slot_used"), at(base + 9 + x, i, 12))
                y = c.y[:, 4 * x:4 * x + 4, BOTH]
                dve.tensor_tensor(y, y, out(x), ALU.add).then_inc(S("down_taken"), 1)
                dve.wait_ge(S("down_taken"), at(x + 2, i, 4))
            if m == 10:
                conv(1, 1, i)
            if m == 11:
                product(1, i)
        lo(1, i)
    st.leave(FF_STEPS - 1)
    n += 8 + 12 * (FF_STEPS - 1)

    def squares(x, base):
        dve.wait_ge(S("y_squared"), base + x + 1)
        if x:
            dve.tensor_tensor(t["acc"][:, :, BOTH], t["acc"][:, :, BOTH], t["sq"][:, :, BOTH], ALU.add).then_inc(S("y_added"), 1)
            dve.wait_ge(S("y_added"), base // 4 * 3 + x)

    for x in range(4):
        split_lo(c, dve, n + 2 + x)
        dve.wait_ge(S("slot_used"), n + x + 1)
        y = c.y[:, 4 * x:4 * x + 4, BOTH]
        dve.tensor_tensor(y, y, out(x), ALU.add).then_inc(S("y_taken"), 1)
        squares(x, 12)
    n = FIRST_SLOT["ple"]
    dve.wait_ge(S("root_done"), 8)
    st.did(dve.reciprocal(t["rs"][:, BOTH], t["sd"][:, BOTH]))
    split_lo(c, dve, n + 2)
    split_lo(c, dve, n + 3)
    n = FIRST_SLOT["ple_gate"]
    operands_dve(c, dve, st, 4, BOTH, t, "post_ffn", None, n)
    for m in range(4, 18):
        if m < 16:
            split_lo(c, dve, n + m)
        if m % 4 == 1:
            x = (m - 5) // 4
            y = c.y[:, 4 * x:4 * x + 4, BOTH]
            dve.wait_ge(S("ple_gated"), x + 1)
            dve.wait_ge(S("e_taken"), 4)
            dve.tensor_tensor(y, y, t["e"][:, 4 * x:4 * x + 4, :], ALU.mult).then_inc(S("y_taken"), 1)
            squares(x, 16)
    dve.wait_ge(S("root_done"), 9)
    st.did(dve.reciprocal(t["rs"][:, BOTH], t["sd"][:, BOTH]))
    for kg in range(4):
        ks = slice(4 * kg, 4 * kg + 4)
        st.did(dve.tensor_tensor(t["tmp"][:, :, BOTH], c.y[:, ks, BOTH], wide(t["rs"][:, BOTH], 4), ALU.mult))
        for j in range(4):
            k = 4 * kg + j
            m = dve.scalar_tensor_tensor(out=c.h[:, k, BOTH], in0=t["tmp"][:, j, BOTH], scalar=c.param("ple_norm", k),
                                         in1=c.h[:, k, BOTH], op0=ALU.mult, op1=ALU.add)
        m.then_inc(S("out_ready"), 1)
        dve.wait_ge(S("out_ready"), kg + 1)


def store_out(c, sp, out):
    for kg in range(4):
        ks = slice(4 * kg, 4 * kg + 4)
        sp.wait_ge(c.sem("out_ready"), kg + 1)
        sp.dma_start(out[:, ks, :], c.h[:, ks, BOTH]).then_inc(c.sem("out_written"), 16)
    sp.wait_ge(c.sem("out_written"), 64)


def program(nc, a):
    with ExitStack() as ctx:
        c = Chip(nc, ctx)
        c.eps = {"eps": c.small[:, 0:1], "rw": c.small[:, 1:2]}
        t = {}

        def place(scope, names):
            return {n: c.sb(scope, n, shape, *rest) for n, shape, *rest in names}

        with ExitStack() as first:
            c.xb = [c.sb(first, f"xb_{x}", [P, KT, ROWS], F32R) for x in ("hi", "lo")]
            consts = c.sb(first, "consts_first", [P, columns(CONSTS_FIRST)[1]])
            with ExitStack() as scope:
                t["attn"] = place(scope, [
                    ("qk", [P, 4, ROWS]), ("rot", [P, 2, ROWS]), ("p", [P, 2, 3, ROWS]), ("a", [P, 3 * 3 * P]),
                    ("at", [P, 3, ROWS]), ("vt", [P, 2, 3 * P]), ("vn", [P, 3, HEAD_V]), ("o", [P, 2, ROWS]),
                    ("osq", [P, 2, ROWS]), ("rs", [P, ROWS]), ("ro", [P, ROWS]), ("so", [P, ROWS]), ("st", [P, 24]),
                    ("lam", [P, 8]), ("gain", [P, 2])])
                t["attn"]["sd"] = t["attn"]["so"]
                t["attn"]["first"] = consts
                flat = t["attn"]["p"][:].rearrange("p a b r -> p (a b r)")
                t["attn"]["acc"] = flat[:, 0:4 * ROWS].rearrange("p (k r) -> p k r", k=4)
                t["attn"]["sq"] = t["attn"]["a"][:, 0:4 * ROWS].rearrange("p (k r) -> p k r", k=4)
            with ExitStack() as scope:
                t["mid"] = place(scope, [
                    ("acc", [P, 4, ROWS]), ("sq", [P, 4, ROWS]), ("tmp", [P, 4, ROWS]),
                    ("u0", [P, 4, ROWS]), ("u1", [P, 4, ROWS]), ("sums0", [P, 4, ROWS]), ("sums1", [P, 4, ROWS]),
                    ("rs_mid", [P, ROWS]), ("sd_mid", [P, ROWS])])
                m = t["mid"]
                m["u"], m["sums"] = [m["u0"], m["u1"]], [m["sums0"], m["sums1"]]
                m["rs"], m["sd"], m["first"], m["mixed"] = m["rs_mid"], m["sd_mid"], consts, m["sq"]

        with ExitStack() as second:
            lasting = place(second, [("kpe", [P, SEQ]), ("cos2", [P, SEQ]), ("sin2", [P, SEQ]), ("rs_2", [P, ROWS]), ("sd_2", [P, ROWS])])
            lasting["rs"], lasting["sd"] = lasting["rs_2"], lasting["sd_2"]
            spare = c.y[:].rearrange("p k r -> p (k r)")[:, 8 * ROWS:]
            tiles = lambda x: x.rearrange("p (j r) -> p j r", j=4)
            units = lambda x: x.rearrange("p (u i) -> p u i", i=RW_N)
            with ExitStack() as scope:
                m = t["rw"] = place(scope, [
                    ("masks", [P, columns(CONSTS_RW)[1]]), ("lora_hi", [P, 3, SEQ], F32R), ("lora_lo", [P, 3, SEQ], F32R),
                    ("ar_flat", [P, 4 * 4 * 2 * RW_N]), ("pb", [P, 8, RW_N]), ("sa", [P, 8, RW_N]), ("state", [P, 4, RW_N]),
                    ("ends", [P, 4, 4])] + [(f"rw_tile{n}", [P, 4 * SEQ]) for n in range(11)])
                m.update(lasting)
                m["ar"] = m["ar_flat"].rearrange("p (j x s) -> p j x s", j=4, x=CHUNKS)
                m["lora"] = m["ar_flat"][:, 0:3 * SEQ].rearrange("p (j r) -> p j r", j=3)
                m["positions"] = m["ar_flat"][:, 4 * SEQ:5 * SEQ].bitcast(I32)
                flat = [m[f"rw_tile{n}"][:] for n in range(11)]
                for n, name in enumerate(("bt", "kt", "v", "bon", "g", "r", "k", "a", "w", "cs", "kk")):
                    m[name] = tiles(flat[n])
                for n, name in enumerate(("la", "mr", "mk", "ll", "xx", "yy")):
                    m[name] = units(flat[5 + n])
                m["nb"], m["nk"], m["nv"] = m["ll"], m["xx"], units(spare[:, 0:4 * SEQ])
                m["yt"], m["sq"] = m["bt"], m["kt"]
                m["tt"], m["tt4"] = units(spare[:, 0:4 * SEQ]), tiles(spare[:, 0:4 * SEQ])
                m["lm"] = units(spare[:, 4 * SEQ:8 * SEQ])
                m["zp"] = tiles(spare[:, 4 * SEQ:8 * SEQ + 4])
                m["acc"] = t["mid"]["acc"]
            late = place(second, [(f"late_{n}", [P, 4, ROWS]) for n in ("acc", "sq", "tmp")])
            late = {n: late[f"late_{n}"] for n in ("acc", "sq", "tmp")}
            with ExitStack() as scope:
                xb_second = [c.sb(scope, f"xb2_{x}", [P, KT, ROWS], F32R) for x in ("hi", "lo")]
                with ExitStack() as inner:
                    m = t["mla"] = place(inner, [
                        ("low_flat", [P, 8 * SEQ]), ("pm", [P, 2, 2, SEQ]), ("at2", [P, 2, 3 * P]), ("low_rs", [P, 2, SEQ]),
                        ("ms", [P, 2, 8])])
                    m.update(lasting)
                    m["low"] = m["low_flat"].rearrange("p (j r) -> p j r", j=8)
                    m["vn2"] = m["low_flat"].rearrange("p (b n) -> p b n", b=2)
                    m["sq4"] = m["vt4"] = late["acc"][:, :, 0:SEQ]
                    m["qp"] = late["tmp"][:, :, 0:SEQ]
                    m["qn"], m["kn"] = c.y[:, 0:8, 0:SEQ], c.y[:, 8:16, 0:SEQ]
                with ExitStack() as inner:
                    m = t["mix"] = place(inner, [("gate_rw", [P, 4, SEQ]), ("gate_mla", [P, 4, SEQ])])
                    m.update(lasting | late)
                    m["gates"] = [m["gate_rw"], m["gate_mla"]]
            m = t["ffn"] = place(second, [
                ("up_gate", [P, 4, SEQ + 2]), ("up_value", [P, 4, SEQ + 2]), ("conv_gate", [P, 4, SEQ]), ("conv_value", [P, 4, SEQ]),
                ("ff", [P, 4, SEQ]), ("ff_hi", [P, 4, SEQ], F32R), ("ff_lo", [P, 4, SEQ], F32R), ("ple", [P, 2, SEQ]),
                ("ple_hi", [P, 2, SEQ], F32R), ("ple_lo", [P, 2, SEQ], F32R), ("e", [P, KT, SEQ])])
            m.update(lasting | late)
            m["up"], m["conv"] = [m["up_gate"], m["up_value"]], [m["conv_gate"], m["conv_value"]]
            c.xf = [m["ff_hi"], m["ff_lo"]]
        xb_first = c.xb

        S = c.sem
        block = ctx.enter_context(nc.Block())

        @block.sync
        def _(sp):
            attn_load(c, t["attn"], sp, a)
            load_weights(c, sp, a["weights"])
            store_out(c, sp, a["out"])

        @block.tensor
        def _(pe):
            c.xb = xb_first
            attn_pe(c, t["attn"], pe)
            mid_pe(c, t["mid"], pe)
            c.xb = xb_second
            rw_pe(c, t["rw"], pe)
            mla_pe(c, t["mla"], pe)
            mix_pe(c, t["mix"], pe)
            ffn_pe(c, t["ffn"], pe)

        @block.scalar
        def _(act):
            act.wait_ge(S("eps_ready"), 2)
            c.xb = xb_first
            attn_act(c, t["attn"], act)
            mid_act(c, t["mid"], act)
            c.xb = xb_second
            rw_act(c, t["rw"], act)
            mla_act(c, t["mla"], act)
            mix_act(c, t["mix"], act)
            ffn_act(c, t["ffn"], act)

        @block.vector
        def _(dve):
            st = Steps(dve, S("dve_step"))
            c.xb = xb_first
            attn_dve(c, t["attn"], dve, st)
            mid_dve(c, t["mid"], dve, st)
            c.xb = xb_second
            rw_dve(c, t["rw"], dve, st)
            mla_dve(c, t["mla"], dve, st)
            mix_dve(c, t["mix"], dve, st)
            ffn_dve(c, t["ffn"], dve, st)

        @block.gpsimd
        def _(pool):
            st = Steps(pool, S("pool_step"))
            attn_pool(c, t["attn"], pool, st)
            mid_pool(c, t["mid"], pool, st)
            rw_pool(c, t["rw"], pool, st, a)
            mla_pool(c, t["mla"], pool, st)
            ffn_pool(c, t["ffn"], pool, st, a)



def channels(v):
    return np.ascontiguousarray(v.reshape(-1, P).T)


def slots(w, cols=SLOT_N):
    k, n = w.shape
    s = w.reshape(k // (SLOT_K * P), SLOT_K, P, n // cols, cols).transpose(3, 0, 2, 1, 4)
    return np.ascontiguousarray(s).reshape(-1, P, SLOT_K, cols)


def pack_weights(x):
    out = np.zeros((N_SLOTS, P, SLOT_K, SLOT_N), np.float32)

    def put(name, parts):
        n = FIRST_SLOT[name]
        for part in parts:
            out[n:n + len(part)] = part
            n += len(part)
        return n

    w = x["attn_w_in"][0].reshape(D, 4, HEADS, HEAD_V)
    put("attn_in", [slots(np.concatenate([w[:, a, h], w[:, a + 1, h]], 1)) for h in range(HEADS) for a in (0, 2)])
    put("attn_out", [slots(x["attn_w_out"][0])])
    put("pool_in", [slots(x["pool_w_in"][0])])
    put("pool_group", [slots(x["pool_w_group"][0, g]) for g in range(4)])
    put("pool_out", [slots(x["pool_w_out"][0])])
    w = x["w_in_2"][0]
    rw, mla, gate = w[:, :3360], w[:, 3360:4448], w[:, 4448:]
    pe = np.concatenate([np.arange(0, 16), np.arange(32, 48), np.arange(16, 32), np.arange(48, 64)])
    down = np.zeros((D, SLOT_N), np.float32)
    down[:, 0:288] = rw[:, 3072:]
    k_pe = mla[:, 1024:][:, pe]
    down[:, 384:448], down[:, 448:512] = k_pe, k_pe
    put("rw_down", [slots(down)])
    for b in range(2):
        n = FIRST_SLOT[f"rw_half{b}"]
        s = slice(512 * b, 512 * b + 512)
        for r, first in ((1, n), (0, n + 5), (2, n + 9)):
            out[first:first + 4] = slots(rw[:, RW_WIDTH * r:][:, s])
        n += 4
        out[n, 0:64, 0], out[n, 64:128, 0] = x["rw_w2_2"][0][:, s], x["rw_a2_2"][0][:, s]
        out[n, :, 1], out[n, 0:32, 2] = x["rw_g2_2"][0][0:128, s], x["rw_g2_2"][0][128:160, s]
    put("mla_in", [slots(mla[:, 0:1024])])
    q = x["mla_w_q_up_2"][0].reshape(512, MLA_HEADS, 192)
    put("mla_q", [slots(np.concatenate([q[:, :, 0:128].reshape(512, -1), q[:, :, 128:][:, :, pe].reshape(512, -1)], 1))])
    kv = x["mla_w_kv_up_2"][0].reshape(512, MLA_HEADS, 256)
    put("mla_kv", [slots(np.concatenate([kv[:, :, 0:128].reshape(512, -1), kv[:, :, 128:].reshape(512, -1)], 1))])
    branch = np.concatenate([x["w_branch_rw_2"][0], x["w_branch_mla_2"][0]], 0)
    put("mix", [slots(m[:, 512 * n:512 * n + 512]) for n in range(4) for m in (gate[:, 0:D], gate[:, D:], branch)])
    put("mix_out", [slots(x["w_out_2"][0])])
    up, down = x["w_up_2"][0], x["w_down_2"][0]
    n = FIRST_SLOT["ffn"]
    for f in range(FF_STEPS + 1):
        if f < FF_STEPS:
            out[n:n + 4] = slots(up[:, 512 * f:512 * f + 512])
            out[n + 4:n + 8] = slots(up[:, D_FF + 512 * f:D_FF + 512 * f + 512])
            n += 8
        if f:
            out[n:n + 4] = slots(down[512 * (f - 1):512 * f])
            n += 4
    e = x["w_ple_2"][0].reshape(2, P, 2, 2, SLOT_N)
    out[FIRST_SLOT["ple"]:FIRST_SLOT["ple"] + 2] = e.transpose(2, 1, 0, 3, 4).reshape(2, P, 4, SLOT_N)
    put("ple_gate", [slots(x["w_ple_gate_2"][0])])
    return out


def pack_params(x):
    out = np.zeros((P, N_PARAMS), np.float32)

    def put(name, v, k=0):
        out[:, PARAM[name] + k:PARAM[name] + k + v.shape[1]] = v

    for n in range(2):
        put(f"pre{n}", channels(x["pre_norm_g"][n]))
        put(f"post{n}", channels(x["post_norm_g"][n]))
    put("subln", channels(x["attn_subln_g"][0]))
    for n, v in enumerate(("attn_lambda_q1", "attn_lambda_k1", "attn_lambda_q2", "attn_lambda_k2")):
        put("lam", x[v][0][:, None], n)
    put("pool_scale", channels(x["pool_scale"][0]))
    put("pre_mix", channels(x["pre_mix_norm_2"][0]))
    mu = x["rw_mu_2"][0]
    put("mu_rkv", channels(mu[0:3072]))
    put("mu_lora", channels(np.concatenate([mu[3072:], np.zeros(96, np.float32)])))
    for name, of in (("w0", "rw_w0_2"), ("a0", "rw_a0_2"), ("k_k", "rw_k_k_2"), ("k_a", "rw_k_a_2"), ("lnx_w", "rw_lnx_w_2"),
                     ("lnx_b", "rw_lnx_b_2"), ("r_k", "rw_r_k_2"), ("q_norm", "mla_q_norm_2"), ("kv_norm", "mla_kv_norm_2"),
                     ("post_mix", "post_mix_norm_2"), ("pre_ffn", "pre_ffn_norm_2"), ("conv_b", "conv_b_2"),
                     ("post_ffn", "post_ffn_norm_2"), ("ple_norm", "ple_norm_2")):
        put(name, channels(x[of][0]))
    for n in range(3):
        put("conv_w", channels(x["conv_w_2"][0, n]), 88 * n)
    p = np.arange(P)
    put("inv_freq", (np.float32(10000.0) ** (-(2 * ((p % 16) + 16 * (p // 32 % 2))).astype(np.float32) / np.float32(64)))[:, None])
    put("rope_sign", np.where(p % 32 < 16, -1.0, 1.0)[:, None])
    return out


def kernel(**inputs):
    import concourse.bacc as bacc
    from concourse.bass_utils import run_bass_kernel_spmd

    x = {n: np.asarray(v) for n, v in inputs.items()}
    base, first, rw = stage_consts()
    rows = np.concatenate([x["meta_tokens"], x["x"][0]], 0)
    arrays = {
        "weights": pack_weights(x), "params": pack_params(x), "consts": base, "consts_first": first, "consts_rw": rw,
        "h0": np.ascontiguousarray(rows.reshape(ROWS, KT, P).transpose(2, 1, 0)),
        "ple_in": np.ascontiguousarray(x["p_2"][0, 0].reshape(SEQ, 2, P).transpose(2, 1, 0)),
        "positions": np.ascontiguousarray(x["positions_2"]),
    }
    nc = bacc.Bacc("TRN2", target_bir_lowering=False, num_devices=1)
    a = {n: nc.dram_tensor(n, v.shape, mybir.dt.from_np(v.dtype), kind="ExternalInput").ap() for n, v in arrays.items()}
    a["out"] = nc.dram_tensor("out", (P, KT, SEQ), F32, kind="ExternalOutput").ap()
    program(nc, a)
    r = run_bass_kernel_spmd(nc, [arrays], core_ids=[0])
    out = r.results[0]["out"]
    return np.ascontiguousarray(out.transpose(2, 1, 0)).reshape(1, SEQ, D)
```

```python
from contextlib import ExitStack
import math

import numpy as np

import concourse.bass as bass
from concourse import mybir

F32 = mybir.dt.float32
F32R = mybir.dt.float32r
I32 = mybir.dt.int32
ALU = mybir.AluOpType
ACT = mybir.ActivationFunctionType
AX = mybir.AxisListType

P = 128
D = 2048
META = 16
SEQ = 256
ROWS = META + SEQ
KT = D // P
SLOT_K = 4
SLOT_N = 512
RAW = 4
SPLIT = 2
BOTH = slice(META, ROWS)
HEADS = 8
HEAD_V = 256
LAM_INIT = 0.8 - 0.6 * math.exp(-0.3 * 0)
EPS = 1e-6
POOL_WINDOWS = (2, 4, 8, 16)
RW_WIDTH = 1024
RW_N = 64
RW_EPS = 64e-5
D_FF = 5632
FF_STEPS = D_FF // SLOT_N
MLA_HEADS = 8
MLA_SCALE = 192 ** -0.5

SLOTS_OF = [
    ("attn_in", HEADS * 8), ("attn_out", 16), ("pool_in", 32), ("pool_group", 4), ("pool_out", 16),
    ("rw_down", 4), ("rw_half0", 14), ("rw_half1", 14), ("mla_in", 8), ("mla_q", 3), ("mla_kv", 4),
    ("mix", 48), ("mix_out", 16), ("ffn", FF_STEPS * 12), ("ple", 2), ("ple_gate", 16),
]
FIRST_SLOT, N_SLOTS = {}, 0
for _name, _count in SLOTS_OF:
    FIRST_SLOT[_name] = N_SLOTS
    N_SLOTS += _count

PARAMS_OF = [
    ("pre0", 16), ("pre1", 16), ("post0", 16), ("post1", 16), ("subln", 2), ("lam", 4), ("pool_scale", 16),
    ("pre_mix", 16), ("mu_rkv", 24), ("mu_lora", 3), ("w0", 8), ("a0", 8), ("k_k", 8), ("k_a", 8), ("r_k", 8),
    ("lnx_w", 8), ("lnx_b", 8), ("q_norm", 4), ("kv_norm", 4), ("post_mix", 16), ("pre_ffn", 16),
    ("conv_w", 3 * 88), ("conv_b", 88), ("post_ffn", 16), ("ple_norm", 16), ("inv_freq", 1), ("rope_sign", 1),
]
PARAM, N_PARAMS = {}, 0
for _name, _count in PARAMS_OF:
    PARAM[_name] = N_PARAMS
    N_PARAMS += _count

CONSTS_OF = [("ident", 128), ("ones", 128), ("head_ones", 128)]
CONSTS_FIRST = [("rope_cos", ROWS), ("rope_sin", ROWS), ("inv_count", 4 * 16)]
CONSTS_RW = [("before", 64), ("upto", 64), ("after", 64), ("eye", 64), ("level0_t", 64)] + [
    (f"level{n}", 64) for n in range(6)]


def columns(table):
    at, n = {}, 0
    for name, count in table:
        at[name] = (n, n + count)
        n += count
    return at, n


def stage_consts():
    def fill(table, parts):
        at, n = columns(table)
        out = np.zeros((P, n), np.float32)
        for name, (a, b) in at.items():
            out[:, a:b] = parts[name]
        return out
    p = np.arange(P)
    head = (p[:, None] // 64 == p[None, :] // 64).astype(np.float32)
    base = fill(CONSTS_OF, {"ident": np.eye(P), "ones": np.ones((P, P)), "head_ones": head})
    inv = np.float32(500000.0) ** (-np.arange(0, 32, 2, dtype=np.float32) / np.float32(32))
    ang = (np.arange(ROWS, dtype=np.float32)[:, None] * inv[None, :]).astype(np.float32)
    ang = ang[:, p % 16].T
    sign = np.where(p % 32 < 16, -1.0, 1.0)[:, None]
    t = np.arange(16)
    counts = np.concatenate([1.0 / np.minimum(t + 1, w) for w in POOL_WINDOWS])
    first = fill(CONSTS_FIRST, {"rope_cos": np.cos(ang), "rope_sin": np.sin(ang) * sign, "inv_count": counts[None]})
    i, t = (p % 64)[:, None], np.arange(64)[None, :]
    parts = {"before": i < t, "upto": i <= t, "after": i > t, "eye": i == t}
    for n in range(6):
        b = 2 ** n
        parts[f"level{n}"] = (i // (2 * b) == t // (2 * b)) & (i // b % 2 == 1) & (t // b % 2 == 0)
    parts["level0_t"] = (t // 2 == i // 2) & (t % 2 == 1) & (i % 2 == 0)
    return base, first, fill(CONSTS_RW, parts)


def at(value, i, step):
    return value if i is None else i * step + value


class Steps:

    def __init__(self, engine, sem):
        self.engine, self.sem, self.n, self.turn, self.per = engine, sem, 0, None, 0

    def did(self, instruction):
        instruction.then_inc(self.sem, 1)
        self.n += 1
        self.settle()

    def settle(self):
        self.engine.wait_ge(self.sem, at(self.n, self.turn, self.per))

    def enter(self, turn, per):
        self.turn, self.per, self.start = turn, per, self.n

    def leave(self, turns):
        assert self.n - self.start == self.per, f"a turn has {self.n - self.start} steps"
        self.n = self.start + self.per * turns
        self.turn = None


class Chip:

    def __init__(self, nc, ctx):
        self.nc, self.ctx, self.names = nc, ctx, {}
        self.raw = [self.sb(ctx, f"raw_weights{i}", [P, SLOT_K, SLOT_N]) for i in range(RAW)]
        self.w_hi = [self.sb(ctx, f"weights_hi{i}", [P, SLOT_K, SLOT_N], F32R) for i in range(SPLIT)]
        self.w_lo = [self.sb(ctx, f"weights_lo{i}", [P, SLOT_K, SLOT_N], F32R) for i in range(SPLIT)]
        self.xa = [self.sb(ctx, f"xa_{x}", [P, KT, ROWS], F32R) for x in ("hi", "lo")]
        self.h = self.sb(ctx, "h", [P, KT, ROWS])
        self.y = self.sb(ctx, "y", [P, KT, ROWS])
        self.params = self.sb(ctx, "params", [P, N_PARAMS])
        self.consts = self.sb(ctx, "consts", [P, columns(CONSTS_OF)[1]])
        self.small = self.sb(ctx, "small", [P, 64])
        self.ps = ctx.enter_context(nc.psum_tensor("banks", [P, 8, 512], F32))
        self.raw_full = [self.sem(f"raw_full{i}") for i in range(RAW)]

    def sb(self, ctx, name, shape, dt=F32):
        return ctx.enter_context(self.nc.sbuf_tensor(name + "_sb", shape, dt))

    def sem(self, name):
        if name not in self.names:
            self.names[name] = self.ctx.enter_context(self.nc.semaphore(name))
        return self.names[name]

    def const(self, name):
        a, b = columns(CONSTS_OF)[0][name]
        return self.consts[:, a:b]

    def param(self, name, k, rows=P):
        return self.params[0:rows, PARAM[name] + k:PARAM[name] + k + 1]


def wide(table, n):
    return table.unsqueeze(1).to_broadcast([P, n, table.shape[1]])


def split_hi(c, act, n, i=None, step=0):
    act.wait_ge(c.raw_full[n % RAW], at(16 * (n // RAW + 1), i, 16 * (step // RAW)))
    if n >= SPLIT:
        act.wait_ge(c.sem("slot_used"), at(n - SPLIT + 1, i, step))
    act.copy(c.w_hi[n % SPLIT][:], c.raw[n % RAW][:]).then_inc(c.sem("hi_done"), 1)


def split_lo(c, dve, n, i=None, step=0):
    dve.wait_ge(c.sem("hi_done"), at(n + 1, i, step))
    dve.tensor_tensor(c.w_lo[n % SPLIT][:], c.raw[n % RAW][:], c.w_hi[n % SPLIT][:].bitcast(F32),
                      ALU.subtract).then_inc(c.sem("lo_done"), 1)


def products(c, pe, n, x, tiles, outs, cols, first, last, i=None, step=0, used=True, pause=None):
    pe.wait_ge(c.sem("lo_done"), at(n + 1, i, step))
    w_hi, w_lo = c.w_hi[n % SPLIT], c.w_lo[n % SPLIT]
    x_hi, x_lo = x
    for j, out in outs:
        if pause and j == 3:
            pause()
        for k, tile in tiles:
            a = slice(j * P, j * P + P)
            begin, end = first and k == tiles[0][0], last and k == tiles[-1][0]
            pe.matmul(out, w_hi[:, k, a], x_hi[:, tile, cols], start=begin, stop=False)
            pe.matmul(out, w_hi[:, k, a], x_lo[:, tile, cols], start=False, stop=False)
            done = pe.matmul(out, w_lo[:, k, a], x_hi[:, tile, cols], start=False, stop=end)
    if used:
        done.then_inc(c.sem("slot_used"), 1)
    return done


def banks(c, half, length):
    return [(j, c.ps[:, 4 * half + j, 0:length]) for j in range(4)]


def load_weights(c, sp, wall):
    for n in range(RAW):
        sp.dma_start(c.raw[n][:], wall[n]).then_inc(c.raw_full[n], 16)
    turns = (N_SLOTS - RAW) // RAW
    with sp.Fori(0, turns) as i:
        for s in range(RAW):
            sp.wait_ge(c.sem("lo_done"), i * RAW + s + 1)
            sp.dma_start(c.raw[s][:], wall[i * RAW + (s + RAW)]).then_inc(c.raw_full[s], 16)
    for n in range(RAW + turns * RAW, N_SLOTS):
        sp.wait_ge(c.sem("lo_done"), n - RAW + 1)
        sp.dma_start(c.raw[n % RAW][:], wall[n]).then_inc(c.raw_full[n % RAW], 16)



def sum_squares(c, pe, acc, bank, cols, ready, value, done):
    pe.wait_ge(ready, value)
    n = cols.stop - cols.start
    for j in range(4):
        m = pe.matmul(c.ps[:, bank, 0:n], c.const("ones"), acc[:, j, cols], start=j == 0, stop=j == 3)
    m.then_inc(done, 1)


def root(c, act, bank, out, cols, ready, value, done, width=D, eps="eps"):
    act.wait_ge(ready, value)
    act.activation(out[:, cols], c.ps[:, bank, 0:cols.stop - cols.start], ACT.Sqrt,
                   bias=c.eps[eps], scale=1.0 / width).then_inc(done, 1)


def operands_dve(c, dve, st, b, cols, t, g_post, g_pre, n):
    for kg in range(4):
        ks = slice(4 * kg, 4 * kg + 4)
        if g_post is not None:
            st.did(dve.tensor_tensor(t["tmp"][:, :, cols], c.y[:, ks, cols], wide(t["rs"][:, cols], 4), ALU.mult))
            for j in range(4):
                k = 4 * kg + j
                m = dve.scalar_tensor_tensor(out=c.h[:, k, cols], in0=t["tmp"][:, j, cols], scalar=c.param(g_post, k),
                                             in1=c.h[:, k, cols], op0=ALU.mult, op1=ALU.add)
                m.then_inc(c.sem("h_ready"), 1)
            dve.wait_ge(c.sem("h_ready"), KT * (b - 1) + 4 * kg + 4)
        for j in range(4):
            k = 4 * kg + j
            dve.wait_ge(c.sem("x_hi_ready"), KT * b + k + 1)
            if g_pre is None:
                m = dve.tensor_tensor(c.xa[1][:, k, cols], c.h[:, k, cols], c.xa[0][:, k, cols].bitcast(F32), ALU.subtract)
            else:
                m = dve.scalar_tensor_tensor(out=c.xa[1][:, k, cols], in0=c.h[:, k, cols], scalar=c.param(g_pre, k),
                                             in1=c.xa[0][:, k, cols].bitcast(F32), op0=ALU.mult, op1=ALU.subtract)
        m.then_inc(c.sem("x_ready"), 1)
        if kg >= 2 and n + kg < N_SLOTS:
            split_lo(c, dve, n + kg)


def operands_act(c, act, b, cols, g_pre, n):
    for kg in range(4):
        for j in range(4):
            k = 4 * kg + j
            if b:
                act.wait_ge(c.sem("h_ready"), KT * (b - 1) + k + 1)
            if g_pre is None:
                m = act.copy(c.xa[0][:, k, cols], c.h[:, k, cols])
            else:
                m = act.activation(c.xa[0][:, k, cols], c.h[:, k, cols], ACT.Copy, scale=c.param(g_pre, k))
            m.then_inc(c.sem("x_hi_ready"), 1)
        if kg >= 2 and n + kg < N_SLOTS:
            split_hi(c, act, n + kg)


def squares_pool(c, pool, st, b, cols, acc, sq):
    for kg in range(4):
        if b:
            pool.wait_ge(c.sem("h_ready"), KT * (b - 1) + 4 * kg + 4)
        hk = c.h[:, 4 * kg:4 * kg + 4, cols]
        st.did(pool.tensor_tensor((sq if kg else acc)[:, :, cols], hk, hk, ALU.mult))
        if 0 < kg < 3:
            st.did(pool.tensor_tensor(acc[:, :, cols], acc[:, :, cols], sq[:, :, cols], ALU.add))
        if kg == 3:
            pool.tensor_tensor(acc[:, :, cols], acc[:, :, cols], sq[:, :, cols], ALU.add).then_inc(c.sem("squares_ready"), 1)



def y_stage_pe(c, pe, n0, x, cols, base, wait_x=None, begun=0):
    for chunk in range(4):
        if chunk >= 2:
            pe.wait_ge(c.sem("y_taken"), base + chunk - 1)
        for s in range(0 if chunk else begun, 4):
            if chunk == 0 and wait_x:
                wait_x(s)
            products(c, pe, n0 + 4 * chunk + s, x, [(k, 4 * s + k) for k in range(4)],
                     banks(c, chunk % 2, cols.stop - cols.start), cols, s == 0, s == 3)


def y_take_act(c, act, chunk, cols, base, t):
    act.wait_ge(c.sem("y_taken"), base + chunk + 1)
    act.activation((t["sq"] if chunk else t["acc"])[:, :, cols], c.y[:, 4 * chunk:4 * chunk + 4, cols],
                   ACT.Square).then_inc(c.sem("y_squared"), 1)


def y_take_dve(c, dve, chunk, done, cols, base, t):
    n = cols.stop - cols.start
    dve.wait_ge(c.sem("slot_used"), done)
    dve.tensor_copy(c.y[:, 4 * chunk:4 * chunk + 4, cols],
                    c.ps[:, 4 * (chunk % 2):4 * (chunk % 2) + 4, 0:n]).then_inc(c.sem("y_taken"), 1)
    dve.wait_ge(c.sem("y_squared"), base + chunk + 1)
    if chunk:
        dve.tensor_tensor(t["acc"][:, :, cols], t["acc"][:, :, cols], t["sq"][:, :, cols],
                          ALU.add).then_inc(c.sem("y_added"), 1)
        dve.wait_ge(c.sem("y_added"), base // 4 * 3 + chunk)


def y_stage_split(c, split, take, n0, begun=2):
    for m in range(begun, 18):
        if m == 17:
            take(3, n0 + 16)
        if n0 + m < N_SLOTS:
            split(n0 + m)
        if m % 4 == 1 and m < 17:
            take((m - 5) // 4, n0 + m - 1)



BLOCKS = [(0, 0, 16, 16), (1, 0, 64, 80), (1, 64, 128, 144), (2, 0, 64, 208), (2, 64, 128, 272)]
QUERIES = [(0, 16), (16, 144), (144, 272)]
SCORES_AT = [0, 16, 160]
SCALE = 128 ** -0.5


def attn_load(c, t, sp, a):
    sp.dma_start(c.h[:], a["h0"]).then_inc(c.sem("h_in"), 16)
    sp.dma_start(c.params[:], a["params"]).then_inc(c.sem("params_in"), 16)
    sp.dma_start(c.consts[:], a["consts"]).then_inc(c.sem("params_in"), 16)
    sp.dma_start(t["first"][:], a["consts_first"]).then_inc(c.sem("params_in"), 16)


def attn_pe(c, t, pe):
    ps, S = c.ps, c.sem
    pe.wait_ge(S("lam_products"), 1)
    pe.matmul(ps[:, 4, 0:2], c.const("ones"), t["lam"][:, 0:2], start=True, stop=True).then_inc(S("lam_sums"), 1)

    def scores(v):
        for comp in range(2):
            for q, (a, b) in enumerate(QUERIES):
                m = pe.matmul(ps[0:b - a, 4 + comp, SCORES_AT[q]:SCORES_AT[q] + b], t["qk"][:, comp, a:b],
                              t["qk"][:, 2 + comp, 0:b], start=True, stop=True)
        m.then_inc(S("scores_done"), 1)

    def out_slot(s):
        pe.wait_ge(S("z_lo_ready"), 2 * s + 2)
        products(c, pe, FIRST_SLOT["attn_out"] + s, c.xb, [(k, 4 * s + k) for k in range(4)], banks(c, 0, ROWS),
                 slice(0, ROWS), s == 0, False)

    def values():
        for j in range(2):
            for kb, (a, b) in enumerate([(0, 272), (16, 272), (144, 272)]):
                m = pe.matmul(ps[:, 6 + j, a:b], t["vn"][:, kb, j * P:j * P + P], t["at"][:, kb, a:b],
                              start=kb == 0, stop=kb == 2)
        m.then_inc(S("values_done"), 1)

    def head(h, i, proj, cur, old):
        s0 = 8 * h
        w = lambda sem, v: pe.wait_ge(S(sem), at(v, i, 1))
        if proj:
            if h:
                w("values_out_taken", h)
            for s in range(4):
                if h == 0:
                    pe.wait_ge(S("x_ready"), s + 1)
                products(c, pe, s0 + s, c.xa, [(k, 4 * s + k) for k in range(4)], banks(c, 0, ROWS),
                         slice(0, ROWS), s == 0, s == 3, i, 8)
            if h == 0:
                sum_squares(c, pe, t["acc"], 7, slice(0, ROWS), S("squares_ready"), 1, S("stats_done"))
        if h == HEADS:
            pe.wait_ge(S("values_out_taken"), HEADS)
            out_slot(0)
        if cur:
            w("qk_ready", h)
            if old:
                w("at_ready", h - 1)
                w("vn_ready", h - 1)
            scores(h)
        if old:
            if not cur:
                w("at_ready", h - 1)
                w("vn_ready", h - 1)
            values()
        if proj:
            w("keys_taken", h + 1)
            for s in range(4):
                products(c, pe, s0 + 4 + s, c.xa, [(k, 4 * s + k) for k in range(4)], banks(c, 0, ROWS),
                         slice(0, ROWS), s == 0, s == 3, i, 8)
        if h == HEADS:
            out_slot(1)
        if old:
            if cur:
                w("probs_ready", h)
            w("osq_ready", h - 1)
            for j in range(2):
                m = pe.matmul(ps[:, 5, 0:ROWS], c.const("ones"), t["osq"][:, j, :], start=j == 0, stop=j == 1)
            m.then_inc(S("osum_done"), 1)
        if h > HEADS:
            out_slot(2)
        if cur:
            w("a_ready", h)
            if old:
                w("o_ready", h - 1)
            idt = c.const("ident")
            a = t["a"].rearrange("p (t k) -> p t k", t=3)
            pe.transpose(ps[:, 6, 16:144], a[:, 1, 0:P], idt)
            pe.transpose(ps[:, 6, 0:16], a[0:16, 0, 0:P], idt[0:16, 0:16])
            pe.transpose(ps[:, 6, 144:272], a[:, 2, 0:P], idt)
            pe.transpose(ps[:, 7, 0:128], a[:, 1, P:2 * P], idt)
            pe.transpose(ps[:, 7, 128:256], a[:, 2, P:2 * P], idt)
            pe.transpose(ps[:, 6, 272:400], a[:, 2, 2 * P:3 * P], idt)
            for j in range(2):
                pe.transpose(ps[:, 4, j * P:j * P + P], t["vt"][:, j, 0:P], idt)
                pe.transpose(ps[:, 4, 256 + j * P:384 + j * P], t["vt"][:, j, P:2 * P], idt)
                m = pe.transpose(ps[:, 7, 256 + j * P:384 + j * P], t["vt"][:, j, 2 * P:3 * P], idt)
            m.then_inc(S("turned"), 1)

    head(0, None, True, False, False)
    head(1, None, True, True, False)
    with pe.Fori(0, HEADS - 2) as i:
        head(2, i, True, True, True)
    head(HEADS, None, False, True, True)
    head(HEADS + 1, None, False, False, True)


def attn_act(c, t, act):
    ps, S = c.ps, c.sem
    for n in range(2):
        split_hi(c, act, n)
    act.wait_ge(S("params_in"), 48)
    act.wait_ge(S("h_in"), 16)
    operands_act(c, act, 0, slice(0, ROWS), "pre0", 0)
    act.wait_ge(S("lam_sums"), 1)
    act.activation(t["lam"][:, 2:4], ps[:, 4, 0:2], ACT.Exp).then_inc(S("lam_exps"), 1)

    def head(h, i, proj, cur, old):
        n = 8 * h
        w = lambda sem, v: act.wait_ge(S(sem), at(v, i, 1))
        sp = lambda s: split_hi(c, act, n + s, i, 8)
        if proj:
            if h:
                sp(2)
                sp(3)
            sp(4)
        if h == 0:
            root(c, act, 7, t["sd"], slice(0, ROWS), S("stats_done"), 1, S("root_done"))
        if proj:
            sp(5)
        if h == HEADS:
            sp(2)
        if cur:
            w("negmax_ready", h)
            if old:
                w("a_ready", h - 1)
            for comp in range(2):
                if comp and proj:
                    sp(6)
                for q, a, b, keys in BLOCKS:
                    s = SCORES_AT[q]
                    m = act.activation(t["p"][a:b, comp, q, 0:keys], ps[a:b, 4 + comp, s:s + keys], ACT.Exp,
                                       bias=t["st"][a:b, 6 + 3 * comp + q:7 + 3 * comp + q], scale=SCALE,
                                       accum_out=t["st"][a:b, 12 + 3 * comp + q:13 + 3 * comp + q])
            m.then_inc(S("probs_ready"), 1)
        if proj:
            if not cur:
                sp(6)
            sp(7)
        if old:
            w("o_ready", h - 1)
            act.activation(t["osq"][:], t["o"][:], ACT.Square).then_inc(S("osq_ready"), 1)
        if proj:
            sp(8)
        if old:
            w("osum_done", h - 1)
            act.activation(t["so"][:], ps[:, 5, 0:ROWS], ACT.Sqrt, bias=c.eps["eps"],
                           scale=1.0 / HEAD_V).then_inc(S("oroot_done"), 1)
        if cur:
            sp(9 if proj else 3)
            w("turned", h)
            act.copy(t["at"][:, 0, :], ps[:, 6, 0:272])
            act.copy(t["at"][:, 1, 16:272], ps[:, 7, 0:256])
            act.copy(t["vn"][:, 2, :], ps[:, 7, 256:512])
            act.copy(t["at"][:, 2, 144:272], ps[:, 6, 272:400]).then_inc(S("at_ready"), 1)
        if proj:
            if not cur:
                sp(9)
            w("g_ready", h + 1)
            g = c.y[:, bass.ds(at(2 * h, i, 2), 2), :]
            act.activation(g, g, ACT.Silu).then_inc(S("gate_ready"), 1)
        if old:
            w("z_ready", h - 1)
            act.copy(c.xb[0][:, bass.ds(at(2 * h - 4, i, 2), 2), :], t["o"][:]).then_inc(S("z_hi_ready"), 1)

    head(0, None, True, False, False)
    head(1, None, True, True, False)
    with act.Fori(0, HEADS - 2) as i:
        head(2, i, True, True, True)
    head(HEADS, None, False, True, True)
    head(HEADS + 1, None, False, False, True)


def attn_pool(c, t, pool, st):
    S = c.sem
    pool.wait_ge(S("h_in"), 16)
    squares_pool(c, pool, st, 0, slice(0, ROWS), t["acc"], t["sq"])
    pool.wait_ge(S("stats_done"), 1)
    pool.memset(t["p"][:], 0.0)
    pool.memset(t["a"][:], 0.0)
    pool.memset(t["at"][:], 0.0)
    pool.memset(t["vt"][:], 0.0)
    pool.memset(t["st"][:, 12:18], 1.0)
    pool.memset(t["st"][:, 0:12], 0.0).then_inc(S("zeros_ready"), 1)


def attn_dve(c, t, dve, st):
    ps, S = c.ps, c.sem
    R = slice(0, ROWS)
    dve.memset(c.small[:, 0:1], EPS).then_inc(S("eps_ready"), 1)
    dve.memset(c.small[:, 1:2], RW_EPS).then_inc(S("eps_ready"), 1)
    for n in range(2):
        split_lo(c, dve, n)
    dve.wait_ge(S("params_in"), 48)
    lam = c.params[:, PARAM["lam"]:PARAM["lam"] + 4].rearrange("p (a b) -> p a b", b=2)
    dve.tensor_tensor(t["lam"][:, 0:2], lam[:, :, 0], lam[:, :, 1], ALU.mult).then_inc(S("lam_products"), 1)
    operands_dve(c, dve, st, 0, R, t, None, "pre0", 0)
    dve.wait_ge(S("lam_exps"), 1)
    st.did(dve.scalar_tensor_tensor(out=t["lam"][:, 4:5], in0=t["lam"][:, 2:3], scalar=LAM_INIT,
                                    in1=t["lam"][:, 3:4], op0=ALU.add, op1=ALU.subtract))
    first, _ = columns(CONSTS_FIRST)
    cos = t["first"][0:32, first["rope_cos"][0]:first["rope_cos"][1]]
    sin = t["first"][0:32, first["rope_sin"][0]:first["rope_sin"][1]]
    wide32 = lambda x, n: x.unsqueeze(1).to_broadcast([32, n, ROWS])
    swap = [(p + 16) % 32 for p in range(32)]
    a3 = t["a"].rearrange("p (t k) -> p t k", t=3)
    stat = lambda n, q: t["st"][:, n + q:n + q + 1]

    def rotate(j):
        q = t["qk"][0:32, j:j + 2, :]
        dve.tensor_tensor(t["osq"][0:32], q, wide32(cos, 2), ALU.mult)
        st.did(dve.stream_shuffle(t["rot"][0:32], q, swap))
        st.did(dve.tensor_tensor(t["rot"][0:32], t["rot"][0:32], wide32(sin, 2), ALU.mult))
        return dve.tensor_tensor(q, t["osq"][0:32], t["rot"][0:32], ALU.add)

    def head(h, i, proj, cur, old):
        n = 8 * h
        w = lambda sem, v: dve.wait_ge(S(sem), at(v, i, 1))
        sp = lambda s: split_lo(c, dve, n + s, i, 8)
        if proj:
            if h:
                sp(2)
                sp(3)
            sp(4)
            if h == 0:
                dve.wait_ge(S("root_done"), 1)
                st.did(dve.reciprocal(t["rs"][:], t["sd"][:]))
            dve.wait_ge(S("slot_used"), at(n + 4, i, 8))
            if cur:
                w("scores_done", h)
            dve.tensor_tensor(t["qk"][:], ps[:, 0:4, 0:ROWS], wide(t["rs"][:], 4), ALU.mult).then_inc(S("keys_taken"), 1)
            w("keys_taken", h + 1)
            sp(5)
        elif cur:
            sp(2)
            w("scores_done", h)
        if cur:
            if h == 1:
                dve.wait_ge(S("zeros_ready"), 1)
            for q, a, b, keys in BLOCKS:
                s = SCORES_AT[q]
                m = dve.tensor_reduce(t["st"][a:b, q:q + 4:3], ps[a:b, 4:6, s:s + keys], AX.X, ALU.max)
            st.did(m)
            dve.tensor_scalar(t["st"][:, 6:12], t["st"][:, 0:6], -SCALE, None, ALU.mult).then_inc(S("negmax_ready"), 1)
        if proj:
            st.did(rotate(0))
            sp(6)
            rotate(2).then_inc(S("qk_ready"), 1)
            w("qk_ready", h + 1)
            sp(7)
        if old:
            w("values_done", h - 1)
            dve.tensor_copy(t["o"][:], ps[:, 6:8, 0:ROWS]).then_inc(S("o_ready"), 1)
        if cur:
            w("probs_ready", h)
            st.did(dve.reciprocal(t["st"][:, 18:24], t["st"][:, 12:18]))
            st.did(dve.tensor_scalar(t["st"][:, 21:24], t["st"][:, 21:24], t["lam"][:, 4:5], None, ALU.mult))
            for q in range(3):
                m = dve.tensor_scalar(t["p"][:, 1, q, :], t["p"][:, 1, q, :], stat(21, q), None, ALU.mult)
            st.did(m)
            for q in range(3):
                m = dve.scalar_tensor_tensor(out=a3[:, q, 0:ROWS], in0=t["p"][:, 0, q, :], scalar=stat(18, q),
                                             in1=t["p"][:, 1, q, :], op0=ALU.mult, op1=ALU.subtract)
            m.then_inc(S("a_ready"), 1)
        if proj:
            sp(8)
            dve.wait_ge(S("slot_used"), at(n + 8, i, 8))
            if h == 0:
                dve.wait_ge(S("zeros_ready"), 1)
            dve.tensor_tensor(c.y[:, bass.ds(at(2 * h, i, 2), 2), :], ps[:, 2:4, 0:ROWS], wide(t["rs"][:], 2),
                              ALU.mult).then_inc(S("g_ready"), 1)
        if cur:
            w("turned", h)
        if proj:
            dve.tensor_tensor(t["vt"][:, :, 0:ROWS], ps[:, 0:2, 0:ROWS], wide(t["rs"][:], 2),
                              ALU.mult).then_inc(S("values_out_taken"), 1)
            sp(9)
        if cur:
            dve.tensor_copy(t["vn"][:, 0:2, :], ps[:, 4, :].rearrange("p (b n) -> p b n", b=2)).then_inc(S("vn_ready"), 1)
            if not proj:
                sp(3)
        if old:
            w("oroot_done", h - 1)
            st.did(dve.reciprocal(t["ro"][:], t["so"][:]))
            w("o_ready", h - 1)
            st.did(dve.tensor_tensor(t["o"][:], t["o"][:], wide(t["ro"][:], 2), ALU.mult))
            w("gate_ready", h - 1)
            for j in range(2):
                m = dve.scalar_tensor_tensor(out=t["o"][:, j, :], in0=t["o"][:, j, :], scalar=t["gain"][:, j:j + 1],
                                             in1=c.y[:, bass.ds(at(2 * h - 4 + j, i, 2), 1), :].rearrange("p a r -> p (a r)"),
                                             op0=ALU.mult, op1=ALU.mult)
            m.then_inc(S("z_ready"), 1)
            w("z_hi_ready", h - 1)
            w("z_ready", h - 1)
            zs = bass.ds(at(2 * h - 4, i, 2), 2)
            dve.tensor_tensor(c.xb[1][:, zs, :], t["o"][:], c.xb[0][:, zs, :].bitcast(F32),
                              ALU.subtract).then_inc(S("z_lo_ready"), 1)
            w("z_lo_ready", h - 1)

    st.did(dve.tensor_scalar(t["gain"][:], c.params[:, PARAM["subln"]:PARAM["subln"] + 2], 1.0 - LAM_INIT, None, ALU.mult))
    head(0, None, True, False, False)
    head(1, None, True, True, False)
    with dve.Fori(0, HEADS - 2) as i:
        st.enter(i, 11)
        head(2, i, True, True, True)
    st.leave(HEADS - 2)
    head(HEADS, None, False, True, True)
    head(HEADS + 1, None, False, False, True)



def norm_between_pe(c, pe, t, base, cols, norm):
    sum_squares(c, pe, t["acc"], 0, cols, c.sem("y_added"), base // 4 * 3 + 3, c.sem("stats_done"))


def boundary_act(c, act, t, b, norm, cols, g_pre, n):
    root(c, act, 0, t["sd"], cols, c.sem("stats_done"), norm + 1, c.sem("root_done"))
    operands_act(c, act, b, cols, g_pre, n)


def boundary_dve(c, dve, st, t, b, norm, cols, g_post, g_pre, n):
    dve.wait_ge(c.sem("root_done"), norm + 1)
    st.did(dve.reciprocal(t["rs"][:, cols], t["sd"][:, cols]))
    operands_dve(c, dve, st, b, cols, t, g_post, g_pre, n)


def pre_root_act(c, act, t, norm, cols):
    root(c, act, 7, t["sd"], cols, c.sem("stats_done"), norm + 1, c.sem("root_done"))


def pre_root_dve(c, dve, st, t, norm, cols):
    dve.wait_ge(c.sem("root_done"), norm + 1)
    st.did(dve.reciprocal(t["rs"][:, cols], t["sd"][:, cols]))


def first_chunk_pe(c, pe, t, n0, x, b, cols, norm, squares):
    for s in range(4):
        pe.wait_ge(c.sem("x_ready"), 4 * b + s + 1)
        products(c, pe, n0 + s, x, [(k, 4 * s + k) for k in range(4)],
                 banks(c, 0, cols.stop - cols.start), cols, s == 0, s == 3)
    if squares:
        sum_squares(c, pe, t["acc"], 7, cols, c.sem("squares_ready"), squares, c.sem("stats_done"))


def mid_pe(c, t, pe):
    S = c.sem
    R = slice(0, ROWS)
    n0 = FIRST_SLOT["attn_out"]
    pe.wait_ge(S("z_lo_ready"), HEADS)
    y_stage_pe(c, pe, n0, c.xb, R, 0, begun=3)
    norm_between_pe(c, pe, t, 0, R, 1)
    n0 = FIRST_SLOT["pool_in"]
    first_chunk_pe(c, pe, t, n0, c.xa, 1, R, 2, 2)

    def chunk(n, half, free, i=None, pause=None):
        if free is not None:
            pe.wait_ge(S("pool_in_taken"), at(free, i, 2))
        for s in range(4):
            products(c, pe, n + s, c.xa, [(k, 4 * s + k) for k in range(4)], banks(c, half, ROWS), R, s == 0, s == 3, i, 8,
                     pause=pause if s == 0 else None)

    chunk(n0 + 4, 1, None, pause=lambda: pe.wait_ge(S("root_done"), 3))
    with pe.Fori(0, 3) as i:
        chunk(n0 + 8, 0, 1, i)
        chunk(n0 + 12, 1, 2, i)
    for g in range(4):
        pe.wait_ge(S("pool_in_taken" if g < 2 else "pooled_done"), 7 + g if g < 2 else g - 1)
        pe.wait_ge(S("mixed_ready"), g + 1)
        products(c, pe, FIRST_SLOT["pool_group"] + g, c.xb, [(k, 4 * g + k) for k in range(4)],
                 banks(c, g % 2, ROWS), R, True, True)
    n0 = FIRST_SLOT["pool_out"]
    pe.wait_ge(S("pooled_done"), 3)
    y_stage_pe(c, pe, n0, c.xa, BOTH, 4, lambda s: pe.wait_ge(S("pooled_ready"), s + 1))
    norm_between_pe(c, pe, t, 4, BOTH, 3)


def mid_act(c, t, act):
    S = c.sem
    R = slice(0, ROWS)
    n0 = FIRST_SLOT["attn_out"]
    y_stage_split(c, lambda n: split_hi(c, act, n), lambda chunk, n: y_take_act(c, act, chunk, R, 0, t), n0, 4)
    boundary_act(c, act, t, 1, 1, R, "pre1", FIRST_SLOT["pool_in"])
    n0 = FIRST_SLOT["pool_in"]

    def mixed(g):
        act.wait_ge(S("mixed_done"), g + 1)
        act.copy(c.xb[0][:, 4 * g:4 * g + 4, :], t["mixed"][:]).then_inc(S("mixed_hi"), 1)

    for m in range(4, 34):
        split_hi(c, act, n0 + m)
        if m == 5:
            pre_root_act(c, act, t, 2, R)
        if m % 4 == 3 and 7 <= m <= 19:
            mixed((m - 7) // 4)
        if m % 4 == 1 and m >= 21:
            chunk = (m - 5) // 4
            act.wait_ge(S("pool_in_taken"), chunk + 1)
            g = c.y[:, 4 * chunk - 16:4 * chunk - 12, :]
            act.activation(g, g, ACT.Silu).then_inc(S("pool_gate"), 1)
    for g in range(4):
        split_hi(c, act, n0 + 34 + g)
        act.wait_ge(S("pooled_done"), g + 1)
        act.copy(c.xa[0][:, 4 * g:4 * g + 4, :], t["tmp"][:]).then_inc(S("pooled_hi"), 1)
    y_stage_split(c, lambda n: split_hi(c, act, n), lambda chunk, n: y_take_act(c, act, chunk, BOTH, 4, t),
           FIRST_SLOT["pool_out"])
    boundary_act(c, act, t, 2, 3, BOTH, "pre_mix", FIRST_SLOT["rw_down"])


def mid_pool(c, t, pool, st):
    S = c.sem
    R = slice(0, ROWS)
    squares_pool(c, pool, st, 1, R, t["acc"], t["sq"])
    first, _ = columns(CONSTS_FIRST)
    for g, width in enumerate(POOL_WINDOWS):
        u = t["u"][g % 2]
        pool.wait_ge(S("pool_in_taken"), g + 1)
        src, flip = u, 0
        for n in range(g + 1):
            s, dst = 2 ** n, t["sums"][flip]
            pool.tensor_copy(dst[:, :, 0:s], src[:, :, 0:s])
            st.did(pool.tensor_tensor(dst[:, :, s:], src[:, :, s:], src[:, :, 0:ROWS - s], ALU.add))
            src, flip = dst, 1 - flip
        a = first["inv_count"][0] + 16 * g
        count = t["first"][:, a:a + 16]
        if g:
            pool.wait_ge(S("mixed_ready"), g)
        pool.tensor_tensor(t["mixed"][:, :, 0:16], src[:, :, 0:16], wide(count, 4), ALU.mult)
        st.did(pool.tensor_scalar(t["mixed"][:, :, 16:], src[:, :, 16:], 1.0 / width, None, ALU.mult))
        pool.tensor_tensor(t["mixed"][:], t["mixed"][:], u[:], ALU.subtract).then_inc(S("mixed_done"), 1)
        pool.wait_ge(S("mixed_done"), g + 1)
    squares_pool(c, pool, st, 2, BOTH, t["acc"], t["sq"])


def mid_dve(c, t, dve, st):
    S, ps = c.sem, c.ps
    R = slice(0, ROWS)
    n0 = FIRST_SLOT["attn_out"]
    y_stage_split(c, lambda n: split_lo(c, dve, n), lambda chunk, n: y_take_dve(c, dve, chunk, n, R, 0, t), n0, 4)
    boundary_dve(c, dve, st, t, 1, 1, R, "post0", "pre1", FIRST_SLOT["pool_in"])
    n0 = FIRST_SLOT["pool_in"]

    def mixed(g):
        dve.wait_ge(S("mixed_hi"), g + 1)
        dve.tensor_tensor(c.xb[1][:, 4 * g:4 * g + 4, :], t["mixed"][:], c.xb[0][:, 4 * g:4 * g + 4, :].bitcast(F32),
                          ALU.subtract).then_inc(S("mixed_ready"), 1)

    for m in range(4, 34):
        split_lo(c, dve, n0 + m)
        if m == 5:
            pre_root_dve(c, dve, st, t, 2, R)
        if m % 4 == 1:
            chunk = (m - 5) // 4
            dve.wait_ge(S("slot_used"), n0 + m - 1)
            if 2 <= chunk < 4:
                dve.wait_ge(S("mixed_done"), chunk - 1)
            out = t["u"][chunk % 2][:] if chunk < 4 else c.y[:, 4 * chunk - 16:4 * chunk - 12, :]
            dve.tensor_tensor(out, ps[:, 4 * (chunk % 2):4 * (chunk % 2) + 4, 0:ROWS], wide(t["rs"][:], 4),
                              ALU.mult).then_inc(S("pool_in_taken"), 1)
        if m % 4 == 3 and 7 <= m <= 19:
            mixed((m - 7) // 4)
    for g in range(4):
        split_lo(c, dve, n0 + 34 + g)
        dve.wait_ge(S("slot_used"), n0 + 33 + g)
        dve.wait_ge(S("pool_gate"), g + 1)
        for j in range(4):
            k = 4 * g + j
            m = dve.scalar_tensor_tensor(out=t["tmp"][:, j, :], in0=ps[:, 4 * (g % 2) + j, 0:ROWS], scalar=c.param("pool_scale", k),
                                         in1=c.y[:, k, :], op0=ALU.mult, op1=ALU.mult)
        m.then_inc(S("pooled_done"), 1)
        dve.wait_ge(S("pooled_done"), g + 1)
        dve.wait_ge(S("pooled_hi"), g + 1)
        dve.tensor_tensor(c.xa[1][:, 4 * g:4 * g + 4, :], t["tmp"][:], c.xa[0][:, 4 * g:4 * g + 4, :].bitcast(F32),
                          ALU.subtract).then_inc(S("pooled_ready"), 1)
        dve.wait_ge(S("pooled_ready"), g + 1)
    y_stage_split(c, lambda n: split_lo(c, dve, n), lambda chunk, n: y_take_dve(c, dve, chunk, n, BOTH, 4, t),
           FIRST_SLOT["pool_out"])
    boundary_dve(c, dve, st, t, 2, 3, BOTH, "post1", "pre_mix", FIRST_SLOT["rw_down"])



CHUNKS = SEQ // RW_N
DECAY = math.exp(-0.5)


def unit(j, cc, p):
    return p * 8 + j * 2 + cc


def angles_dve(c, t, dve, st):
    pi = 3.1415925
    parts = (6.28125, 2029 * 2.0 ** -20, 2 * math.pi - 6.28125 - 2029 * 2.0 ** -20)
    x, turns = t["cos2"], t["sin2"]
    dve.wait_ge(c.sem("positions_in"), 16)
    st.did(dve.tensor_copy(t["kpe"][:], t["positions"][:]))
    st.did(dve.tensor_scalar(x[:], t["kpe"][:], c.param("inv_freq", 0), None, ALU.mult))
    st.did(dve.tensor_scalar(turns[:], x[:], 1 / (2 * math.pi), 12582912.0, ALU.mult, ALU.add))
    st.did(dve.tensor_scalar(turns[:], turns[:], 12582912.0, None, ALU.subtract))
    for part in parts:
        st.did(dve.scalar_tensor_tensor(out=x[:], in0=turns[:], scalar=-part, in1=x[:], op0=ALU.mult, op1=ALU.add))
    st.did(dve.tensor_scalar(turns[:], x[:], pi, -pi, ALU.min, ALU.max))
    st.did(dve.tensor_scalar(t["kpe"][:], x[:], math.pi / 2, 2 * math.pi, ALU.is_gt, ALU.mult))
    st.did(dve.scalar_tensor_tensor(out=x[:], in0=x[:], scalar=math.pi / 2, in1=t["kpe"][:], op0=ALU.add, op1=ALU.subtract))
    dve.tensor_scalar(x[:], x[:], pi, -pi, ALU.min, ALU.max).then_inc(c.sem("angles_ready"), 1)


def shifted(c, dve, st, t, half, tiles, mu, mu_at, out, taken, split=None):
    z = t["zp"]
    dve.memset(z[:, :, 0:1], 0.0)
    turn = c.turns[taken] = c.turns.get(taken, 0) + 1
    dve.tensor_tensor(z[:, :, 1:257], c.ps[:, 4 * half:4 * half + 4, 0:SEQ], wide(t["rs"][:, BOTH], 4),
                      ALU.mult).then_inc(c.sem(taken), 1)
    if split:
        split_lo(c, dve, split)
    dve.wait_ge(c.sem(taken), turn)
    st.did(dve.tensor_tensor(out[:, 0:tiles, :], z[:, 0:tiles, 0:256], z[:, 0:tiles, 1:257], ALU.subtract))
    for j in range(tiles):
        m = dve.scalar_tensor_tensor(out=out[:, j, :], in0=out[:, j, :], scalar=c.param(mu, mu_at + j),
                                     in1=z[:, j, 1:257], op0=ALU.mult, op1=ALU.add)
    m.then_inc(c.sem(taken + "_out"), 1)
    dve.wait_ge(c.sem(taken + "_out"), turn)


def rw_pe(c, t, pe):
    ps, S = c.ps, c.sem
    first_chunk_pe(c, pe, t, FIRST_SLOT["rw_down"], c.xa, 2, BOTH, 4, 3)
    t4 = lambda s: [(k, 4 * s + k) for k in range(4)]
    ones = c.const("head_ones")
    at_, cuts = [slice(0, 64), slice(64, 128)], [slice(64 * x, 64 * x + 64) for x in range(CHUNKS)]

    def head_sums(src, bank, done):
        for j in range(4):
            m = pe.matmul(ps[:, bank + j // 2, 256 * (j % 2):256 * (j % 2) + 256], ones, src[:, j, :], start=True, stop=True)
        m.then_inc(S(done), 1)

    for b in range(2):
        n = FIRST_SLOT[f"rw_half{b}"]
        if b:
            pe.wait_ge(S("yt_added"), 3)
        for s in range(4):
            pause = (lambda: pe.wait_ge(S("root_done"), 5)) if s == b == 0 else None
            products(c, pe, n + s, c.xa, t4(s), banks(c, 1, SEQ), BOTH, s == 0, s == 3, pause=pause)
            if s == 0 and b:
                pe.wait_ge(S("centred_squared"), 1)
                head_sums(t["sq"], 2, "vars_done")

        def small(slot, parts):
            w_hi, w_lo = c.w_hi[slot % SPLIT], c.w_lo[slot % SPLIT]
            x_hi, x_lo = t["lora_hi"], t["lora_lo"]
            pe.wait_ge(S("lo_done"), slot + 1)
            for bank, tiles in parts:
                for j in range(4):
                    out = ps[:, bank + j // 2, 256 * (j % 2):256 * (j % 2) + 256]
                    for k, rows in tiles:
                        a = slice(j * P, j * P + P)
                        pe.matmul(out, w_hi[rows, k, a], x_hi[rows, k, :], start=k == tiles[0][0], stop=False)
                        pe.matmul(out, w_hi[rows, k, a], x_lo[rows, k, :], start=False, stop=False)
                        m = pe.matmul(out, w_lo[rows, k, a], x_hi[rows, k, :], start=False, stop=k == tiles[-1][0])
            m.then_inc(S("slot_used"), 1)

        pe.wait_ge(S("lora_ready"), 1)
        pe.wait_ge(S("vars_rooted" if b else "down_taken_rw"), 1)
        small(n + 4, [(0, [(0, at_[0])]), (2, [(0, at_[1])])])
        pe.wait_ge(S("rw_k_taken"), b + 1)
        for s in range(4):
            products(c, pe, n + 5 + s, c.xa, t4(s), banks(c, 1, SEQ), BOTH, s == 0, s == 3)
            if s == 1:
                pe.wait_ge(S("wa_taken"), b + 1)
                pe.wait_ge(S("kk_squared"), b + 1)
                head_sums(t["bon"], 2, "kk_summed")
        small(n + 9, [(0, [(1, slice(0, P)), (2, slice(0, P))])])
        pe.wait_ge(S("rw_r_taken"), b + 1)
        for s in range(4):
            products(c, pe, n + 10 + s, c.xa, t4(s), banks(c, 1, SEQ), BOTH, s == 0, s == 3)
            if s == 2:
                pe.wait_ge(S("bonus_in"), b + 1)
                head_sums(t["bon"], 2, "bonus_summed")
        pe.wait_ge(S("tilde_ready"), b + 1)
        pe.wait_ge(S("g_taken"), b + 1)
        pe.wait_ge(S("bonus_taken"), b + 1)
        for base, src, done in ((0, t["bt"], "gram_b"), (4, t["kt"], "gram_k")):
            if base:
                pe.wait_ge(S("rw_v_taken"), b + 1)
            for j in range(4):
                for x in range(CHUNKS):
                    for p in range(2):
                        u = unit(j, x // 2, p)
                        m = pe.matmul(ps[at_[x % 2], base + u // 4, 128 * (u % 4):128 * (u % 4) + 128],
                                      src[at_[p], j, cuts[x]], t["ar"][at_[p], j, x, :], start=True, stop=True)
            m.then_inc(S(done), 1)
        pe.wait_ge(S("gram_b_taken"), b + 1)
        for j in range(4):
            for x in range(CHUNKS):
                for p in range(2):
                    u = unit(j, x // 2, p)
                    m = pe.matmul(ps[at_[x % 2], u // 8, 64 * (u % 8):64 * (u % 8) + 64],
                                  t["ar"][at_[p], j, x, 0:64], t["bt"][at_[p], j, cuts[x]], start=True, stop=True)
        m.then_inc(S("gram_l"), 1)
        pe.wait_ge(S("gram_k_taken"), b + 1)
        pe.wait_ge(S("gram_l_taken"), b + 1)
        for level in range(1, 6):
            v = 2 * (5 * b + level - 1)
            pe.wait_ge(S("masked_ready"), 5 * b + level)
            for g in range(2):
                if level > 1:
                    pe.wait_ge(S("xy_ready"), v - 2 + g + 1)
                for u in range(8 * g, 8 * g + 8):
                    for q in range(2):
                        m = pe.matmul(ps[at_[q], g, 64 * (u % 8):64 * (u % 8) + 64], t["lm"][at_[q], u, :],
                                      t["yy"][at_[q], u, :], start=True, stop=True)
                m.then_inc(S("tm_done"), 1)
            for g in range(2):
                pe.wait_ge(S("t_ready"), v + g + 1)
                for u in range(8 * g, 8 * g + 8):
                    for q in range(2):
                        cut = slice(64 * (u % 8), 64 * (u % 8) + 64)
                        if level < 5:
                            pe.matmul(ps[at_[q], 2 + g, cut], t["tt"][at_[q], u, :], t["xx"][at_[q], u, :], start=True, stop=True)
                        m = pe.matmul(ps[at_[q], 4 + g, cut], t["xx"][at_[q], u, :], t["tt"][at_[q], u, :], start=True, stop=True)
                m.then_inc(S("xy_done"), 1)
        pe.wait_ge(S("xy_ready"), 10 * b + 10)
        for n_, (src, base) in enumerate(((t["bt"], 0), (t["kt"], 2), (t["v"], 6))):
            for j in range(4):
                for cc in range(2):
                    m = pe.transpose(ps[:, base + j // 2, 128 * (2 * (j % 2) + cc):128 * (2 * (j % 2) + cc) + 128],
                                     src[:, j, 128 * cc:128 * cc + 128], c.const("ident"))
            m.then_inc(S("turned_rw"), 1)
        pe.wait_ge(S("turned_taken"), 3 * b + 3)
        for p in range(2):
            for u in range(8 * p, 8 * p + 8):
                for q in range(2):
                    m = pe.matmul(ps[at_[q], p, 64 * (u % 8):64 * (u % 8) + 64], t["la"][at_[q], u, :], t["nv"][at_[q], u, :],
                                  start=True, stop=True)
        m.then_inc(S("lv_done"), 1)
        pe.wait_ge(S("lv_taken"), b + 1)
        for x in range(CHUNKS):
            q, cc, v = x % 2, x // 2, CHUNKS * b + x
            own = [(p, j, unit(j, cc, p), 4 * p + j, slice(64 * j, 64 * j + 64)) for p in range(2) for j in range(4)]
            if x:
                pe.wait_ge(S("state_ready"), 3 * b + x)
                for p, j, u, u8, cut in own:
                    m = pe.matmul(ps[at_[q], 4 + p, cut], t["ar"][at_[p], j, x, 0:64], t["state"][at_[p], j, :], start=True, stop=True)
                m.then_inc(S("p_done"), 1)
                pe.wait_ge(S("yt_copied"), v)
                if x > 1:
                    pe.wait_ge(S("yt_added"), 3 * b + x - 1)
                for p, j, u, u8, cut in own:
                    m = pe.matmul(ps[at_[p], 2, cut], t["state"][at_[p], j, :], t["ar"][at_[p], j, x, 64:128], start=True, stop=True)
                m.then_inc(S("ys_done"), 1)
                pe.wait_ge(S("p_taken"), 3 * b + x)
            for p, j, u, u8, cut in own:
                rhs = t["pb"][at_[q], u8, :] if x else t["la"][at_[q], u, :]
                m = pe.matmul(ps[at_[q], 6, 64 * u8:64 * u8 + 64], t["yy"][at_[q], u, :], rhs, start=True, stop=True)
            m.then_inc(S("sa_done"), 1)
            pe.wait_ge(S("sa_taken"), v + 1)
            if x < CHUNKS - 1:
                for p, j, u, u8, cut in own:
                    out = ps[at_[p], 7, cut]
                    pe.matmul(out, t["nb"][at_[q], u, :], t["sa"][at_[q], u8, :], start=True, stop=False)
                    m = pe.matmul(out, t["nk"][at_[q], u, :], t["nv"][at_[q], u, :], start=False, stop=True)
                m.then_inc(S("ds_done"), 1)
            for p, j, u, u8, cut in own:
                out = ps[at_[p], 3, cut]
                pe.matmul(out, t["sa"][at_[q], u8, :], t["mr"][at_[q], u, :], start=True, stop=False)
                m = pe.matmul(out, t["nv"][at_[q], u, :], t["mk"][at_[q], u, :], start=False, stop=True)
            m.then_inc(S("yt_done"), 1)
        pe.wait_ge(S("yt_added"), 3 * (b + 1))
        head_sums(t["yt"], 0, "means_done")


def rw_act(c, t, act):
    ps, S = c.ps, c.sem
    n = FIRST_SLOT["rw_down"]
    half = lambda x: ps[:, x:x + 2, :].rearrange("p b (j r) -> p (b j) r", j=2)
    for m in range(4, 6):
        split_hi(c, act, n + m)
    root(c, act, 7, t["sd"], BOTH, S("stats_done"), 5, S("root_done"))
    first = FIRST_SLOT["rw_half0"]
    split_hi(c, act, first + 2)
    act.wait_ge(S("down_taken_rw_out"), 1)
    x = t["lora"]
    act.activation(x[0:64, 0, :], x[0:64, 0, :], ACT.Tanh)
    act.activation(x[:, 1:3, :], x[:, 1:3, :], ACT.Sigmoid).then_inc(S("act_step"), 1)
    act.wait_ge(S("act_step"), 1)
    act.copy(t["lora_hi"][:], x[:]).then_inc(S("lora_hi"), 1)
    split_hi(c, act, first + 3)
    split_hi(c, act, first + 4)
    act.wait_ge(S("angles_ready"), 1)
    act.activation(t["sin2"][:], t["sin2"][:], ACT.Sin)
    act.activation(t["cos2"][:], t["cos2"][:], ACT.Sin).then_inc(S("sines_ready"), 1)
    for b in range(2):
        n = FIRST_SLOT[f"rw_half{b}"]
        if b:
            split_hi(c, act, n + 2)
            rw_root(c, t, act, 0)
        for m in range(3 if b else 5, 7):
            split_hi(c, act, n + m)
        for bank, out, name in ((0, t["w"], "w0"), (2, t["a"], "a0")):
            for j in range(4):
                m = act.activation(out[:, j, :], ps[:, bank + j // 2, 256 * (j % 2):256 * (j % 2) + 256], ACT.Sigmoid,
                                   bias=c.param(name, 4 * b + j))
        m.then_inc(S("wa_taken"), 1)
        split_hi(c, act, n + 7)
        act.wait_ge(S("kk_summed"), b + 1)
        act.activation(t["bon"][:], half(2), ACT.Sqrt).then_inc(S("kk_rooted"), 1)
        split_hi(c, act, n + 8)
        act.wait_ge(S("logs_ready"), b + 1)
        act.activation(t["w"][:], t["w"][:], ACT.Exp, scale=-DECAY)
        act.activation(t["cs"][:], t["tt4"], ACT.Exp, scale=-DECAY).then_inc(S("act_step"), 1)
        act.wait_ge(S("act_step"), b + 2)
        act.activation(t["tt4"], t["tt4"], ACT.Exp, scale=DECAY).then_inc(S("exps_ready"), 1)
        split_hi(c, act, n + 9)
        split_hi(c, act, n + 10)
        split_hi(c, act, n + 11)
        if b:
            act.wait_ge(S("rw_out"), 1)
        act.copy(t["g"][:], half(0)).then_inc(S("g_taken"), 1)
        for m in range(12, 15):
            split_hi(c, act, n + m)
        act.wait_ge(S("bonus_summed"), b + 1)
        act.copy(t["bon"][:], half(2)).then_inc(S("bonus_taken"), 1)
        split_hi(c, act, n + 15)
        for level in range(1, 6):
            for g in range(2):
                v = 2 * (5 * b + level - 1) + g + 1
                act.wait_ge(S("tm_done"), v)
                act.copy(t["tt"][:, 8 * g:8 * g + 8, :], ps[:, g, :].rearrange("p (u i) -> p u i", u=8)).then_inc(S("t_ready"), 1)
        for i, (dst, base) in enumerate(((t["nb"], 0), (t["nk"], 2), (t["nv"], 6))):
            act.wait_ge(S("turned_rw"), 3 * b + i + 1)
            act.copy(dst[:].rearrange("p (q u) i -> p q u i", q=2),
                     ps[:, base:base + 2, :].rearrange("p b (m q i) -> p q (b m) i", m=4, q=2)).then_inc(S("turned_taken"), 1)
        act.wait_ge(S("lv_done"), b + 1)
        act.copy(t["la"][:], ps[:, 0:2, :].rearrange("p b (u i) -> p (b u) i", u=8)).then_inc(S("lv_taken"), 1)
        for x in range(CHUNKS):
            q, v = slice(64 * (x % 2), 64 * (x % 2) + 64), CHUNKS * b + x + 1
            act.wait_ge(S("sa_done"), v)
            act.copy(t["sa"][q], ps[q, 6, :].rearrange("p (u i) -> p u i", u=8)).then_inc(S("sa_taken"), 1)
            act.wait_ge(S("yt_done"), v)
            act.copy(t["yt"][:, :, 64 * x:64 * x + 64], ps[:, 3, 0:256].rearrange("p (j i) -> p j i", j=4)).then_inc(S("yt_copied"), 1)
        act.wait_ge(S("centred"), b + 1)
        act.activation(t["sq"][:], t["yt"][:], ACT.Square).then_inc(S("centred_squared"), 1)


def rw_root(c, t, act, b):
    act.wait_ge(c.sem("vars_done"), b + 1)
    act.activation(t["sq"][:], c.ps[:, 2:4, :].rearrange("p b (j r) -> p (b j) r", j=2), ACT.Sqrt, bias=c.eps["rw"],
                   scale=1.0 / RW_N).then_inc(c.sem("vars_rooted"), 1)


def rw_pool(c, t, pool, st, a):
    S = c.sem
    pool.wait_ge(S("squares_ready"), 3)
    pool.wait_ge(S("stats_done"), 5)
    pool.wait_ge(S("x_ready"), 12)
    pool.dma_start(t["masks"][:], a["consts_rw"]).then_inc(S("consts_rw_in"), 16)
    pool.dma_start(t["positions"][:], a["positions"].partition_broadcast(P)).then_inc(S("positions_in"), 16)
    masks, _ = columns(CONSTS_RW)
    k_a = PARAM["k_a"]
    st.did(pool.tensor_scalar(c.small[:, 8:16], c.params[:, k_a:k_a + 8], -1.0, 1.0, ALU.mult, ALU.add))
    for b in range(2):
        if b:
            rw_gated(c, t, pool, st, 0)
        pool.wait_ge(S("rw_k_taken_out"), b + 1)
        for j in range(4):
            m = pool.tensor_scalar(t["kk"][:, j, :], t["k"][:, j, :], c.param("k_k", 4 * b + j), None, ALU.mult)
        st.did(m)
        pool.tensor_tensor(t["bon"][:], t["kk"][:], t["kk"][:], ALU.mult).then_inc(S("kk_squared"), 1)
        pool.wait_ge(S("wa_taken"), b + 1)
        for j in range(4):
            m = pool.tensor_scalar(t["r"][:, j, :], t["a"][:, j, :], c.param("k_a", 4 * b + j),
                                   c.small[:, 8 + 4 * b + j:9 + 4 * b + j], ALU.mult, ALU.add)
        st.did(m)
        pool.tensor_tensor(t["k"][:], t["k"][:], t["r"][:], ALU.mult).then_inc(S("key_scaled"), 1)
        pool.wait_ge(S("key_scaled"), b + 1)
        pool.wait_ge(S("exps_ready"), b + 1)
        pool.tensor_tensor(t["kt"][:], t["k"][:], t["tt4"], ALU.mult)
        pool.tensor_tensor(t["a"][:], t["a"][:], t["tt4"], ALU.mult).then_inc(S("key_tilde"), 1)
        pool.wait_ge(S("consts_rw_in"), 16)
        pool.wait_ge(S("gram_l_taken"), b + 1)
        for level in range(1, 6):
            if level > 1:
                pool.wait_ge(S("tm_done"), 2 * (5 * b + level - 1))
            mask = t["masks"][:, masks[f"level{level}"][0]:masks[f"level{level}"][1]]
            pool.tensor_tensor(t["lm"][:], t["ll"][:], wide(mask, 16), ALU.mult).then_inc(S("masked_ready"), 1)


def rw_dve(c, t, dve, st):
    ps, S = c.ps, c.sem
    n = FIRST_SLOT["rw_down"]
    masks, _ = columns(CONSTS_RW)
    mask = lambda name, k=16: wide(t["masks"][:, masks[name][0]:masks[name][1]], k)
    half = lambda x: ps[:, x:x + 2, :].rearrange("p b (j r) -> p (b j) r", j=2)
    for m in range(4, 6):
        split_lo(c, dve, n + m)
    dve.wait_ge(S("root_done"), 5)
    st.did(dve.reciprocal(t["rs"][:, BOTH], t["sd"][:, BOTH]))
    dve.wait_ge(S("slot_used"), n + 4)
    shifted(c, dve, st, t, 0, 3, "mu_lora", 0, t["lora"], "down_taken_rw")
    split_lo(c, dve, FIRST_SLOT["rw_half0"] + 2)
    dve.wait_ge(S("lora_hi"), 1)
    dve.tensor_tensor(t["lora_lo"][:], t["lora"][:], t["lora_hi"][:].bitcast(F32), ALU.subtract).then_inc(S("lora_ready"), 1)
    split_lo(c, dve, FIRST_SLOT["rw_half0"] + 3)
    dve.wait_ge(S("consts_rw_in"), 16)
    angles_dve(c, t, dve, st)
    split_lo(c, dve, FIRST_SLOT["rw_half0"] + 4)
    dve.wait_ge(S("sines_ready"), 1)
    st.did(dve.tensor_scalar(t["sin2"][:], t["sin2"][:], c.param("rope_sign", 0), None, ALU.mult))
    swap = [(p + 16) % 32 for p in range(32)]
    key = t["zp"][:, 3, 1:257]
    st.did(dve.stream_shuffle(t["kpe"][:], key, swap))
    dve.tensor_tensor(t["kpe"][:], t["kpe"][:], t["sin2"][:], ALU.mult)
    st.did(dve.tensor_tensor(key, key, t["cos2"][:], ALU.mult))
    st.did(dve.tensor_tensor(t["kpe"][:], t["kpe"][:], key, ALU.add))
    for b in range(2):
        n = FIRST_SLOT[f"rw_half{b}"]
        if b:
            split_lo(c, dve, n + 2)
            rw_finish(c, t, dve, st, 0, lambda m: split_lo(c, dve, n + m))
        dve.wait_ge(S("slot_used"), n + 4)
        shifted(c, dve, st, t, 1, 4, "mu_rkv", 8 + 4 * b, t["k"], "rw_k_taken", n + 5)
        split_lo(c, dve, n + 6)
        dve.wait_ge(S("wa_taken"), b + 1)
        by_chunk = lambda x: x.rearrange("p j (x i) -> p (j x) i", x=CHUNKS)
        src, dst, other = t["w"][:], t["cs"][:], t["tt4"]
        for level in range(6):
            s, a, d = 2 ** level, by_chunk(src), by_chunk(dst)
            dve.tensor_copy(d[:, :, 0:s], a[:, :, 0:s])
            st.did(dve.tensor_tensor(d[:, :, s:], a[:, :, s:], a[:, :, 0:RW_N - s], ALU.add))
            src, dst, other = dst, other, dst
            if level in (1, 4):
                split_lo(c, dve, n + (7 if level == 1 else 8))
        dve.tensor_tensor(t["w"][:], src, t["w"][:], ALU.subtract).then_inc(S("logs_ready"), 1)
        dve.wait_ge(S("kk_rooted"), b + 1)
        st.did(dve.tensor_scalar(t["bon"][:], t["bon"][:], 1e-12, None, ALU.max))
        dve.reciprocal(t["bon"][:, 0:2], t["bon"][:, 0:2])
        split_lo(c, dve, n + 9)
        st.did(dve.reciprocal(t["bon"][:, 2:4], t["bon"][:, 2:4]))
        split_lo(c, dve, n + 10)
        dve.wait_ge(S("slot_used"), n + 9)
        dve.wait_ge(S("key_scaled"), b + 1)
        shifted(c, dve, st, t, 1, 4, "mu_rkv", 4 * b, t["r"], "rw_r_taken", n + 11)
        st.did(dve.tensor_tensor(t["kk"][:], t["kk"][:], t["bon"][:], ALU.mult))
        for j in range(4):
            m = dve.scalar_tensor_tensor(out=t["bon"][:, j, :], in0=t["r"][:, j, :], scalar=c.param("r_k", 4 * b + j),
                                         in1=t["k"][:, j, :], op0=ALU.mult, op1=ALU.mult)
        m.then_inc(S("bonus_in"), 1)
        split_lo(c, dve, n + 12)
        dve.wait_ge(S("exps_ready"), b + 1)
        ar = t["ar"][:].rearrange("p j x (s i) -> p (j x) s i", s=2)
        dve.scalar_tensor_tensor(out=ar[:, :, 0, :], in0=by_chunk(t["kk"][:]), scalar=-1.0, in1=by_chunk(t["w"][:]),
                                 op0=ALU.mult, op1=ALU.mult)
        split_lo(c, dve, n + 13)
        dve.wait_ge(S("key_tilde"), b + 1)
        dve.tensor_tensor(t["bt"][:], t["kk"][:], t["a"][:], ALU.mult)
        dve.tensor_copy(t["ends"][:], t["cs"][:].rearrange("p j (x i) -> p j x i", x=CHUNKS)[:, :, :, RW_N - 1])
        dve.tensor_tensor(ar[:, :, 1, :], by_chunk(t["r"][:]), by_chunk(t["cs"][:]), ALU.mult).then_inc(S("tilde_ready"), 1)
        split_lo(c, dve, n + 14)
        dve.wait_ge(S("tilde_ready"), b + 1)
        dve.wait_ge(S("slot_used"), n + 14)
        shifted(c, dve, st, t, 1, 4, "mu_rkv", 16 + 4 * b, t["v"], "rw_v_taken", n + 15)
        dve.wait_ge(S("gram_b"), b + 1)
        gram = lambda x, s: ps[:, x:x + 4, :].rearrange("p b (u s i) -> p (b u) s i", u=4, s=2)[:, :, s, :]
        dve.tensor_tensor(t["mr"][:], gram(0, 1), mask("upto"), ALU.mult)
        dve.tensor_tensor(t["yy"][:], gram(0, 0), mask("level0_t"), ALU.mult).then_inc(S("gram_b_taken"), 1)
        dve.wait_ge(S("gram_b_taken"), b + 1)
        st.did(dve.tensor_tensor(t["yy"][:], t["yy"][:], mask("eye"), ALU.add))
        dve.wait_ge(S("gram_k"), b + 1)
        dve.tensor_tensor(t["la"][:], gram(4, 0), mask("before"), ALU.mult)
        dve.tensor_tensor(t["mk"][:], gram(4, 1), mask("upto"), ALU.mult).then_inc(S("gram_k_taken"), 1)
        dve.wait_ge(S("gram_l"), b + 1)
        lower = ps[:, 0:2, :].rearrange("p b (u i) -> p (b u) i", u=8)
        st.did(dve.tensor_tensor(t["ll"][:], lower, mask("after"), ALU.mult))
        st.did(dve.tensor_tensor(t["xx"][:], t["ll"][:], mask("level0"), ALU.mult))
        dve.tensor_tensor(t["xx"][:], t["xx"][:], mask("eye"), ALU.add).then_inc(S("gram_l_taken"), 1)
        dve.wait_ge(S("gram_l_taken"), b + 1)
        for level in range(1, 6):
            for g in range(2):
                v = 2 * (5 * b + level - 1) + g + 1
                dve.wait_ge(S("xy_done"), v)
                us = slice(8 * g, 8 * g + 8)
                if level < 5:
                    st.did(dve.tensor_tensor(t["xx"][:, us, :], t["xx"][:, us, :], ps[:, 2 + g, :].rearrange("p (u i) -> p u i", u=8), ALU.add))
                dve.tensor_tensor(t["yy"][:, us, :], t["yy"][:, us, :], ps[:, 4 + g, :].rearrange("p (u i) -> p u i", u=8),
                                  ALU.add).then_inc(S("xy_ready"), 1)
                dve.wait_ge(S("xy_ready"), v)
        st.did(dve.tensor_tensor(t["bon"][:], t["bon"][:], t["v"][:], ALU.mult))
        lv = t["la"][:].rearrange("p (q j y) i -> p q j y i", q=2, y=2)

        def y_added(x):
            dve.wait_ge(S("yt_copied"), CHUNKS * b + x + 1)
            dve.wait_ge(S("ys_done"), 3 * b + x)
            y = t["yt"][:, :, 64 * x:64 * x + 64]
            dve.tensor_tensor(y, y, ps[:, 2, 0:256].rearrange("p (j i) -> p j i", j=4), ALU.add).then_inc(S("yt_added"), 1)

        for x in range(CHUNKS):
            q, v = slice(64 * (x % 2), 64 * (x % 2) + 64), CHUNKS * b + x + 1
            if x:
                dve.wait_ge(S("p_done"), 3 * b + x)
                dve.tensor_tensor(t["pb"][q].rearrange("p (q j) i -> p q j i", q=2), lv[q, :, :, x // 2, :],
                                  ps[q, 4:6, 0:256].rearrange("p b (j i) -> p b j i", j=4), ALU.add).then_inc(S("p_taken"), 1)
            if x < CHUNKS - 1:
                end = t["ends"][:, :, x:x + 1].to_broadcast([P, 4, RW_N])
                grown = ps[:, 7, 0:256].rearrange("p (j i) -> p j i", j=4)
                dve.wait_ge(S("ds_done"), 3 * b + x + 1)
                if x:
                    st.did(dve.tensor_tensor(t["state"][:], t["state"][:], grown, ALU.add))
                    grown = t["state"][:]
                dve.tensor_tensor(t["state"][:], grown, end, ALU.mult).then_inc(S("state_ready"), 1)
                dve.wait_ge(S("state_ready"), 3 * b + x + 1)
            if x:
                y_added(x)
        dve.wait_ge(S("means_done"), b + 1)
        dve.scalar_tensor_tensor(out=t["yt"][:], in0=half(0), scalar=-1.0 / RW_N, in1=t["yt"][:],
                                 op0=ALU.mult, op1=ALU.add).then_inc(S("centred"), 1)


def rw_finish(c, t, dve, st, b, split):
    dve.wait_ge(c.sem("vars_rooted"), b + 1)
    dve.reciprocal(t["sq"][:, 0:2], t["sq"][:, 0:2])
    split(3)
    st.did(dve.reciprocal(t["sq"][:, 2:4], t["sq"][:, 2:4]))
    split(4)
    st.did(dve.tensor_tensor(t["yt"][:], t["yt"][:], t["sq"][:], ALU.mult))
    for j in range(4):
        m = dve.tensor_scalar(t["yt"][:, j, :], t["yt"][:, j, :], c.param("lnx_w", 4 * b + j),
                              c.param("lnx_b", 4 * b + j), ALU.mult, ALU.add)
    m.then_inc(c.sem("rw_normed"), 1)


def rw_gated(c, t, pool, st, b):
    pool.wait_ge(c.sem("rw_normed"), b + 1)
    st.did(pool.tensor_tensor(t["yt"][:], t["yt"][:], t["bon"][:], ALU.add))
    pool.tensor_tensor(c.y[:, 4 * b:4 * b + 4, 0:SEQ], t["yt"][:], t["g"][:], ALU.mult).then_inc(c.sem("rw_out"), 1)
    pool.wait_ge(c.sem("rw_out"), b + 1)



MLA_BLOCKS = [(0, 0, 64, 64), (0, 64, 128, 128), (1, 0, 64, 192), (1, 64, 128, 256)]


def mla_pe(c, t, rw, pe):
    ps, S = c.ps, c.sem
    n = FIRST_SLOT["mla_in"]

    def low_sums(x):
        pe.wait_ge(S("low_squared"), x + 1)
        for j in range(4):
            m = pe.matmul(ps[:, 4 + x, 0:SEQ], c.const("ones"), t["sq4"][:, j, :], start=j == 0, stop=j == 3)
        m.then_inc(S("low_summed"), 1)

    for x in range(2):
        if x:
            pe.wait_ge(S("vars_rooted"), 2)
        for s in range(4):
            products(c, pe, n + 4 * x + s, c.xa, [(k, 4 * s + k) for k in range(4)], banks(c, 1 - x, SEQ), BOTH, s == 0, s == 3)
            if (x, s) == (1, 1):
                low_sums(0)
            if s == x == 0:
                pe.wait_ge(S("centred_squared"), 2)
                for j in range(4):
                    m = pe.matmul(ps[:, 2 + j // 2, 256 * (j % 2):256 * (j % 2) + 256], c.const("head_ones"),
                                  rw["sq"][:, j, :], start=True, stop=True)
                m.then_inc(S("vars_done"), 1)
    n = FIRST_SLOT["mla_q"]
    for x in range(7):
        if x == 0:
            pe.wait_ge(S("low_taken"), 2)
        elif x == 1:
            low_sums(1)
            pe.wait_ge(S("low_rooted"), 2)
        else:
            pe.wait_ge(S("up_taken"), x - 1)
        pe.wait_ge(S("low_ready"), 1 if x < 3 else 2)
        products(c, pe, n + x, c.xb, [(k, (8 if x < 3 else 12) + k) for k in range(4)], banks(c, x % 2, SEQ), BOTH, True, True)
        if x >= 5:
            pe.wait_ge(S("up_taken"), x + 1)
            for j in range(4):
                for kb in range(2):
                    m = pe.transpose(ps[:, 4 * (x % 2) + kb, P * j:P * j + P], t["vt4"][:, j, P * kb:P * kb + P], c.const("ident"))
            m.then_inc(S("v_turned"), 1)

    def scores(h):
        e, bank = h % 2, h % 2
        rows = slice(64 * e, 64 * e + 64)
        for b in range(2):
            out = ps[:, bank, SEQ * b:SEQ * b + P * (b + 1)]
            pe.matmul(out, t["qn"][:, h, P * b:P * b + P], t["kn"][:, h, 0:P * (b + 1)], start=True, stop=False)
            m = pe.matmul(out, t["qp"][rows, h // 2, P * b:P * b + P], t["kpe"][rows, 0:P * (b + 1)], start=False, stop=True)
        m.then_inc(S("mla_scores"), 1)

    def turned(h):
        bank = 2 + h % 2
        pe.wait_ge(S("mla_probs"), h + 1)
        pe.transpose(ps[:, bank, 0:P], t["pm"][:, h % 2, 0, 0:P], c.const("ident"))
        pe.transpose(ps[:, bank, P:2 * P], t["pm"][:, h % 2, 1, 0:P], c.const("ident"))
        pe.transpose(ps[:, bank, 2 * P:3 * P], t["pm"][:, h % 2, 1, P:2 * P], c.const("ident")).then_inc(S("mla_turned"), 1)

    def values(h):
        out = ps[:, 4 + h % 2, 0:SEQ]
        pe.wait_ge(S("mla_turned_taken"), h + 1)
        if h >= 2:
            pe.wait_ge(S("mla_out"), h - 1)
        pe.matmul(out, t["vn2"][:, 0, P * h:P * h + P], t["at2"][:, h % 2, 0:SEQ], start=True, stop=False)
        pe.matmul(out[:, P:], t["vn2"][:, 1, P * h:P * h + P], t["at2"][:, h % 2, SEQ:SEQ + P], start=False,
                  stop=True).then_inc(S("mla_values"), 1)

    pe.wait_ge(S("q_roped"), 1)
    pe.wait_ge(S("v_taken"), 2)
    scores(0)
    scores(1)
    for h in range(MLA_HEADS):
        turned(h)
        if h + 2 < MLA_HEADS:
            scores(h + 2)
        if h:
            values(h - 1)
    values(MLA_HEADS - 1)


def mla_act(c, t, rw, act):
    ps, S = c.ps, c.sem
    n = FIRST_SLOT["mla_in"]

    def low_root(x):
        act.wait_ge(S("low_summed"), x + 1)
        act.activation(t["low_rs"][:, x, :], ps[:, 4 + x, 0:SEQ], ACT.Sqrt, bias=c.eps["eps"], scale=1.0 / 512).then_inc(S("low_rooted"), 1)

    for m in range(2, 10):
        split_hi(c, act, n + m)
        if m == 2:
            rw_root(c, rw, act, 1)
        if m == 6:
            act.wait_ge(S("rw_out"), 2)
            act.copy(c.xb[0][:, 0:8, BOTH], c.y[:, 0:8, 0:SEQ]).then_inc(S("rw_hi"), 1)
        if m in (5, 9):
            x = (m - 5) // 4
            act.wait_ge(S("low_taken"), x + 1)
            if x:
                act.wait_ge(S("low_summed"), 1)
            act.activation(t["sq4"][:], t["low"][:, 4 * x:4 * x + 4, :], ACT.Square).then_inc(S("low_squared"), 1)
            for j in range(4):
                m_ = act.activation(c.xb[0][:, 8 + 4 * x + j, BOTH], t["low"][:, 4 * x + j, :], ACT.Copy,
                                    scale=c.param(("q_norm", "kv_norm")[x], j))
            m_.then_inc(S("low_hi"), 1)
        if m == 8:
            low_root(0)
    n = FIRST_SLOT["mla_q"]
    for x in range(7):
        split_hi(c, act, n + 2 + x)
        if x == 0:
            low_root(1)
        if x >= 5:
            act.wait_ge(S("v_turned"), x - 4)
            for kb in range(2):
                m = act.copy(t["vn2"][:, kb, 512 * (x - 5):512 * (x - 5) + 512], ps[:, 4 * (x % 2) + kb, :])
            m.then_inc(S("v_taken"), 1)

    def turned_taken(h):
        act.wait_ge(S("mla_turned"), h + 1)
        if h >= 2:
            act.wait_ge(S("mla_values"), h - 1)
        act.copy(t["at2"][:, h % 2, :], ps[:, 2 + h % 2, 0:3 * P]).then_inc(S("mla_turned_taken"), 1)

    def out_hi(h):
        act.wait_ge(S("mla_values"), h + 1)
        act.copy(c.xb[0][:, 8 + h, BOTH], ps[:, 4 + h % 2, 0:SEQ]).then_inc(S("mla_hi"), 1)

    for h in range(MLA_HEADS):
        act.wait_ge(S("mla_negmax"), h + 1)
        if h >= 2:
            act.wait_ge(S("mla_turned"), h - 1)
        for i, (b, a, z, keys) in enumerate(MLA_BLOCKS):
            m = act.activation(t["pm"][a:z, h % 2, b, 0:keys], ps[a:z, h % 2, SEQ * b:SEQ * b + keys], ACT.Exp,
                               bias=t["ms"][a:z, h % 2, 2 + b:3 + b], scale=MLA_SCALE, accum_out=t["ms"][a:z, h % 2, 4 + b:5 + b])
        m.then_inc(S("mla_exps"), 1)
        if h:
            turned_taken(h - 1)
        if h >= 2:
            out_hi(h - 2)
    turned_taken(MLA_HEADS - 1)
    out_hi(MLA_HEADS - 2)
    out_hi(MLA_HEADS - 1)


def mla_pool(c, t, rw, pool, st):
    rw_gated(c, rw, pool, st, 1)
    pool.wait_ge(c.sem("low_taken"), 1)
    pool.memset(t["pm"][:], 0.0)
    pool.memset(t["ms"][:], 0.0).then_inc(c.sem("mla_zeros"), 1)


def mla_dve(c, t, rw, dve, st):
    ps, S = c.ps, c.sem
    n = FIRST_SLOT["mla_in"]

    def low_lo(x):
        dve.wait_ge(S("low_hi"), x + 1)
        for j in range(4):
            m = dve.scalar_tensor_tensor(out=c.xb[1][:, 8 + 4 * x + j, BOTH], in0=t["low"][:, 4 * x + j, :],
                                         scalar=c.param(("q_norm", "kv_norm")[x], j),
                                         in1=c.xb[0][:, 8 + 4 * x + j, BOTH].bitcast(F32), op0=ALU.mult, op1=ALU.subtract)
        m.then_inc(S("low_ready"), 1)

    split_lo(c, dve, n + 2)
    rw_finish(c, rw, dve, st, 1, lambda m: split_lo(c, dve, n + m))
    for m in range(5, 10):
        if m in (5, 9):
            x = (m - 5) // 4
            dve.wait_ge(S("slot_used"), n + 4 * x + 4)
            if x == 0:
                dve.wait_ge(S("rw_out"), 2)
            dve.tensor_tensor(t["low"][:, 4 * x:4 * x + 4, :], ps[:, 4 * (1 - x):4 * (1 - x) + 4, 0:SEQ], wide(t["rs"][:, BOTH], 4),
                              ALU.mult).then_inc(S("low_taken"), 1)
        split_lo(c, dve, n + m)
        if m == 6:
            low_lo(0)
        if m == 7:
            dve.wait_ge(S("rw_hi"), 1)
            dve.tensor_tensor(c.xb[1][:, 0:8, BOTH], c.y[:, 0:8, 0:SEQ], c.xb[0][:, 0:8, BOTH].bitcast(F32),
                              ALU.subtract).then_inc(S("rw_operand"), 1)
    dve.wait_ge(S("rw_operand"), 1)
    dve.wait_ge(S("low_rooted"), 1)
    st.did(dve.reciprocal(t["low_rs"][:, 0, :], t["low_rs"][:, 0, :]))
    n = FIRST_SLOT["mla_q"]
    outs = [t["qn"][:, 0:4, :], t["qn"][:, 4:8, :], t["qp"][:], t["kn"][:, 0:4, :], t["kn"][:, 4:8, :], t["vt4"][:], t["vt4"][:]]
    swap = [(p + 16) % 32 for p in range(32)]
    for x in range(7):
        dve.wait_ge(S("slot_used"), n + x + 1)
        if x == 5:
            dve.wait_ge(S("q_roped"), 1)
        if x == 6:
            dve.wait_ge(S("v_turned"), 1)
        dve.tensor_tensor(outs[x], ps[:, 4 * (x % 2):4 * (x % 2) + 4, 0:SEQ], wide(t["low_rs"][:, x // 3 if x < 6 else 1, :], 4),
                          ALU.mult).then_inc(S("up_taken"), 1)
        split_lo(c, dve, n + 2 + x)
        if x == 0:
            low_lo(1)
        if x == 1:
            dve.wait_ge(S("low_rooted"), 2)
            st.did(dve.reciprocal(t["low_rs"][:, 1, :], t["low_rs"][:, 1, :]))
        if x == 2:
            dve.wait_ge(S("up_taken"), 3)
            st.did(dve.stream_shuffle(t["vt4"][:], t["qp"][:], swap))
        if x == 3:
            dve.tensor_tensor(t["vt4"][:], t["vt4"][:], wide(t["sin2"][:], 4), ALU.mult)
            st.did(dve.tensor_tensor(t["qp"][:], t["qp"][:], wide(t["cos2"][:], 4), ALU.mult))
        if x == 4:
            dve.tensor_tensor(t["qp"][:], t["qp"][:], t["vt4"][:], ALU.add).then_inc(S("q_roped"), 1)
    dve.wait_ge(S("mla_zeros"), 1)

    def out_lo(h):
        dve.wait_ge(S("mla_hi"), h + 1)
        dve.tensor_tensor(c.xb[1][:, 8 + h, BOTH], ps[:, 4 + h % 2, 0:SEQ], c.xb[0][:, 8 + h, BOTH].bitcast(F32),
                          ALU.subtract).then_inc(S("mla_out"), 1)

    def maxima(h):
        dve.wait_ge(S("mla_scores"), h + 1)
        ms = t["ms"][:, h % 2, :]
        for b, a, z, keys in MLA_BLOCKS:
            m = dve.tensor_reduce(ms[a:z, b:b + 1], ps[a:z, h % 2, SEQ * b:SEQ * b + keys], AX.X, ALU.max)
        st.did(m)
        dve.tensor_scalar(ms[:, 2:4], ms[:, 0:2], -MLA_SCALE, None, ALU.mult).then_inc(S("mla_negmax"), 1)

    def probs(h):
        dve.wait_ge(S("mla_exps"), h + 1)
        ms = t["ms"][:, h % 2, :]
        st.did(dve.reciprocal(ms[:, 6:8], ms[:, 4:6]))
        for b in range(2):
            m = dve.tensor_scalar(t["pm"][:, h % 2, b, :], t["pm"][:, h % 2, b, :], ms[:, 6 + b:7 + b], None, ALU.mult)
        m.then_inc(S("mla_probs"), 1)
        dve.wait_ge(S("mla_probs"), h + 1)

    maxima(0)
    maxima(1)
    for h in range(MLA_HEADS):
        probs(h)
        if h + 2 < MLA_HEADS:
            maxima(h + 2)
        if h >= 2:
            out_lo(h - 2)
    out_lo(MLA_HEADS - 2)
    out_lo(MLA_HEADS - 1)



def mix_pe(c, t, pe):
    S = c.sem
    n = FIRST_SLOT["mix"]
    t4 = lambda s: [(k, 4 * s + k) for k in range(4)]
    pe.wait_ge(S("mla_out"), MLA_HEADS)

    def turn(n, k, i=None):
        for x, (x_op, first, count) in enumerate(((c.xa, 0, 4), (c.xa, 4, 4), (c.xb, 8, 2), (c.xb, 10, 2))):
            if x >= 2 or k:
                pe.wait_ge(S("mix_taken"), at(4 * k + x - 1, i, 4))
            for s in range(count):
                products(c, pe, n + first + s, x_op, t4(s + (2 if x == 3 else 0)), banks(c, x % 2, SEQ), BOTH,
                         s == 0, s == count - 1, i, 12)

    turn(n, 0)
    with pe.Fori(0, 2) as i:
        turn(n + 12, 1, i)
    turn(n + 36, 3)
    n = FIRST_SLOT["mix_out"]
    pe.wait_ge(S("mix_taken"), 15)
    y_stage_pe(c, pe, n, c.xa, BOTH, 8, lambda s: pe.wait_ge(S("mix_ready"), s + 1))
    norm_between_pe(c, pe, t, 8, BOTH, 5)


MIX_TAKES = {5: 0, 9: 1, 11: 2, 13: 3}


def mix_act(c, t, act):
    S = c.sem
    n = FIRST_SLOT["mix"]

    def operand(kg):
        ks = slice(4 * kg, 4 * kg + 4)
        act.wait_ge(S("mixed"), kg + 1)
        act.copy(c.xa[0][:, ks, BOTH], c.y[:, ks, 0:SEQ]).then_inc(S("mix_hi"), 1)

    def turn(n, k, i=None):
        for m in range(2, 14):
            split_hi(c, act, n + m, i, 12)
            if k == 3 and m >= 11:
                operand(m - 11)
            if m in (5, 9):
                x = MIX_TAKES[m]
                act.wait_ge(S("mix_taken"), at(4 * k + x + 1, i, 4))
                act.activation(t["gates"][x][:], t["gates"][x][:], ACT.Sigmoid).then_inc(S("mix_gate"), 1)

    turn(n, 0)
    with act.Fori(0, 2) as i:
        turn(n + 12, 1, i)
    turn(n + 36, 3)
    n = FIRST_SLOT["mix_out"]
    operand(3)
    y_stage_split(c, lambda n: split_hi(c, act, n), lambda chunk, n: y_take_act(c, act, chunk, BOTH, 8, t), n)
    boundary_act(c, act, t, 3, 5, BOTH, "pre_ffn", FIRST_SLOT["ffn"])


def mix_dve(c, t, dve, st):
    S, ps = c.sem, c.ps
    n = FIRST_SLOT["mix"]

    def operand(kg):
        ks = slice(4 * kg, 4 * kg + 4)
        dve.wait_ge(S("mix_hi"), kg + 1)
        dve.tensor_tensor(c.xa[1][:, ks, BOTH], c.y[:, ks, 0:SEQ], c.xa[0][:, ks, BOTH].bitcast(F32),
                          ALU.subtract).then_inc(S("mix_ready"), 1)

    def turn(n, base, i=None):
        for m in range(2, 14):
            split_lo(c, dve, n + m, i, 12)
            if base == 3 and m >= 11:
                operand(m - 11)
            if m in MIX_TAKES:
                x = MIX_TAKES[m]
                out = ps[:, 4 * (x % 2):4 * (x % 2) + 4, 0:SEQ]
                dve.wait_ge(S("slot_used"), at(n + m - 1, i, 12))
                if x < 2:
                    dve.tensor_tensor(t["gates"][x][:], out, wide(t["rs"][:, BOTH], 4), ALU.mult).then_inc(S("mix_taken"), 1)
                else:
                    dve.wait_ge(S("mix_gate"), at(2 * base + x - 1, i, 2))
                    dve.tensor_tensor(t["gates"][x - 2][:], out, t["gates"][x - 2][:], ALU.mult).then_inc(S("mix_taken"), 1)
        dve.wait_ge(S("mix_taken"), at(4 * base + 4, i, 4))
        ks = slice(4 * base, 4 * base + 4) if i is None else bass.ds(at(4, i, 4), 4)
        dve.tensor_tensor(c.y[:, ks, 0:SEQ], t["gates"][0][:], t["gates"][1][:], ALU.add).then_inc(S("mixed"), 1)
        dve.wait_ge(S("mixed"), at(base + 1, i, 1))

    turn(n, 0)
    with dve.Fori(0, 2) as i:
        turn(n + 12, 1, i)
    turn(n + 36, 3)
    n = FIRST_SLOT["mix_out"]
    operand(3)
    dve.wait_ge(S("mix_ready"), 4)
    y_stage_split(c, lambda n: split_lo(c, dve, n), lambda chunk, n: y_take_dve(c, dve, chunk, n, BOTH, 8, t), n)
    boundary_dve(c, dve, st, t, 3, 5, BOTH, "post_mix", "pre_ffn", FIRST_SLOT["ffn"])



def ffn_pe(c, t, pe):
    S = c.sem
    n = FIRST_SLOT["ffn"]
    t4 = lambda s: [(k, 4 * s + k) for k in range(4)]
    first_chunk_pe(c, pe, t, n, c.xa, 3, BOTH, 6, 4)
    for s in range(4):
        pause = (lambda: pe.wait_ge(S("root_done"), 7)) if s == 0 else None
        products(c, pe, n + 4 + s, c.xa, t4(s), banks(c, 1, SEQ), BOTH, s == 0, s == 3, pause=pause)

    def down(n, x, i=None):
        products(c, pe, n + x, c.xf, [(k, k) for k in range(4)], banks(c, x % 2, SEQ), slice(0, SEQ), True, True, i, 12)

    with pe.Fori(0, FF_STEPS - 1) as i:
        for x in range(2):
            if x == 0:
                pe.wait_ge(S("up_out_taken"), i * 2 + 1)
                pe.wait_ge(S("down_taken"), i * 4 + 1)
            else:
                pe.wait_ge(S("up_out_taken"), i * 2 + 2)
                pe.wait_ge(S("down_taken"), i * 4 + 2)
            for s in range(4):
                products(c, pe, n + 8 + 4 * x + s, c.xa, t4(s), banks(c, x, SEQ), BOTH, s == 0, s == 3, i, 12)
        pe.wait_ge(S("ff_ready"), i + 1)
        for x in range(4):
            if x < 2:
                pe.wait_ge(S("up_out_taken"), i * 2 + (3 + x))
            else:
                pe.wait_ge(S("down_taken"), i * 4 + (x + 1))
            down(n + 16, x, i)
    n += 8 + 12 * (FF_STEPS - 1)
    pe.wait_ge(S("ff_ready"), FF_STEPS)
    pe.wait_ge(S("down_taken"), 4 * (FF_STEPS - 1) + 2)
    pe.wait_ge(S("up_out_taken"), 2 * FF_STEPS)
    for x in range(4):
        if x >= 2:
            pe.wait_ge(S("y_taken"), 12 + x - 1)
        down(n, x)
    n = FIRST_SLOT["ple"]

    def ple(slot, j2, half):
        w_hi, w_lo = c.w_hi[(n + slot) % SPLIT], c.w_lo[(n + slot) % SPLIT]
        pe.wait_ge(S("lo_done"), n + slot + 1)
        for j in range(4):
            out, a = c.ps[:, 4 * half + j, 0:SEQ], slice(P * j, P * j + P)
            for k in range(2):
                pe.matmul(out, w_hi[:, 2 * k + j2, a], t["ple_hi"][:, k, :], start=k == 0, stop=False)
                pe.matmul(out, w_hi[:, 2 * k + j2, a], t["ple_lo"][:, k, :], start=False, stop=False)
                m = pe.matmul(out, w_lo[:, 2 * k + j2, a], t["ple_hi"][:, k, :], start=False, stop=k == 1)
        m.then_inc(S("slot_used" if j2 else "ple_done"), 1)

    pe.wait_ge(S("ple_ready"), 1)
    pe.wait_ge(S("y_taken"), 15)
    ple(0, 0, 0)
    pe.wait_ge(S("y_taken"), 16)
    ple(0, 1, 1)
    pe.wait_ge(S("e_taken"), 1)
    norm_between_pe(c, pe, t, 12, BOTH, 7)
    pe.wait_ge(S("e_taken"), 2)
    ple(1, 0, 1)
    pe.wait_ge(S("root_done"), 8)
    ple(1, 1, 0)
    n = FIRST_SLOT["ple_gate"]
    pe.wait_ge(S("e_taken"), 4)
    y_stage_pe(c, pe, n, c.xa, BOTH, 16, lambda s: pe.wait_ge(S("x_ready"), 17 + s))
    norm_between_pe(c, pe, t, 16, BOTH, 8)


def conv_param(c, tap, tile, i):
    first = PARAM["conv_b"] if tap == 3 else PARAM["conv_w"] + 88 * tap
    return c.params[:, bass.ds(at(first + tile, i, 4), 1)] if i is not None else c.params[:, first + tile:first + tile + 1]


def ffn_act(c, t, act):
    S = c.sem
    n = FIRST_SLOT["ffn"]

    def scaled(x, f, i):
        act.wait_ge(S("up_out_taken"), at(2 * f + x + 1, i, 2))
        if x == 0 and i is not None:
            act.wait_ge(S("ff_f"), at(f, i, 1))
        for j in range(4):
            tile = 44 * x + 4 * f + j
            m = act.activation(t["conv"][x][:, j, :], t["up"][x][:, j, 2:], ACT.Identity,
                               bias=conv_param(c, 3, tile, i), scale=conv_param(c, 2, tile, i))
        m.then_inc(S("conv_scaled"), 1)

    def gelu(f, i):
        act.wait_ge(S("conv_done"), at(2 * f + 1, i, 2))
        act.activation(t["conv"][0][:], t["conv"][0][:], ACT.Gelu_apprx_tanh).then_inc(S("gelu_done"), 1)

    def hi(f, i):
        act.wait_ge(S("ff_f"), at(f + 1, i, 1))
        act.copy(c.xf[0][:], t["ff"][:]).then_inc(S("ff_hi"), 1)

    for m in range(4, 6):
        split_hi(c, act, n + m)
    root(c, act, 7, t["sd"], BOTH, S("stats_done"), 7, S("root_done"))
    scaled(0, 0, None)
    for m in range(6, 9):
        split_hi(c, act, n + m)
    gelu(0, None)
    scaled(1, 0, None)
    act.wait_ge(S("ple_in"), 16)
    act.copy(t["ple_hi"][:], t["ple"][:]).then_inc(S("ple_hi"), 1)
    with act.Fori(0, FF_STEPS - 1) as i:
        for m in range(1, 13):
            split_hi(c, act, n + 8 + m, i, 12)
            if m == 2:
                hi(0, i)
            if m == 5:
                scaled(0, 1, i)
            if m == 8:
                gelu(1, i)
            if m == 9:
                scaled(1, 1, i)
    n += 8 + 12 * (FF_STEPS - 1)
    act.wait_ge(S("slot_used"), n)
    hi(FF_STEPS - 1, None)
    split_hi(c, act, n + 1)

    def squares(x, base):
        act.wait_ge(S("y_taken"), base + x + 1)
        act.activation((t["sq"] if x else t["acc"])[:, :, BOTH], c.y[:, 4 * x:4 * x + 4, BOTH], ACT.Square).then_inc(S("y_squared"), 1)

    for x in range(4):
        split_hi(c, act, n + 2 + x)
        squares(x, 12)
    n = FIRST_SLOT["ple"]

    def e_taken(x, half):
        act.wait_ge(S("slot_used" if x % 2 else "ple_done"), n + x // 2 + 1 if x % 2 else x // 2 + 1)
        act.copy(t["e"][:, 4 * x:4 * x + 4, :], c.ps[:, 4 * half:4 * half + 4, 0:SEQ]).then_inc(S("e_taken"), 1)

    e_taken(0, 0)
    e_taken(1, 1)
    root(c, act, 0, t["sd"], BOTH, S("stats_done"), 8, S("root_done"))
    e_taken(2, 1)
    split_hi(c, act, n + 2)
    e_taken(3, 0)
    split_hi(c, act, n + 3)
    n = FIRST_SLOT["ple_gate"]
    operands_act(c, act, 4, BOTH, None, n)
    for m in range(4, 18):
        if m < 16:
            split_hi(c, act, n + m)
        if m % 4 == 1:
            x = (m - 5) // 4
            act.wait_ge(S("slot_used"), n + m - 1)
            act.activation(c.y[:, 4 * x:4 * x + 4, BOTH], c.ps[:, 4 * (x % 2):4 * (x % 2) + 4, 0:SEQ],
                           ACT.Sigmoid).then_inc(S("ple_gated"), 1)
            squares(x, 16)
    root(c, act, 0, t["sd"], BOTH, S("stats_done"), 9, S("root_done"))


def ffn_pool(c, t, pool, st, a):
    S = c.sem
    squares_pool(c, pool, st, 3, BOTH, t["acc"], t["sq"])
    pool.wait_ge(S("h_ready"), 48)
    pool.memset(c.y[:], 0.0).then_inc(S("down_taken"), 2)
    for x in range(2):
        m = pool.memset(t["up"][x][:, :, 0:2], 0.0)
    m.then_inc(S("ffn_zeros"), 1)
    pool.dma_start(t["ple"][:], a["ple_in"]).then_inc(S("ple_in"), 16)


def ffn_dve(c, t, dve, st):
    S, ps = c.sem, c.ps
    n = FIRST_SLOT["ffn"]
    out = lambda x: ps[:, 4 * (x % 2):4 * (x % 2) + 4, 0:SEQ]

    def taken(x, f, i, done):
        dve.wait_ge(S("slot_used"), done)
        dve.tensor_tensor(t["up"][x][:, :, 2:], out(x), wide(t["rs"][:, BOTH], 4), ALU.mult).then_inc(S("up_out_taken"), 1)

    def conv_tap(tap, x, f, i):
        if tap:
            dve.wait_ge(S("conv_scaled"), at(2 * f + x + 1, i, 2))
        for j in range(4):
            m = dve.scalar_tensor_tensor(out=t["conv"][x][:, j, :], in0=t["up"][x][:, j, tap:tap + SEQ],
                                         scalar=conv_param(c, tap, 44 * x + 4 * f + j, i),
                                         in1=t["conv"][x][:, j, :], op0=ALU.mult, op1=ALU.add)
        if tap:
            st.did(m)
        else:
            m.then_inc(S("conv_done"), 1)
            dve.wait_ge(S("conv_done"), at(2 * f + x + 1, i, 2))

    def product(f, i):
        dve.wait_ge(S("gelu_done"), at(f + 1, i, 1))
        dve.tensor_tensor(t["ff"][:], t["conv"][0][:], t["conv"][1][:], ALU.mult).then_inc(S("ff_f"), 1)

    def lo(f, i):
        dve.wait_ge(S("ff_hi"), at(f + 1, i, 1))
        dve.tensor_tensor(c.xf[1][:], t["ff"][:], c.xf[0][:].bitcast(F32), ALU.subtract).then_inc(S("ff_ready"), 1)
        dve.wait_ge(S("ff_ready"), at(f + 1, i, 1))

    for m in range(4, 6):
        split_lo(c, dve, n + m)
    pre_root_dve(c, dve, st, t, 6, BOTH)
    dve.wait_ge(S("ffn_zeros"), 1)
    taken(0, 0, None, n + 4)
    split_lo(c, dve, n + 6)
    conv_tap(1, 0, 0, None)
    conv_tap(0, 0, 0, None)
    for m in range(7, 9):
        split_lo(c, dve, n + m)
    taken(1, 0, None, n + 8)
    conv_tap(1, 1, 0, None)
    conv_tap(0, 1, 0, None)
    product(0, None)
    dve.wait_ge(S("ple_hi"), 1)
    dve.tensor_tensor(t["ple_lo"][:], t["ple"][:], t["ple_hi"][:].bitcast(F32), ALU.subtract).then_inc(S("ple_ready"), 1)
    with dve.Fori(0, FF_STEPS - 1) as i:
        st.enter(i, 2)
        base = n + 8
        def added(x):
            dve.wait_ge(S("slot_used"), at(base + 9 + x, i, 12))
            y = c.y[:, 4 * x:4 * x + 4, BOTH]
            dve.tensor_tensor(y, y, out(x), ALU.add).then_inc(S("down_taken"), 1)

        for m in range(1, 13):
            if m == 5:
                taken(0, 1, i, at(base + 4, i, 12))
            if m == 9:
                taken(1, 1, i, at(base + 8, i, 12))
            if m >= 10:
                added(m - 10)
            split_lo(c, dve, base + m, i, 12)
            if m == 3:
                lo(0, i)
            if m in (6, 7):
                conv_tap(7 - m, 0, 1, i)
            if m in (10, 11):
                conv_tap(11 - m, 1, 1, i)
            if m == 12:
                product(1, i)
        added(3)
        dve.wait_ge(S("down_taken"), at(6, i, 4))
    st.leave(FF_STEPS - 1)
    lo(FF_STEPS - 1, None)
    split_lo(c, dve, n + 9 + 12 * (FF_STEPS - 1))
    n += 8 + 12 * (FF_STEPS - 1)

    def squares(x, base):
        dve.wait_ge(S("y_squared"), base + x + 1)
        if x:
            dve.tensor_tensor(t["acc"][:, :, BOTH], t["acc"][:, :, BOTH], t["sq"][:, :, BOTH], ALU.add).then_inc(S("y_added"), 1)
            dve.wait_ge(S("y_added"), base // 4 * 3 + x)

    for x in range(4):
        split_lo(c, dve, n + 2 + x)
        dve.wait_ge(S("slot_used"), n + x + 1)
        y = c.y[:, 4 * x:4 * x + 4, BOTH]
        dve.tensor_tensor(y, y, out(x), ALU.add).then_inc(S("y_taken"), 1)
        squares(x, 12)
    n = FIRST_SLOT["ple"]
    dve.wait_ge(S("root_done"), 8)
    st.did(dve.reciprocal(t["rs"][:, BOTH], t["sd"][:, BOTH]))
    split_lo(c, dve, n + 2)
    split_lo(c, dve, n + 3)
    n = FIRST_SLOT["ple_gate"]
    operands_dve(c, dve, st, 4, BOTH, t, "post_ffn", None, n)
    for m in range(4, 18):
        if m < 16:
            split_lo(c, dve, n + m)
        if m % 4 == 1:
            x = (m - 5) // 4
            y = c.y[:, 4 * x:4 * x + 4, BOTH]
            dve.wait_ge(S("ple_gated"), x + 1)
            dve.wait_ge(S("e_taken"), 4)
            dve.tensor_tensor(y, y, t["e"][:, 4 * x:4 * x + 4, :], ALU.mult).then_inc(S("y_taken"), 1)
            squares(x, 16)
    dve.wait_ge(S("root_done"), 9)
    st.did(dve.reciprocal(t["rs"][:, BOTH], t["sd"][:, BOTH]))
    for kg in range(4):
        ks = slice(4 * kg, 4 * kg + 4)
        st.did(dve.tensor_tensor(t["tmp"][:, :, BOTH], c.y[:, ks, BOTH], wide(t["rs"][:, BOTH], 4), ALU.mult))
        for j in range(4):
            k = 4 * kg + j
            m = dve.scalar_tensor_tensor(out=c.h[:, k, BOTH], in0=t["tmp"][:, j, BOTH], scalar=c.param("ple_norm", k),
                                         in1=c.h[:, k, BOTH], op0=ALU.mult, op1=ALU.add)
        m.then_inc(S("out_ready"), 1)
        dve.wait_ge(S("out_ready"), kg + 1)


def store_out(c, sp, out):
    for kg in range(4):
        ks = slice(4 * kg, 4 * kg + 4)
        sp.wait_ge(c.sem("out_ready"), kg + 1)
        sp.dma_start(out[:, ks, :], c.h[:, ks, BOTH]).then_inc(c.sem("out_written"), 16)
    sp.wait_ge(c.sem("out_written"), 64)


def program(nc, a):
    with ExitStack() as ctx:
        c = Chip(nc, ctx)
        c.turns = {}
        c.eps = {"eps": c.small[:, 0:1], "rw": c.small[:, 1:2]}
        t = {}

        def place(scope, names):
            return {n: c.sb(scope, n, shape, *rest) for n, shape, *rest in names}

        with ExitStack() as first:
            c.xb = [c.sb(first, f"xb_{x}", [P, KT, ROWS], F32R) for x in ("hi", "lo")]
            consts = c.sb(first, "consts_first", [P, columns(CONSTS_FIRST)[1]])
            with ExitStack() as scope:
                t["attn"] = place(scope, [
                    ("qk", [P, 4, ROWS]), ("rot", [P, 2, ROWS]), ("p", [P, 2, 3, ROWS]), ("a", [P, 3 * 3 * P]),
                    ("at", [P, 3, ROWS]), ("vt", [P, 2, 3 * P]), ("vn", [P, 3, HEAD_V]), ("o", [P, 2, ROWS]),
                    ("osq", [P, 2, ROWS]), ("rs", [P, ROWS]), ("ro", [P, ROWS]), ("so", [P, ROWS]), ("st", [P, 24]),
                    ("lam", [P, 8]), ("gain", [P, 2])])
                t["attn"]["sd"] = t["attn"]["so"]
                t["attn"]["first"] = consts
                flat = t["attn"]["p"][:].rearrange("p a b r -> p (a b r)")
                t["attn"]["acc"] = flat[:, 0:4 * ROWS].rearrange("p (k r) -> p k r", k=4)
                t["attn"]["sq"] = t["attn"]["a"][:, 0:4 * ROWS].rearrange("p (k r) -> p k r", k=4)
            with ExitStack() as scope:
                t["mid"] = place(scope, [
                    ("acc", [P, 4, ROWS]), ("sq", [P, 4, ROWS]), ("tmp", [P, 4, ROWS]),
                    ("u0", [P, 4, ROWS]), ("u1", [P, 4, ROWS]), ("sums0", [P, 4, ROWS]), ("sums1", [P, 4, ROWS]),
                    ("rs_mid", [P, ROWS]), ("sd_mid", [P, ROWS])])
                m = t["mid"]
                m["u"], m["sums"] = [m["u0"], m["u1"]], [m["sums0"], m["sums1"]]
                m["rs"], m["sd"], m["first"], m["mixed"] = m["rs_mid"], m["sd_mid"], consts, m["sq"]

        with ExitStack() as second:
            lasting = place(second, [("kpe", [P, SEQ]), ("cos2", [P, SEQ]), ("sin2", [P, SEQ]), ("rs_2", [P, ROWS]), ("sd_2", [P, ROWS])])
            lasting["rs"], lasting["sd"] = lasting["rs_2"], lasting["sd_2"]
            spare = c.y[:].rearrange("p k r -> p (k r)")[:, 8 * ROWS:]
            tiles = lambda x: x.rearrange("p (j r) -> p j r", j=4)
            units = lambda x: x.rearrange("p (u i) -> p u i", i=RW_N)
            with ExitStack() as scope:
                m = t["rw"] = place(scope, [
                    ("masks", [P, columns(CONSTS_RW)[1]]), ("lora_hi", [P, 3, SEQ], F32R), ("lora_lo", [P, 3, SEQ], F32R),
                    ("ar_flat", [P, 4 * 4 * 2 * RW_N]), ("pb", [P, 8, RW_N]), ("sa", [P, 8, RW_N]), ("state", [P, 4, RW_N]),
                    ("ends", [P, 4, 4])] + [(f"rw_tile{n}", [P, 4 * SEQ]) for n in range(11)])
                m.update(lasting)
                m["ar"] = m["ar_flat"].rearrange("p (j x s) -> p j x s", j=4, x=CHUNKS)
                m["lora"] = m["ar_flat"][:, 0:3 * SEQ].rearrange("p (j r) -> p j r", j=3)
                m["positions"] = m["ar_flat"][:, 4 * SEQ:5 * SEQ].bitcast(I32)
                flat = [m[f"rw_tile{n}"][:] for n in range(11)]
                for n, name in enumerate(("bt", "kt", "v", "bon", "g", "r", "k", "a", "w", "cs", "kk")):
                    m[name] = tiles(flat[n])
                for n, name in enumerate(("la", "mr", "mk", "ll", "xx", "yy")):
                    m[name] = units(flat[5 + n])
                m["nb"], m["nk"], m["nv"] = m["ll"], m["xx"], units(spare[:, 0:4 * SEQ])
                m["yt"], m["sq"] = m["bt"], m["kt"]
                m["tt"], m["tt4"] = units(spare[:, 0:4 * SEQ]), tiles(spare[:, 0:4 * SEQ])
                m["lm"] = units(spare[:, 4 * SEQ:8 * SEQ])
                m["zp"] = tiles(spare[:, 4 * SEQ:8 * SEQ + 4])
                m["acc"] = t["mid"]["acc"]
            late = place(second, [(f"late_{n}", [P, 4, ROWS]) for n in ("acc", "sq", "tmp")])
            late = {n: late[f"late_{n}"] for n in ("acc", "sq", "tmp")}
            with ExitStack() as scope:
                xb_second = [c.sb(scope, f"xb2_{x}", [P, KT, ROWS], F32R) for x in ("hi", "lo")]
                with ExitStack() as inner:
                    m = t["mla"] = place(inner, [
                        ("low_flat", [P, 8 * SEQ]), ("pm", [P, 2, 2, SEQ]), ("at2", [P, 2, 3 * P]), ("low_rs", [P, 2, SEQ]),
                        ("ms", [P, 2, 8])])
                    m.update(lasting)
                    m["low"] = m["low_flat"].rearrange("p (j r) -> p j r", j=8)
                    m["vn2"] = m["low_flat"].rearrange("p (b n) -> p b n", b=2)
                    m["sq4"] = m["vt4"] = late["acc"][:, :, 0:SEQ]
                    m["qp"] = late["tmp"][:, :, 0:SEQ]
                    m["qn"], m["kn"] = c.y[:, 0:8, 0:SEQ], c.y[:, 8:16, 0:SEQ]
                with ExitStack() as inner:
                    m = t["mix"] = place(inner, [("gate_rw", [P, 4, SEQ]), ("gate_mla", [P, 4, SEQ])])
                    m.update(lasting | late)
                    m["gates"] = [m["gate_rw"], m["gate_mla"]]
            m = t["ffn"] = place(second, [
                ("up_gate", [P, 4, SEQ + 2]), ("up_value", [P, 4, SEQ + 2]), ("conv_gate", [P, 4, SEQ]), ("conv_value", [P, 4, SEQ]),
                ("ff", [P, 4, SEQ]), ("ff_hi", [P, 4, SEQ], F32R), ("ff_lo", [P, 4, SEQ], F32R), ("ple", [P, 2, SEQ]),
                ("ple_hi", [P, 2, SEQ], F32R), ("ple_lo", [P, 2, SEQ], F32R), ("e", [P, KT, SEQ])])
            m.update(lasting | late)
            m["up"], m["conv"] = [m["up_gate"], m["up_value"]], [m["conv_gate"], m["conv_value"]]
            c.xf = [m["ff_hi"], m["ff_lo"]]
        xb_first = c.xb

        S = c.sem
        block = ctx.enter_context(nc.Block())

        @block.sync
        def _(sp):
            attn_load(c, t["attn"], sp, a)
            load_weights(c, sp, a["weights"])
            store_out(c, sp, a["out"])

        @block.tensor
        def _(pe):
            c.xb = xb_first
            attn_pe(c, t["attn"], pe)
            mid_pe(c, t["mid"], pe)
            c.xb = xb_second
            rw_pe(c, t["rw"], pe)
            mla_pe(c, t["mla"], t["rw"], pe)
            mix_pe(c, t["mix"], pe)
            ffn_pe(c, t["ffn"], pe)

        @block.scalar
        def _(act):
            act.wait_ge(S("eps_ready"), 2)
            c.xb = xb_first
            attn_act(c, t["attn"], act)
            mid_act(c, t["mid"], act)
            c.xb = xb_second
            rw_act(c, t["rw"], act)
            mla_act(c, t["mla"], t["rw"], act)
            mix_act(c, t["mix"], act)
            ffn_act(c, t["ffn"], act)

        @block.vector
        def _(dve):
            st = Steps(dve, S("dve_step"))
            c.xb = xb_first
            attn_dve(c, t["attn"], dve, st)
            mid_dve(c, t["mid"], dve, st)
            c.xb = xb_second
            rw_dve(c, t["rw"], dve, st)
            mla_dve(c, t["mla"], t["rw"], dve, st)
            mix_dve(c, t["mix"], dve, st)
            ffn_dve(c, t["ffn"], dve, st)

        @block.gpsimd
        def _(pool):
            st = Steps(pool, S("pool_step"))
            attn_pool(c, t["attn"], pool, st)
            mid_pool(c, t["mid"], pool, st)
            rw_pool(c, t["rw"], pool, st, a)
            mla_pool(c, t["mla"], t["rw"], pool, st)
            ffn_pool(c, t["ffn"], pool, st, a)



def channels(v):
    return np.ascontiguousarray(v.reshape(-1, P).T)


def slots(w, cols=SLOT_N):
    k, n = w.shape
    s = w.reshape(k // (SLOT_K * P), SLOT_K, P, n // cols, cols).transpose(3, 0, 2, 1, 4)
    return np.ascontiguousarray(s).reshape(-1, P, SLOT_K, cols)


def pack_weights(x):
    out = np.zeros((N_SLOTS, P, SLOT_K, SLOT_N), np.float32)

    def put(name, parts):
        n = FIRST_SLOT[name]
        for part in parts:
            out[n:n + len(part)] = part
            n += len(part)
        return n

    w = x["attn_w_in"][0].reshape(D, 4, HEADS, HEAD_V)
    put("attn_in", [slots(np.concatenate([w[:, a, h], w[:, a + 1, h]], 1)) for h in range(HEADS) for a in (0, 2)])
    put("attn_out", [slots(x["attn_w_out"][0])])
    put("pool_in", [slots(x["pool_w_in"][0])])
    put("pool_group", [slots(x["pool_w_group"][0, g]) for g in range(4)])
    put("pool_out", [slots(x["pool_w_out"][0])])
    w = x["w_in_2"][0]
    rw, mla, gate = w[:, :3360], w[:, 3360:4448], w[:, 4448:]
    pe = np.concatenate([np.arange(0, 16), np.arange(32, 48), np.arange(16, 32), np.arange(48, 64)])
    down = np.zeros((D, SLOT_N), np.float32)
    down[:, 0:288] = rw[:, 3072:]
    k_pe = mla[:, 1024:][:, pe]
    down[:, 384:448], down[:, 448:512] = k_pe, k_pe
    put("rw_down", [slots(down)])
    for b in range(2):
        n = FIRST_SLOT[f"rw_half{b}"]
        s = slice(512 * b, 512 * b + 512)
        for r, first in ((1, n), (0, n + 5), (2, n + 10)):
            out[first:first + 4] = slots(rw[:, RW_WIDTH * r:][:, s])
        n += 4
        out[n, 0:64, 0], out[n, 64:128, 0] = x["rw_w2_2"][0][:, s], x["rw_a2_2"][0][:, s]
        out[n + 5, :, 1], out[n + 5, 0:32, 2] = x["rw_g2_2"][0][0:128, s], x["rw_g2_2"][0][128:160, s]
    put("mla_in", [slots(mla[:, 0:1024])])
    q = x["mla_w_q_up_2"][0].reshape(512, MLA_HEADS, 192)
    put("mla_q", [slots(np.concatenate([q[:, :, 0:128].reshape(512, -1), q[:, :, 128:][:, :, pe].reshape(512, -1)], 1))])
    kv = x["mla_w_kv_up_2"][0].reshape(512, MLA_HEADS, 256)
    put("mla_kv", [slots(np.concatenate([kv[:, :, 0:128].reshape(512, -1), kv[:, :, 128:].reshape(512, -1)], 1))])
    branch = np.concatenate([x["w_branch_rw_2"][0], x["w_branch_mla_2"][0]], 0)
    put("mix", [slots(m[:, 512 * n:512 * n + 512]) for n in range(4) for m in (gate[:, 0:D], gate[:, D:], branch)])
    put("mix_out", [slots(x["w_out_2"][0])])
    up, down = x["w_up_2"][0], x["w_down_2"][0]
    n = FIRST_SLOT["ffn"]
    for f in range(FF_STEPS + 1):
        if f < FF_STEPS:
            out[n:n + 4] = slots(up[:, 512 * f:512 * f + 512])
            out[n + 4:n + 8] = slots(up[:, D_FF + 512 * f:D_FF + 512 * f + 512])
            n += 8
        if f:
            out[n:n + 4] = slots(down[512 * (f - 1):512 * f])
            n += 4
    e = x["w_ple_2"][0].reshape(2, P, 2, 2, SLOT_N)
    out[FIRST_SLOT["ple"]:FIRST_SLOT["ple"] + 2] = e.transpose(2, 1, 0, 3, 4).reshape(2, P, 4, SLOT_N)
    put("ple_gate", [slots(x["w_ple_gate_2"][0])])
    return out


def pack_params(x):
    out = np.zeros((P, N_PARAMS), np.float32)

    def put(name, v, k=0):
        out[:, PARAM[name] + k:PARAM[name] + k + v.shape[1]] = v

    for n in range(2):
        put(f"pre{n}", channels(x["pre_norm_g"][n]))
        put(f"post{n}", channels(x["post_norm_g"][n]))
    put("subln", channels(x["attn_subln_g"][0]))
    for n, v in enumerate(("attn_lambda_q1", "attn_lambda_k1", "attn_lambda_q2", "attn_lambda_k2")):
        put("lam", x[v][0][:, None], n)
    put("pool_scale", channels(x["pool_scale"][0]))
    put("pre_mix", channels(x["pre_mix_norm_2"][0]))
    mu = x["rw_mu_2"][0]
    put("mu_rkv", channels(mu[0:3072]))
    put("mu_lora", channels(np.concatenate([mu[3072:], np.zeros(96, np.float32)])))
    for name, of in (("w0", "rw_w0_2"), ("a0", "rw_a0_2"), ("k_k", "rw_k_k_2"), ("k_a", "rw_k_a_2"), ("lnx_w", "rw_lnx_w_2"),
                     ("lnx_b", "rw_lnx_b_2"), ("r_k", "rw_r_k_2"), ("q_norm", "mla_q_norm_2"), ("kv_norm", "mla_kv_norm_2"),
                     ("post_mix", "post_mix_norm_2"), ("pre_ffn", "pre_ffn_norm_2"), ("conv_b", "conv_b_2"),
                     ("post_ffn", "post_ffn_norm_2"), ("ple_norm", "ple_norm_2")):
        put(name, channels(x[of][0]))
    for n in range(3):
        put("conv_w", channels(x["conv_w_2"][0, n]), 88 * n)
    p = np.arange(P)
    put("inv_freq", (np.float32(10000.0) ** (-(2 * ((p % 16) + 16 * (p // 32 % 2))).astype(np.float32) / np.float32(64)))[:, None])
    put("rope_sign", np.where(p % 32 < 16, -1.0, 1.0)[:, None])
    return out


def kernel(**inputs):
    import concourse.bacc as bacc
    from concourse.bass_utils import run_bass_kernel_spmd

    x = {n: np.asarray(v) for n, v in inputs.items()}
    base, first, rw = stage_consts()
    rows = np.concatenate([x["meta_tokens"], x["x"][0]], 0)
    arrays = {
        "weights": pack_weights(x), "params": pack_params(x), "consts": base, "consts_first": first, "consts_rw": rw,
        "h0": np.ascontiguousarray(rows.reshape(ROWS, KT, P).transpose(2, 1, 0)),
        "ple_in": np.ascontiguousarray(x["p_2"][0, 0].reshape(SEQ, 2, P).transpose(2, 1, 0)),
        "positions": np.ascontiguousarray(x["positions_2"]),
    }
    nc = bacc.Bacc("TRN2", target_bir_lowering=False, num_devices=1)
    a = {n: nc.dram_tensor(n, v.shape, mybir.dt.from_np(v.dtype), kind="ExternalInput").ap() for n, v in arrays.items()}
    a["out"] = nc.dram_tensor("out", (P, KT, SEQ), F32, kind="ExternalOutput").ap()
    program(nc, a)
    r = run_bass_kernel_spmd(nc, [arrays], core_ids=[0])
    out = r.results[0]["out"]
    return np.ascontiguousarray(out.transpose(2, 1, 0)).reshape(1, SEQ, D)
```
